# Optimizing a Trainium2 kernel written in Bass

```python
import jax, jax.numpy as jnp
from jax import lax
import numpy as np

D_MODEL = 1024
BATCH = 1
SEQ = 1024
DEPTH = 1

PLE_DIM = 256
RET_HEADS = 8
RET_HEAD_DIM = 64
RET_WIDTH = RET_HEADS * RET_HEAD_DIM
RET_CHUNK = 128
MLA_HEADS = 8
MLA_NOPE_DIM = 64
MLA_ROPE_DIM = 32
MLA_QK_DIM = MLA_NOPE_DIM + MLA_ROPE_DIM
MLA_V_DIM = 64
MLA_Q_RANK = 256
MLA_KV_RANK = 128
MLA_WIDTH = MLA_HEADS * MLA_V_DIM
MIX_WIDTH = RET_WIDTH + MLA_WIDTH
Q_BLOCK = 128
IN_COLS = 4 * RET_WIDTH + MLA_Q_RANK + MLA_KV_RANK + MLA_ROPE_DIM
D_FF = 2816
CONV_WIDTH = 3
ROPE_BASE = 10000.0
EPS = 1e-6

kernel_name = "hybrid_retention_mla_convffn_block"

def rms_norm(x, g):
    xf = x.astype(jnp.float32)
    y = xf * lax.rsqrt(jnp.mean(xf * xf, axis=-1, keepdims=True) + EPS)
    return (y * g.astype(jnp.float32)).astype(x.dtype)

def rope(x, pos):
    d = x.shape[-1]
    inv_freq = ROPE_BASE ** (-jnp.arange(0, d, 2, dtype=jnp.float32) / d)
    ang = pos.astype(jnp.float32)[..., None] * inv_freq
    cos = jnp.cos(ang)[:, :, None, :]
    sin = jnp.sin(ang)[:, :, None, :]
    xf = x.astype(jnp.float32)
    x1, x2 = xf[..., : d // 2], xf[..., d // 2:]
    out = jnp.concatenate([x1 * cos - x2 * sin, x2 * cos + x1 * sin], axis=-1)
    return out.astype(x.dtype)

def retention_chunkwise(q, k, v):
    B, S, H, D = q.shape
    C = RET_CHUNK
    N = S // C
    log_gamma = jnp.log1p(-jnp.exp2(-5.0 - jnp.arange(H, dtype=jnp.float32)))
    idx = jnp.arange(C, dtype=jnp.float32)
    rel = idx[:, None] - idx[None, :]
    intra = jnp.where(rel >= 0, jnp.exp(log_gamma[:, None, None] * jnp.maximum(rel, 0.0)), 0.0)
    inner = jnp.exp(log_gamma[:, None] * (idx + 1.0))
    tail = jnp.exp(log_gamma[:, None] * (C - 1.0 - idx))
    chunk_decay = jnp.exp(log_gamma * C)

    def to_chunks(t):
        return t.astype(jnp.float32).reshape(B, N, C, H, D).transpose(1, 0, 3, 2, 4)

    qc = to_chunks(q)
    kc = to_chunks(k) * (D ** -0.5)
    vc = to_chunks(v)

    def step(state, inp):
        q_i, k_i, v_i = inp
        cross = jnp.einsum('bhcd,bhde->bhce', q_i, state) * inner[None, :, :, None]
        scores = jnp.einsum('bhcd,bhmd->bhcm', q_i, k_i) * intra[None]
        within = jnp.einsum('bhcm,bhme->bhce', scores, v_i)
        state = state * chunk_decay[None, :, None, None] + jnp.einsum(
            'bhmd,bhme->bhde', k_i * tail[None, :, :, None], v_i)
        return state, cross + within

    state0 = jnp.zeros((B, H, D, D), jnp.float32)
    _, out = lax.scan(step, state0, (qc, kc, vc))
    return out.transpose(1, 0, 3, 2, 4).reshape(B, S, H, D)

def causal_block_attention(q, k, v):
    B, S, H, Dq = q.shape
    Dv = v.shape[-1]
    NB = S // Q_BLOCK
    scale = Dq ** -0.5
    qb = q.reshape(B, NB, Q_BLOCK, H, Dq).transpose(1, 0, 2, 3, 4)
    key_idx = jnp.arange(S)

    def one_block(args):
        q_blk, blk = args
        s = jnp.einsum('bqhd,bkhd->bhqk', q_blk, k).astype(jnp.float32) * scale
        q_idx = blk * Q_BLOCK + jnp.arange(Q_BLOCK)
        mask = key_idx[None, :] <= q_idx[:, None]
        s = jnp.where(mask[None, None], s, -jnp.inf)
        pr = jax.nn.softmax(s, axis=-1).astype(v.dtype)
        return jnp.einsum('bhqk,bkhe->bqhe', pr, v)

    out = lax.map(one_block, (qb, jnp.arange(NB)))
    return out.transpose(1, 0, 2, 3, 4).reshape(B, S, H * Dv)

def causal_depthwise_conv(h, w, b):
    C = h.shape[-1]
    y = lax.conv_general_dilated(
        h, w[:, None, :].astype(h.dtype), window_strides=(1,),
        padding=[(CONV_WIDTH - 1, 0)], dimension_numbers=('NWC', 'WIO', 'NWC'),
        feature_group_count=C)
    return y + b.astype(h.dtype)

def setup_inputs(seed: int = 0) -> dict:
    key = jax.random.key(seed)
    ks = jax.random.split(key, 24)
    f32 = jnp.float32

    def w(k, shape, fan_in):
        return jax.random.normal(k, shape, f32) * (fan_in ** -0.5)

    def gain(k, shape):
        return 1.0 + 0.05 * jax.random.normal(k, shape, f32)

    x = jax.random.normal(ks[0], (BATCH, SEQ, D_MODEL), f32)
    p = jax.random.normal(ks[1], (DEPTH, BATCH, SEQ, PLE_DIM), f32)
    offsets = jax.random.randint(ks[2], (BATCH, 1), 0, 4096, dtype=jnp.int32)
    positions = jnp.arange(SEQ, dtype=jnp.int32)[None, :] + offsets
    return {
        "x": x,
        "p": p,
        "positions": positions,
        "w_in": w(ks[3], (DEPTH, D_MODEL, IN_COLS), D_MODEL),
        "w_uq": w(ks[4], (DEPTH, MLA_Q_RANK, MLA_HEADS * MLA_QK_DIM), MLA_Q_RANK),
        "w_ukv": w(ks[5], (DEPTH, MLA_KV_RANK, MLA_HEADS * (MLA_NOPE_DIM + MLA_V_DIM)), MLA_KV_RANK),
        "w_o": w(ks[6], (DEPTH, MIX_WIDTH, D_MODEL), MIX_WIDTH),
        "g_pre_mix": gain(ks[7], (DEPTH, D_MODEL)),
        "g_post_mix": gain(ks[8], (DEPTH, D_MODEL)),
        "g_q_a": gain(ks[9], (DEPTH, MLA_Q_RANK)),
        "g_kv_a": gain(ks[10], (DEPTH, MLA_KV_RANK)),
        "g_ret_gn": gain(ks[11], (DEPTH, RET_WIDTH)),
        "w_up": w(ks[12], (DEPTH, D_MODEL, 2 * D_FF), D_MODEL),
        "conv_w": w(ks[13], (DEPTH, CONV_WIDTH, 2 * D_FF), CONV_WIDTH),
        "conv_b": 0.02 * jax.random.normal(ks[14], (DEPTH, 2 * D_FF), f32),
        "w_down": w(ks[15], (DEPTH, D_FF, D_MODEL), D_FF),
        "g_pre_ffn": gain(ks[16], (DEPTH, D_MODEL)),
        "g_post_ffn": gain(ks[17], (DEPTH, D_MODEL)),
        "w_ple": w(ks[18], (DEPTH, PLE_DIM, D_MODEL), PLE_DIM),
        "w_ple_gate": w(ks[19], (DEPTH, D_MODEL, D_MODEL), D_MODEL),
        "b_ple_gate": 0.02 * jax.random.normal(ks[20], (DEPTH, D_MODEL), f32),
        "g_post_ple": gain(ks[21], (DEPTH, D_MODEL)),
    }

def reference(x, p, positions, w_in, w_uq, w_ukv, w_o, g_pre_mix, g_post_mix, g_q_a, g_kv_a,
              g_ret_gn, w_up, conv_w, conv_b, w_down, g_pre_ffn, g_post_ffn, w_ple,
              w_ple_gate, b_ple_gate, g_post_ple):
    B, S, _ = x.shape
    splits = [RET_WIDTH, 2 * RET_WIDTH, 3 * RET_WIDTH, 4 * RET_WIDTH,
              4 * RET_WIDTH + MLA_Q_RANK, 4 * RET_WIDTH + MLA_Q_RANK + MLA_KV_RANK]
    for i in range(DEPTH):
        h = rms_norm(x, g_pre_mix[i])
        z = h @ w_in[i]
        q_r, k_r, v_r, g_r, c_q, c_kv, k_pe = jnp.split(z, splits, axis=-1)

        q_r = rope(q_r.reshape(B, S, RET_HEADS, RET_HEAD_DIM), positions)
        k_r = rope(k_r.reshape(B, S, RET_HEADS, RET_HEAD_DIM), positions)
        v_r = v_r.reshape(B, S, RET_HEADS, RET_HEAD_DIM)
        o_r = retention_chunkwise(q_r, k_r, v_r)
        mu = jnp.mean(o_r, axis=-1, keepdims=True)
        var = jnp.mean(jnp.square(o_r - mu), axis=-1, keepdims=True)
        o_r = ((o_r - mu) * lax.rsqrt(var + EPS)).reshape(B, S, RET_WIDTH)
        o_r = (o_r * g_ret_gn[i].astype(jnp.float32)).astype(x.dtype)
        y_ret = jax.nn.silu(g_r) * o_r

        q_m = (rms_norm(c_q, g_q_a[i]) @ w_uq[i]).reshape(B, S, MLA_HEADS, MLA_QK_DIM)
        q_m = jnp.concatenate([q_m[..., :MLA_NOPE_DIM], rope(q_m[..., MLA_NOPE_DIM:], positions)], axis=-1)
        kv = (rms_norm(c_kv, g_kv_a[i]) @ w_ukv[i]).reshape(B, S, MLA_HEADS, MLA_NOPE_DIM + MLA_V_DIM)
        k_nope, v_m = kv[..., :MLA_NOPE_DIM], kv[..., MLA_NOPE_DIM:]
        k_rot = rope(k_pe[:, :, None, :], positions)
        k_m = jnp.concatenate(
            [k_nope, jnp.broadcast_to(k_rot, (B, S, MLA_HEADS, MLA_ROPE_DIM))], axis=-1)
        y_mla = causal_block_attention(q_m, k_m, v_m)

        mix = jnp.concatenate([y_ret, y_mla], axis=-1) @ w_o[i]
        x = x + rms_norm(mix, g_post_mix[i])

        h = rms_norm(x, g_pre_ffn[i])
        u = causal_depthwise_conv(h @ w_up[i], conv_w[i], conv_b[i])
        gate, up = u[..., :D_FF], u[..., D_FF:]
        f = (jax.nn.gelu(gate, approximate=True) * up) @ w_down[i]
        x = x + rms_norm(f, g_post_ffn[i])

        e = (p[i] @ w_ple[i]) * jax.nn.sigmoid(x @ w_ple_gate[i] + b_ple_gate[i])
        x = x + rms_norm(e, g_post_ple[i])
    return x


_drawn_inputs = setup_inputs


def setup_inputs(seed=0):
    import zlib

    import numpy as np

    out = dict(_drawn_inputs(seed))
    spreads = {}
    factors = {'g_q_a': 7.072, 'g_kv_a': 3.981, 'conv_b': 3.911, 'b_ple_gate': 8.0, 'g_ret_gn': 8.0}
    for name, (base, spread) in spreads.items():
        noise = np.random.default_rng([zlib.crc32(name.encode()), seed]).standard_normal(out[name].shape)
        drawn = base * np.exp(spread * noise) if base else spread * noise
        out[name] = __import__('jax').numpy.asarray(drawn.astype(out[name].dtype))
    for name, factor in factors.items():
        out[name] = (out[name] * factor).astype(out[name].dtype)
    return out
```

```python
from contextlib import ExitStack

import numpy as np

import concourse.bass as bass
from concourse import mybir

P = 128
BANK = 512

D_MODEL = 1024
SEQ = 1024
PLE_DIM = 256
RET_HEADS = 8
RET_HEAD_DIM = 64
RET_WIDTH = RET_HEADS * RET_HEAD_DIM
MLA_HEADS = 8
MLA_NOPE_DIM = 64
MLA_ROPE_DIM = 32
MLA_QK_DIM = MLA_NOPE_DIM + MLA_ROPE_DIM
MLA_V_DIM = 64
MLA_Q_RANK = 256
MLA_KV_RANK = 128
LATENT = MLA_Q_RANK + MLA_KV_RANK + MLA_ROPE_DIM
D_FF = 2816
CONV_WIDTH = 3
ROPE_BASE = 10000.0
EPS = 1e-6

TILES = SEQ // P
KD = D_MODEL // P
PAIRS = RET_HEADS // 2
FF_TILES = D_FF // P
KQ = MLA_Q_RANK // P
HALF = RET_HEAD_DIM // 2
MHALF = MLA_ROPE_DIM // 2
NFREQ = HALF + MHALF
NEG = -3.0e38

F32 = mybir.dt.float32
F32R = mybir.dt.float32r
I32 = mybir.dt.int32
ALU = mybir.AluOpType
ACT = mybir.ActivationFunctionType
AX = mybir.AxisListType.X

COL_W0, COL_W1 = 0, 2 * FF_TILES
COL_PRE_MIX = 4 * FF_TILES
COL_PRE_FFN = COL_PRE_MIX + KD
COL_Q_A = COL_PRE_FFN + KD
COL_KV_A = COL_Q_A + KQ
COL_RET_GN = COL_KV_A + 1
ROWS_1 = COL_RET_GN + RET_WIDTH // P
COL_W2 = P
COL_BIAS = COL_W2 + 2 * FF_TILES
ROWS_2 = 4 * FF_TILES
COL_POS = 2 * P
COLS = COL_POS + TILES

C_IDENT = 0
C_NEG = C_IDENT + P
C_BEFORE = C_NEG + P
C_KSCALE = C_BEFORE + P
C_INNER = C_KSCALE + RET_HEADS
C_DECAY = C_INNER + RET_HEADS
C_FREQ = C_DECAY + PAIRS * P
CONSTS = C_FREQ + NFREQ


def shape_constants():
    c = np.zeros((P, CONSTS), np.float32)
    i = np.arange(P, dtype=np.float64)
    c[:, C_IDENT:C_IDENT + P] = np.eye(P)
    c[:, C_NEG:C_NEG + P] = np.where(i[None, :] > i[:, None], NEG, 0.0)
    c[:, C_BEFORE:C_BEFORE + P] = i[None, :] >= i[:, None]
    log_gamma = np.log1p(-np.exp2(-5.0 - np.arange(RET_HEADS)))
    c[:, C_KSCALE:C_KSCALE + RET_HEADS] = np.exp(-log_gamma[None, :] * (i[:, None] + 1)) * RET_HEAD_DIM ** -0.5
    c[:, C_INNER:C_INNER + RET_HEADS] = np.exp(log_gamma[None, :] * (i[:, None] + 1))
    same = (np.arange(P)[:, None] // RET_HEAD_DIM) == (np.arange(P)[None, :] // RET_HEAD_DIM)
    for pair in range(PAIRS):
        head = 2 * pair + np.arange(P) // RET_HEAD_DIM
        c[:, C_DECAY + pair * P:C_DECAY + (pair + 1) * P] = same * np.exp(log_gamma[head] * P)[:, None]
    ret = (ROPE_BASE ** (-np.arange(0, RET_HEAD_DIM, 2) / RET_HEAD_DIM)).astype(np.float32)
    mla = (ROPE_BASE ** (-np.arange(0, MLA_ROPE_DIM, 2) / MLA_ROPE_DIM)).astype(np.float32)
    c[:, C_FREQ:C_FREQ + NFREQ] = np.concatenate([ret, mla])[None, :]
    return c


def two_pi_pieces():
    rest, out = 2 * np.pi, []
    for _ in range(3):
        scale = 2.0 ** (np.floor(np.log2(rest)) - 7)
        piece = np.floor(rest / scale) * scale
        out.append(float(piece))
        rest -= piece
    return out + [float(np.float32(rest))]


class Inputs:

    def __init__(self, x, p, positions, w_in, w_uq, w_ukv, w_o, g_pre_mix, g_post_mix, g_q_a, g_kv_a, g_ret_gn, w_up,
                 conv_w, conv_b, w_down, g_pre_ffn, g_post_ffn, w_ple, w_ple_gate, b_ple_gate, g_post_ple, consts, out, x1):
        self.x, self.p, self.positions, self.consts, self.out, self.x1 = x, p, positions, consts, out, x1
        self.w_in, self.w_uq, self.w_ukv, self.w_o = w_in, w_uq, w_ukv, w_o
        self.w_up, self.conv_w, self.conv_b, self.w_down = w_up, conv_w, conv_b, w_down
        self.w_ple, self.w_ple_gate, self.b_ple_gate = w_ple, w_ple_gate, b_ple_gate
        self.g_pre_mix, self.g_post_mix, self.g_q_a, self.g_kv_a = g_pre_mix, g_post_mix, g_q_a, g_kv_a
        self.g_ret_gn, self.g_pre_ffn, self.g_post_ffn, self.g_post_ple = g_ret_gn, g_pre_ffn, g_post_ffn, g_post_ple


class Keep:
    pass


class Own:

    def __init__(self, eng, sem):
        self.eng, self.sem, self.n = eng, sem, 0

    def __call__(self, ins):
        self.n += 1
        ins.then_inc(self.sem, 1)
        self.eng.wait_ge(self.sem, self.n)


def split_product(eng, out, hi, lo, whi, wlo, first, last):
    eng.matmul(out, hi, whi, start=first, stop=False)
    eng.matmul(out, hi, wlo, start=False, stop=False)
    return eng.matmul(out, lo, whi, start=False, stop=last)


def retention_and_projection(nc, io, keep):
    groups = [("q", 0, 512), ("k", 512, 512), ("v", 1024, 512), ("latent", 4 * RET_WIDTH, LATENT), ("gate", 3 * RET_WIDTH, 512)]
    SLOTS = len(groups) * TILES
    SLICES = len(groups) * KD
    RAW = 4
    RING = 9
    RET0 = 3 * TILES

    with ExitStack() as ctx:
        def sb(name, shape, dt=F32):
            return ctx.enter_context(nc.sbuf_tensor(name, shape, dt))

        def sem(name):
            return ctx.enter_context(nc.semaphore(name))

        kret = sb("kret", [P, TILES, RET_WIDTH])
        vret = sb("vret", [P, TILES, RET_WIDTH])
        wraw = sb("wraw", [P, RAW, 512])
        wHi = sb("wHi", [P, RING, 512], F32R)
        wLo = sb("wLo", [P, RING, 512], F32R)
        scratch = sb("scratchA", [P, 8, 512])
        mrope = sb("mrope", [P, 2, 2, 512])
        rows1 = sb("rows1", [P, P])
        rows2 = sb("rows2", [P, P])
        posr = sb("posr", [TILES, 2, P])
        posi = sb("posi", [TILES, P], I32)
        small = sb("small", [P, 8, 8])
        junk = sb("junkA", [P, MLA_Q_RANK + MLA_KV_RANK])
        cosr = sb("cosr", [P, TILES, HALF])
        sinr = sb("sinr", [P, TILES, HALF])
        ctab = sb("ctab", [P, CONSTS - C_BEFORE])
        ps = ctx.enter_context(nc.psum_tensor("psA", [P, 8, BANK], F32))

        xt = scratch[:, 0:4, :].rearrange("p (b h) n -> p b (h n)", b=2)
        ht = scratch[:, 4:8, :].rearrange("p (b h) n -> p b (h n)", b=2)
        q_zero = scratch[:, 0:2, :].rearrange("p a n -> p (a n)").rearrange("p (r z c) -> p r z c", r=PAIRS, z=2)
        kT = scratch[:, 2, :].rearrange("p (r c) -> p r c", r=PAIRS)
        qT = scratch[:, 3:5, :].rearrange("p b (r c) -> p b r c", r=PAIRS)
        sT = scratch[:, 5:7, :].rearrange("p a n -> p (a n)").rearrange("p (h c) -> p h c", h=RET_HEADS)
        state = scratch[:, 7, :]
        orow = mrope[:, 0, 0, :]
        osq = mrope[:, 0, 1, :]
        gate = mrope[:, 1, :, :]
        NA = TILES * NFREQ
        angle = mrope[:, 0, 0, 0:NA]
        turns = mrope[:, 0, 1, 0:NA]
        cosin = mrope[:, 1, 0, 0:NA]

        def const(col, n):
            return ctab[:, col - C_BEFORE:col - C_BEFORE + n]

        ident = keep.ident
        ssx = small[:, 0, :]
        rstdx = small[:, 1, :]
        neghalf = keep.neghalf
        meanv = small[:, 3, :]
        varv = small[:, 4, :]
        rstdo = small[:, 5, :]
        scr8 = small[:, 6, :]

        small_in = sem("small_in")
        x_in = [sem("x_in0"), sem("x_in1")]
        raw_in = [sem(f"raw_in{i}") for i in range(RAW)]
        w_hi = sem("w_hi")
        w_lo = sem("w_lo")
        slice_used = sem("slice_used")
        sq_done = sem("sq_done")
        rstd_done = sem("rstd_done")
        h_done = sem("h_done")
        turned = sem("turned")
        hT_hi = sem("hT_hi")
        hT_lo = sem("hT_lo")
        z_ready = sem("z_ready")
        z_dve = sem("z_used_dve")
        z_act = sem("z_used_act")
        rope_out = sem("rope_out")
        setup_turned = sem("setup_turned")
        pos_ready = sem("pos_ready")
        cols_ready = sem("cols_ready")
        trig_arg = sem("trig_arg")
        trig_done = sem("trig_done")
        dve_own = sem("dve_ownA")
        act_own = sem("act_ownA")
        pool_own = sem("pool_ownA")
        zeros_done = sem("zeros_done")
        qk_turned = sem("qk_turned")
        kT_copied = sem("kT_copied")
        qT_copied = sem("qT_copied")
        qz_copied = sem("qz_copied")
        scores_done = sem("scores_done")
        masked = sem("masked")
        out_done = sem("out_done")
        kv_done = sem("kv_done")
        state_done = sem("state_done")
        out_read = sem("out_read")
        mean_sub = sem("mean_sub")
        osq_done = sem("osq_done")
        var_done = sem("var_done")
        ornorm = sem("rstd_head")
        gate_done = sem("gate_done")
        y_done = sem("y_done")

        w3 = io.w_in[0].rearrange("(k p) n -> p k n", p=P)
        xr = io.x[0].rearrange("(t p) d -> t p d", p=P)

        POOL_BEFORE_Y = 1 + 3 * TILES + 4
        block = ctx.enter_context(nc.Block())

        @block.sync
        def _(sp):
            sp.dma_start(ident, io.consts[:, C_IDENT:C_IDENT + P]).then_inc(small_in, 16)
            cw = io.conv_w[0].rearrange("w (j p) -> w j p", p=P)
            F2 = 2 * FF_TILES
            pieces = [(rows1, COL_W0, cw[0]), (rows1, COL_W1, cw[1]),
                      (rows1, COL_PRE_MIX, io.g_pre_mix.rearrange("a (j p) -> (a j) p", p=P)),
                      (rows1, COL_PRE_FFN, io.g_pre_ffn.rearrange("a (j p) -> (a j) p", p=P)),
                      (rows1, COL_Q_A, io.g_q_a.rearrange("a (j p) -> (a j) p", p=P)),
                      (rows1, COL_KV_A, io.g_kv_a.rearrange("a (j p) -> (a j) p", p=P)),
                      (rows1, COL_RET_GN, io.g_ret_gn.rearrange("a (j p) -> (a j) p", p=P)),
                      (rows2, 0, cw[2]), (rows2, F2, io.conv_b.rearrange("a (j p) -> (a j) p", p=P))]
            for tile, row, src in pieces:
                sp.dma_start(tile[row:row + src.shape[0], :], src).then_inc(small_in, 16)
            sp.dma_start(posi[:, :], io.positions.rearrange("b (t p) -> (b t) p", p=P)).then_inc(small_in, 16)
            sp.dma_start(ctab[:, :], io.consts[:, C_BEFORE:CONSTS]).then_inc(small_in, 16)
            sp.dma_start(keep.neg, io.consts[:, C_NEG:C_NEG + P]).then_inc(small_in, 16)

            def load_x(t):
                if t >= 2:
                    sp.wait_ge(h_done, t - 1)
                sp.dma_start(xt[:, t % 2, :], xr[t]).then_inc(x_in[t % 2], 16)

            def load_w(s):
                name, col, width = groups[s // KD]
                if s >= RAW:
                    sp.wait_ge(w_lo, s - RAW + 1)
                sp.dma_start(wraw[:, s % RAW, 0:width], w3[:, s % KD, col:col + width]).then_inc(raw_in[s % RAW], 16)

            load_x(0)
            load_x(1)
            for s in range(KD):
                load_w(s)
            for t in range(2, TILES):
                load_x(t)
            for s in range(KD, SLICES):
                load_w(s)

        def slices_before(n, after):
            gi, t = divmod(n, TILES)
            if gi + 1 >= len(groups):
                return []
            spare = RING - KD
            if t == 1 and not after:
                return [(gi + 1) * KD + k for k in range(spare)]
            if t == TILES - 1 and not after:
                return [(gi + 1) * KD + k for k in range(spare, KD)]
            return []

        @block.gpsimd
        def _(pool):
            own = Own(pool, pool_own)
            own(pool.memset(neghalf, -0.5))

            def rope_rows(n):
                t = n % TILES
                rows = keep.q_y if n < TILES else kret
                dst = rows[:, t, :].rearrange("p (h z d) -> p h z d", h=RET_HEADS, z=2)
                cs = mrope[:, n % 2, 0, :].rearrange("p (h z d) -> p h z d", h=RET_HEADS, z=2)
                sn = mrope[:, n % 2, 1, :].rearrange("p (h z d) -> p h z d", h=RET_HEADS, z=2)
                pool.wait_ge(z_dve, n + 1)
                pool.tensor_tensor(dst[:, :, 0, :], cs[:, :, 0, :], sn[:, :, 1, :], ALU.subtract).then_inc(rope_out, 1)
                pool.tensor_tensor(dst[:, :, 1, :], cs[:, :, 1, :], sn[:, :, 0, :], ALU.add).then_inc(rope_out, 1)

            for t in range(TILES):
                pool.wait_ge(sq_done, t + 1)
                own(pool.tensor_scalar(scr8[:, t:t + 1], ssx[:, t:t + 1], 1.0 / D_MODEL, EPS, ALU.mult, ALU.add))
                pool.tensor_tensor(rstdx[:, t:t + 1], scr8[:, t:t + 1], neghalf[:, 0:1], ALU.pow).then_inc(rstd_done, 1)
                if t >= 3:
                    rope_rows(t - 3)
            for n in range(TILES - 3, 2 * TILES):
                rope_rows(n)
            pool.wait_ge(rope_out, 4 * TILES)
            for t in range(TILES):
                dst = kret[:, t, :].rearrange("p (h d) -> p h d", h=RET_HEADS)
                own(pool.tensor_tensor(dst, dst, const(C_KSCALE, RET_HEADS).unsqueeze(2).broadcast_to([P, RET_HEADS, RET_HEAD_DIM]), ALU.mult))
                if t == 0:
                    pool.wait_ge(turned, TILES)
                    pool.memset(q_zero[64:128, :, 0, :], 0.0).then_inc(zeros_done, 1)
                    pool.wait_ge(zeros_done, 1)
                    pool.memset(q_zero[0:64, :, 1, :], 0.0).then_inc(zeros_done, 1)
                    pool.wait_ge(zeros_done, 2)
            for c in range(TILES):
                pool.wait_ge(var_done, c + 1)
                own(pool.tensor_scalar(varv, varv, 1.0 / RET_HEAD_DIM, EPS, ALU.mult, ALU.add))
                pool.tensor_tensor(rstdo, varv, neghalf, ALU.pow).then_inc(ornorm, 1)
            pool.wait_ge(z_act, 2 * TILES)
            for part, width in enumerate((MLA_Q_RANK, MLA_KV_RANK)):
                lat = keep.rstd_lat[:, part, :]
                own(pool.tensor_scalar(lat, lat, 1.0 / width, EPS, ALU.mult, ALU.add))
                own(pool.tensor_tensor(lat, lat, neghalf, ALU.pow))
            for c in range(TILES):
                y = keep.q_y[:, c, :]
                pool.wait_ge(gate_done, c + 1)
                pool.wait_ge(y_done, c + 1)
                own(pool.tensor_tensor(y, y, gate[:, c % 2, :], ALU.mult))

        @block.scalar
        def _(act):
            own = Own(act, act_own)

            def split_hi(s):
                gi, k = divmod(s, KD)
                width = groups[gi][2]
                act.wait_ge(raw_in[s % RAW], 16 * (s // RAW + 1))
                if s == 0:
                    act.wait_ge(cols_ready, 1)
                if s >= RING:
                    before, kb = divmod(s - RING, KD)
                    if kb == KD - 1:
                        act.wait_ge(z_ready, (before + 1) * TILES)
                    else:
                        act.wait_ge(slice_used, before * (KD - 1) + kb + 1)
                act.activation(wHi[:, s % RING, 0:width], wraw[:, s % RAW, 0:width], ACT.Identity,
                               scale=keep.cols[:, COL_PRE_MIX + k:COL_PRE_MIX + k + 1]).then_inc(w_hi, 1)

            def hT_hi_part(t):
                act.wait_ge(turned, t + 1)
                bank = 2 + 2 * (t % 2)
                act.activation(keep.actHi[:, :, t * P:(t + 1) * P],
                               ps[:, bank:bank + 2, :].rearrange("p a (b c) -> p (a b) c", c=P), ACT.Copy).then_inc(hT_hi, 1)

            for t in range(TILES):
                act.wait_ge(x_in[t % 2], 16 * (t // 2 + 1))
                if t >= 2:
                    act.wait_ge(turned, t - 1)
                act.activation(ht[:, t % 2, :], xt[:, t % 2, :], ACT.Square, accum_out=ssx[:, t:t + 1]).then_inc(sq_done, 1)
                if t < 2:
                    for s in range(4 * t, 4 * t + 4):
                        split_hi(s)
                if t >= 1:
                    hT_hi_part(t - 1)
                if t == 1:
                    act.wait_ge(trig_arg, 2)
                    act.activation(keep.sin, angle.rearrange("p (t f) -> p t f", t=TILES), ACT.Sin).then_inc(trig_done, 1)
                    act.activation(keep.cos, cosin.rearrange("p (t f) -> p t f", t=TILES), ACT.Sin, scale=-1.0).then_inc(trig_done, 1)
            hT_hi_part(TILES - 1)
            for s in slices_before(1, False) + slices_before(TILES - 1, False):
                split_hi(s)
            for n in range(TILES, SLOTS + 2):
                if n < SLOTS:
                    gi, t = divmod(n, TILES)
                    for s in slices_before(n, False):
                        split_hi(s)
                    name, col, width = groups[gi]
                    if gi >= 2:
                        act.wait_ge(z_ready, n + 1)
                        z = ps[:, n % 2, 0:width]
                        if name == "v":
                            act.activation(vret[:, t, :], z, ACT.Copy).then_inc(z_act, 1)
                        elif name == "latent":
                            own(act.activation(keep.latent[:, t, :], z, ACT.Copy))
                            own(act.activation(junk[:, 0:MLA_Q_RANK], z[:, 0:MLA_Q_RANK], ACT.Square,
                                               accum_out=keep.rstd_lat[:, 0, t:t + 1]))
                            act.activation(junk[:, MLA_Q_RANK:MLA_Q_RANK + MLA_KV_RANK], z[:, MLA_Q_RANK:MLA_Q_RANK + MLA_KV_RANK],
                                           ACT.Square, accum_out=keep.rstd_lat[:, 1, t:t + 1]).then_inc(z_act, 1)
                            act.wait_ge(z_act, n + 1 - 2 * TILES)
                        else:
                            if t >= 2:
                                act.wait_ge(pool_own, POOL_BEFORE_Y + t - 1)
                            else:
                                act.wait_ge(rope_out, 4 * TILES)
                            act.activation(gate[:, t % 2, :], z, ACT.Silu).then_inc(gate_done, 1)
                c = n - RET0
                if 0 <= c < TILES:
                    act.wait_ge(qk_turned, c + 1)
                    if c >= 1:
                        act.wait_ge(scores_done, c)
                    act.activation(kT, ps[:, 3, :].rearrange("p (r c) -> p r c", r=PAIRS), ACT.Copy).then_inc(kT_copied, 1)
                    if c >= 2:
                        act.wait_ge(out_done, c - 1)
                    act.activation(qT[:, c % 2], ps[:, 2, :].rearrange("p (r c) -> p r c", r=PAIRS), ACT.Copy).then_inc(qT_copied, 1)
                c = n - RET0 - 2
                if 0 <= c < TILES:
                    act.wait_ge(mean_sub, c + 1)
                    act.activation(osq, orow, ACT.Square).then_inc(osq_done, 1)

        @block.vector
        def _(dve):
            own = Own(dve, dve_own)
            dve.wait_ge(small_in, 16 * 13)
            own(dve.tensor_copy(posr[:, 0, :], posi[:, :]))
            dve.sem_inc(pos_ready, 1)
            dve.wait_ge(setup_turned, 1)
            own(dve.tensor_copy(keep.cols[:, 0:ROWS_1], ps[:, 6, 0:ROWS_1]))
            own(dve.tensor_copy(keep.cols[:, COL_W2:COL_W2 + ROWS_2], ps[:, 6, COL_W2:COL_W2 + ROWS_2]))
            own(dve.tensor_copy(keep.cols[:, COL_POS:COLS], ps[:, 6, COL_POS:COLS]))
            dve.sem_inc(cols_ready, 1)
            def split_lo(s):
                gi, k = divmod(s, KD)
                width = groups[gi][2]
                dve.wait_ge(w_hi, s + 1)
                dve.scalar_tensor_tensor(wLo[:, s % RING, 0:width], wraw[:, s % RAW, 0:width],
                                         keep.cols[:, COL_PRE_MIX + k:COL_PRE_MIX + k + 1],
                                         wHi[:, s % RING, 0:width].bitcast(F32), ALU.mult, ALU.subtract).then_inc(w_lo, 1)

            def norm_x(t):
                dve.wait_ge(rstd_done, t + 1)
                dve.tensor_scalar(ht[:, t % 2, :], xt[:, t % 2, :], rstdx[:, t:t + 1], None, ALU.mult).then_inc(h_done, 1)

            def hT_lo_part(t):
                dve.wait_ge(hT_hi, t + 1)
                bank = 2 + 2 * (t % 2)
                dve.tensor_tensor(keep.actLo[:, :, t * P:(t + 1) * P],
                                  ps[:, bank:bank + 2, :].rearrange("p a (b c) -> p (a b) c", c=P),
                                  keep.actHi[:, :, t * P:(t + 1) * P].bitcast(F32), ALU.subtract).then_inc(hT_lo, 1)

            def rope(n):
                t = n % TILES
                z = ps[:, n % 2, :].rearrange("p (g d) -> p g d", d=HALF)
                dve.wait_ge(z_ready, n + 1)
                if n == 0:
                    dve.wait_ge(trig_done, 2)
                if n >= 2:
                    dve.wait_ge(rope_out, 2 * (n - 1))
                cs = mrope[:, n % 2, 0, :].rearrange("p (g d) -> p g d", d=HALF)
                sn = mrope[:, n % 2, 1, :].rearrange("p (g d) -> p g d", d=HALF)
                own(dve.tensor_tensor(cs, z, keep.cos[:, t, 0:HALF].unsqueeze(1).broadcast_to([P, 2 * RET_HEADS, HALF]), ALU.mult))
                dve.tensor_tensor(sn, z, keep.sin[:, t, 0:HALF].unsqueeze(1).broadcast_to([P, 2 * RET_HEADS, HALF]),
                                  ALU.mult).then_inc(z_dve, 1)

            def zero_padded_q(c):
                dve.wait_ge(qk_turned, c + 1)
                if c == 0:
                    dve.wait_ge(zeros_done, 2)
                if c >= 1:
                    dve.wait_ge(scores_done, c)
                src = ps[:, 2, :].rearrange("p (r c) -> p r c", r=PAIRS)
                dve.wait_ge(qT_copied, c + 1)
                dve.tensor_copy(q_zero[0:64, :, 0, :], src[0:64]).then_inc(qz_copied, 1)
                dve.tensor_copy(q_zero[64:128, :, 1, :], src[64:128]).then_inc(qz_copied, 1)

            def mask_scores(c):
                dve.wait_ge(scores_done, c + 1)
                src = ps[:, 4:6, :].rearrange("p a (h c) -> p (a h) c", c=P)
                dve.tensor_tensor(sT, src, const(C_BEFORE, P).unsqueeze(1).broadcast_to([P, RET_HEADS, P]),
                                  ALU.mult).then_inc(masked, 1)

            def heads(ap):
                return ap.rearrange("p (h d) -> p h d", h=RET_HEADS)

            def each_head(ap):
                return ap.unsqueeze(2).broadcast_to([P, RET_HEADS, RET_HEAD_DIM])

            def finish_chunk(c):
                dve.wait_ge(out_done, c + 1)
                dve.wait_ge(rope_out, 4 * TILES)
                if c >= 1:
                    dve.wait_ge(osq_done, c)
                dve.tensor_tensor(heads(orow), heads(ps[:, 7, :]), each_head(const(C_INNER, RET_HEADS)), ALU.mult).then_inc(out_read, 1)
                if c < TILES - 1:
                    dve.wait_ge(kv_done, c + 1)
                    if c > 0:
                        own(dve.tensor_tensor(state, ps[:, 6, :], state, ALU.add))
                        dve.tensor_tensor(state, state, const(C_DECAY, PAIRS * P), ALU.mult).then_inc(state_done, 1)
                    else:
                        dve.tensor_tensor(state, ps[:, 6, :], const(C_DECAY, PAIRS * P), ALU.mult).then_inc(state_done, 1)
                dve.wait_ge(out_read, c + 1)
                own(dve.tensor_reduce(meanv, heads(orow), AX, ALU.add))
                own(dve.tensor_scalar(meanv, meanv, 1.0 / RET_HEAD_DIM, None, ALU.mult))
                dve.tensor_tensor(heads(orow), heads(orow), each_head(meanv), ALU.subtract).then_inc(mean_sub, 1)
                dve.wait_ge(osq_done, c + 1)
                if c >= 1:
                    dve.wait_ge(ornorm, c)
                dve.tensor_reduce(varv, heads(osq), AX, ALU.add).then_inc(var_done, 1)
                dve.wait_ge(ornorm, c + 1)
                dve.tensor_tensor(heads(keep.q_y[:, c, :]), heads(orow), each_head(rstdo), ALU.mult).then_inc(y_done, 1)
                dve.wait_ge(y_done, c + 1)

            def angles():
                a3 = angle.rearrange("p (t f) -> p t f", t=TILES)
                own(dve.tensor_tensor(a3, keep.cols[:, COL_POS:COLS].unsqueeze(2).broadcast_to([P, TILES, NFREQ]),
                                      const(C_FREQ, NFREQ).unsqueeze(1).broadcast_to([P, TILES, NFREQ]), ALU.mult))
                magic = 1.5 * 2.0 ** 23
                for unit in (4096.0, 1.0):
                    own(dve.tensor_scalar(turns, angle, 1.0 / (2 * np.pi * unit), magic, ALU.mult, ALU.add))
                    own(dve.tensor_scalar(turns, turns, -magic, unit, ALU.add, ALU.mult))
                    for piece in two_pi_pieces():
                        own(dve.scalar_tensor_tensor(angle, turns, -piece, angle, ALU.mult, ALU.add))
                pi_below = 3.1415925
                own(dve.tensor_scalar(angle, angle, pi_below, -pi_below, ALU.min, ALU.max))
                dve.sem_inc(trig_arg, 1)
                own(dve.scalar_tensor_tensor(turns, angle, -1.0, angle, ALU.mult, ALU.max))
                dve.tensor_scalar(cosin, turns, -float(np.pi / 2), None, ALU.add).then_inc(trig_arg, 1)

            norm_x(0)
            for s in range(4):
                split_lo(s)
            for t in range(1, TILES):
                norm_x(t)
                if t == 1:
                    for s in range(4, KD):
                        split_lo(s)
                hT_lo_part(t - 1)
                if t == 1:
                    angles()
                if t >= 2:
                    rope(t - 2)
            hT_lo_part(TILES - 1)
            rope(TILES - 2)
            for s in slices_before(1, False) + slices_before(TILES - 1, False):
                split_lo(s)
            rope(TILES - 1)
            for n in range(TILES, SLOTS + 2):
                if n < SLOTS:
                    for s in slices_before(n, False):
                        split_lo(s)
                    if n < 2 * TILES:
                        rope(n)
                if 0 <= n - RET0 - 2 < TILES:
                    finish_chunk(n - RET0 - 2)
                if 0 <= n - RET0 - 1 < TILES:
                    mask_scores(n - RET0 - 1)
                if 0 <= n - RET0 < TILES:
                    zero_padded_q(n - RET0)

        @block.tensor
        def _(pe):
            pe.wait_ge(small_in, 16 * 13)
            pe.transpose(ps[:, 6, 0:ROWS_1], rows1[0:ROWS_1, :], ident[0:ROWS_1, 0:ROWS_1])
            pe.transpose(ps[:, 6, COL_W2:COL_W2 + ROWS_2], rows2[0:ROWS_2, :], ident[0:ROWS_2, 0:ROWS_2])
            pe.wait_ge(pos_ready, 1)
            pe.transpose(ps[:, 6, COL_POS:COLS], posr[:, 0, :], ident[0:TILES, 0:TILES]).then_inc(setup_turned, 1)

            def turn_x(t):
                pe.wait_ge(h_done, t + 1)
                if t >= 2:
                    pe.wait_ge(hT_lo, t - 1)
                bank = 2 + 2 * (t % 2)
                for k in range(KD):
                    last = pe.transpose(ps[:, bank + k // 4, (k % 4) * P:(k % 4 + 1) * P], ht[:, t % 2, k * P:(k + 1) * P], ident)
                last.then_inc(turned, 1)

            def product(n):
                gi, t = divmod(n, TILES)
                width = groups[gi][2]
                if gi == 0:
                    pe.wait_ge(hT_lo, t + 1)
                if n >= 2:
                    if n - 2 < 2 * TILES:
                        pe.wait_ge(z_dve, n - 1)
                    elif n - 2 < 4 * TILES:
                        pe.wait_ge(z_act, n - 1 - 2 * TILES)
                    else:
                        pe.wait_ge(gate_done, n - 1 - 4 * TILES)
                for k in range(KD):
                    s = gi * KD + k
                    if t == 0:
                        pe.wait_ge(w_lo, s + 1)
                    last = split_product(pe, ps[:, n % 2, 0:width],
                                         keep.actHi[:, k, t * P:(t + 1) * P], keep.actLo[:, k, t * P:(t + 1) * P],
                                         wHi[:, s % RING, 0:width], wLo[:, s % RING, 0:width], k == 0, k == KD - 1)
                    if t == TILES - 1 and k < KD - 1:
                        last.then_inc(slice_used, 1)
                last.then_inc(z_ready, 1)

            def turn_chunk(c):
                if c == 0:
                    pe.wait_ge(pool_own, 1 + TILES + 1)
                    pe.wait_ge(hT_lo, TILES)
                else:
                    pe.wait_ge(pool_own, 1 + TILES + 1 + c)
                    pe.wait_ge(kT_copied, c)
                    pe.wait_ge(qz_copied, 2 * c)
                for pair in range(PAIRS):
                    pe.transpose(ps[:, 2, pair * P:(pair + 1) * P], keep.q_y[:, c, pair * P:(pair + 1) * P], ident)
                for pair in range(PAIRS):
                    last = pe.transpose(ps[:, 3, pair * P:(pair + 1) * P], kret[:, c, pair * P:(pair + 1) * P], ident)
                last.then_inc(qk_turned, 1)

            def score_chunk(c):
                pe.wait_ge(kT_copied, c + 1)
                pe.wait_ge(qz_copied, 2 * c + 2)
                if c >= 1:
                    pe.wait_ge(masked, c)
                for pair in range(PAIRS):
                    last = pe.matmul(ps[:, 4 + pair // 2, (pair % 2) * 256:(pair % 2 + 1) * 256], kT[:, pair, :],
                                     q_zero[:, pair, :, :], start=True, stop=True)
                last.then_inc(scores_done, 1)

            def finish_chunk(c):
                pe.wait_ge(masked, c + 1)
                if c >= 1:
                    pe.wait_ge(state_done, c)
                    pe.wait_ge(out_read, c)
                else:
                    pe.wait_ge(z_act, TILES)
                for pair in range(PAIRS):
                    cols = slice(pair * P, (pair + 1) * P)
                    if c >= 1:
                        pe.matmul(ps[:, 7, cols], qT[:, c % 2, pair, :], state[:, cols], start=True, stop=False, skip_group_check=True)
                    for z in range(2):
                        h = 2 * pair + z
                        hc = slice(h * RET_HEAD_DIM, (h + 1) * RET_HEAD_DIM)
                        last = pe.matmul(ps[:, 7, hc], sT[:, h, :], vret[:, c, hc], start=(c == 0), stop=True,
                                         skip_group_check=True)
                last.then_inc(out_done, 1)
                if c < TILES - 1:
                    for pair in range(PAIRS):
                        cols = slice(pair * P, (pair + 1) * P)
                        last = pe.matmul(ps[:, 6, cols], kret[:, c, cols], vret[:, c, cols], start=True, stop=True)
                    last.then_inc(kv_done, 1)

            turn_x(0)
            turn_x(1)
            for n in range(SLOTS + 2):
                if n < SLOTS:
                    product(n)
                if 2 <= n + 2 < TILES:
                    turn_x(n + 2)
                if 0 <= n - RET0 - 2 < TILES:
                    finish_chunk(n - RET0 - 2)
                if 0 <= n - RET0 - 1 < TILES:
                    score_chunk(n - RET0 - 1)
                if 0 <= n - RET0 < TILES:
                    turn_chunk(n - RET0)


def latent_attention(nc, io, keep):
    SCALE = MLA_QK_DIM ** -0.5
    BLOCK_ROWS = 4
    STEPS = MLA_HEADS * TILES
    LAG = 3
    ROT = MLA_NOPE_DIM
    PT_OFF = [j * BANK for j in range(5)] + [5 * BANK, 5 * BANK + 384, 5 * BANK + 768]
    PT_COLS = PT_OFF[-1] + P

    def groups_of(m):
        i = m % TILES
        if i < BLOCK_ROWS:
            return [(0, [(0, i + 1)])]
        tail = [(4, 1)] + ([(5, i - 4)] if i > 4 else [])
        return [(0, [(0, 4)]), (4, tail)]

    def pt_view(buf, m, first, count):
        i = m % TILES
        if i < BLOCK_ROWS:
            start, step = i * P, BANK - P
        elif first == 0:
            start, step = (i - BLOCK_ROWS) * P, BANK
        elif first == 4:
            start, step = PT_OFF[4] + (i - 4) * P, P
        else:
            start, step = PT_OFF[5] + (i - 5) * P, PT_OFF[6] - PT_OFF[5] - P
        if count == 1:
            return buf[:, start:start + P].unsqueeze(1)
        return bass_view(buf, start, step, count)

    def bass_view(buf, start, step, count):
        width = count * step
        if start + width <= buf.shape[1]:
            return buf[:, start:start + width].rearrange("p (j s) -> p j s", s=step)[:, :, 0:P]
        lead = start + width - buf.shape[1]
        return buf[:, start - lead:start - lead + width].rearrange("p (j s) -> p j s", s=step)[:, :, lead:lead + P]

    ROW_AT = [21, 15, 8, 0, 21, 15, 8, 0]
    ROWS = 4

    bank_of = {}
    for m in range(STEPS):
        for b, _ in groups_of(m):
            bank_of[(m, b)] = len(bank_of)
    through = [max(v for (mm, _), v in bank_of.items() if mm == m) + 1 for m in range(STEPS)]

    with ExitStack() as ctx:
        def sb(name, shape, dt=F32):
            return ctx.enter_context(nc.sbuf_tensor(name, shape, dt))

        def sem(name):
            return ctx.enter_context(nc.semaphore(name))

        wq = [sb("wqHi", [P, KQ, MLA_HEADS, P], F32R), sb("wqLo", [P, KQ, MLA_HEADS, P], F32R)]
        wk = [sb("wkHi", [P, MLA_HEADS, MLA_NOPE_DIM], F32R), sb("wkLo", [P, MLA_HEADS, MLA_NOPE_DIM], F32R)]
        v = [sb("vHi", [P, TILES, MLA_HEADS * MLA_V_DIM], F32R), sb("vLo", [P, TILES, MLA_HEADS * MLA_V_DIM], F32R)]
        table = sb("rope_table", [P, SEQ])
        q1 = [sb("q1Hi", [P, SEQ], F32R), sb("q1Lo", [P, SEQ], F32R)]
        k0 = [sb("k0Hi", [P, SEQ], F32R), sb("k0Lo", [P, SEQ], F32R)]
        k1 = [sb("k1Hi", [P, SEQ], F32R), sb("k1Lo", [P, SEQ], F32R)]
        identR = sb("identR", [P, P], F32R)
        maskR = sb("maskR", [P, P], F32R)
        st = sb("softmax_small", [P, 4, 4])
        act_parts = (keep.actHi, keep.actLo)
        cT = [a[:, 0:KQ + 1, :] for a in act_parts]
        qbuf = [[a[:, KQ + 1, :] for a in act_parts], [a[:, :] for a in q1]]
        kbuf = [[a[:, :] for a in k0], [a[:, :] for a in k1]]
        prob_rows = keep.latent.rearrange("p t n -> p (t n)")

        def prob(m):
            i = m % TILES
            return prob_rows[:, ROW_AT[i] * P:(ROW_AT[i] + i + 1) * P]

        lat = keep.latent
        top, neg_top, total, inverse = (st[:, i, :] for i in range(4))

        with ExitStack() as early:
            def eb(name, shape, dt=F32):
                return early.enter_context(nc.sbuf_tensor(name, shape, dt))
            raw_uq = eb("raw_uq", [P, KQ, MLA_HEADS, MLA_QK_DIM])
            raw_ukv = eb("raw_ukv", [P, MLA_HEADS, MLA_NOPE_DIM + MLA_V_DIM])
            wv = [eb("wvHi", [P, MLA_HEADS * MLA_V_DIM], F32R), eb("wvLo", [P, MLA_HEADS * MLA_V_DIM], F32R)]
            krow = eb("krow", [P, TILES, P])
            trow = eb("trow", [P, TILES, P])
            ktmp = eb("ktmp", [P, 2, TILES, MLA_ROPE_DIM])
        pT = [sb("pTHi", [P, PT_COLS], F32R)[:, :], sb("pTLo", [P, PT_COLS], F32R)[:, :]]
        ps = ctx.enter_context(nc.psum_tensor("psB", [P, 8, BANK], F32))

        uq_in = sem("uq_in")
        ukv_in = sem("ukv_in")
        lat_normed = sem("lat_normed")
        krow_ready = sem("krow_ready")
        trow_ready = sem("trow_ready")
        lat_turned = sem("lat_turned")
        lat_hi = sem("lat_hi")
        lat_lo = sem("lat_lo")
        rot_turned = sem("rot_turned")
        tab_turned = sem("tab_turned")
        rot_hi = sem("rot_hi")
        rot_lo = sem("rot_lo")
        tab_copied = sem("tab_copied")
        mask_ready = sem("mask_ready")
        w_hi = sem("w_hiB")
        w_lo = sem("w_loB")
        v_done = sem("v_done")
        v_hi = sem("v_hi")
        v_lo = sem("v_lo")
        proj_done = sem("proj_done")
        proj_roped = sem("proj_roped")
        proj_hi = sem("proj_hi")
        proj_lo = sem("proj_lo")
        score_done = sem("score_done")
        top_ready = sem("top_ready")
        exp_done = sem("exp_done")
        inverse_ready = sem("inverse_ready")
        prob_ready = sem("prob_ready")
        pt_turned = sem("pt_turned")
        pt_hi = sem("pt_hi")
        pt_lo = sem("pt_lo")
        pv_done = sem("pv_done")
        out_hi = sem("out_hi")
        out_lo = sem("out_lo")
        dve_own = sem("dve_ownB")
        act_own = sem("act_ownB")
        pool_own = sem("pool_ownB")

        PIECES = [(0, 0, MLA_QK_DIM), (MLA_QK_DIM, MLA_QK_DIM - MHALF, MHALF), (MLA_QK_DIM + MHALF, MLA_NOPE_DIM, MHALF)]
        PIECE_AT = [0, 2, 4, 6]
        gain_kv = keep.cols[:, COL_KV_A:COL_KV_A + 1]

        def gain_q(k):
            return keep.cols[:, COL_Q_A + k:COL_Q_A + k + 1]

        def projections(m):
            h, i = divmod(m, TILES)
            return [(h + 1, PIECE_AT.index(i))] if 0 <= h < MLA_HEADS - 1 and i in PIECE_AT else []

        def chunk_of(t):
            return [t // BLOCK_ROWS] if 0 <= t < STEPS and t % BLOCK_ROWS == BLOCK_ROWS - 1 else []

        block = ctx.enter_context(nc.Block())

        @block.sync
        def _(sp):
            sp.dma_start(raw_uq[:, :, :, :], io.w_uq[0].rearrange("(k p) (h n) -> p k h n", p=P, h=MLA_HEADS)).then_inc(uq_in, 16)
            sp.dma_start(raw_ukv[:, :, :], io.w_ukv[0].rearrange("p (h n) -> p h n", h=MLA_HEADS)).then_inc(ukv_in, 16)

        @block.gpsimd
        def _(pool):
            own = Own(pool, pool_own)
            own(pool.memset(krow[:, :, 0:ROT], 0.0))
            own(pool.memset(trow[:, :, 0:ROT], 1.0))
            kpe = lat[:, :, MLA_Q_RANK + MLA_KV_RANK:LATENT].rearrange("p t (z d) -> p t z d", z=2)
            shape = [P, TILES, 2, MHALF]
            cs, sn = (ktmp[:, j].rearrange("p t (z d) -> p t z d", z=2) for j in range(2))
            for z in range(2):
                own(pool.tensor_tensor(cs[:, :, z, :], kpe[:, :, z, :], keep.cos[:, :, HALF:NFREQ], ALU.mult))
                own(pool.tensor_tensor(sn[:, :, z, :], kpe[:, :, z, :], keep.sin[:, :, HALF:NFREQ], ALU.mult))
            for copy in range(2):
                at = ROT + copy * MLA_ROPE_DIM
                own(pool.tensor_tensor(krow[:, :, at:at + MHALF], cs[:, :, 0, :], sn[:, :, 1, :], ALU.subtract))
                pool.tensor_tensor(krow[:, :, at + MHALF:at + 2 * MHALF], cs[:, :, 1, :], sn[:, :, 0, :], ALU.add).then_inc(krow_ready, 1)
            for m in range(STEPS):
                pool.wait_ge(inverse_ready, m + 1)
                row = prob(m)
                pool.tensor_scalar(row, row, inverse[:, m % 4:m % 4 + 1], 1.0, ALU.mult, ALU.mult).then_inc(prob_ready, 1)

        @block.scalar
        def _(act):
            own = Own(act, act_own)
            act.activation(identR[:, :], keep.ident, ACT.Copy).then_inc(mask_ready, 1)
            act.activation(maskR[:, :], keep.neg, ACT.Copy).then_inc(mask_ready, 1)
            act.wait_ge(uq_in, 16)
            act.wait_ge(ukv_in, 16)
            act.activation(wv[0][:, :].rearrange("p (h n) -> p h n", h=MLA_HEADS), raw_ukv[:, :, MLA_NOPE_DIM:], ACT.Identity,
                           scale=gain_kv).then_inc(w_hi, 1)
            for t in range(TILES):
                act.wait_ge(lat_turned, t + 1)
                act.activation(cT[0][:, :, t * P:(t + 1) * P], ps[:, t % 2, 0:(KQ + 1) * P].rearrange("p (k c) -> p k c", c=P),
                               ACT.Copy).then_inc(lat_hi, 1)
                if t == 0:
                    act.activation(wk[0][:, :, :], raw_ukv[:, :, 0:MLA_NOPE_DIM], ACT.Identity, scale=gain_kv).then_inc(w_hi, 1)
                    for k in range(KQ):
                        for dst, src, width in PIECES:
                            act.activation(wq[0][:, k, :, dst:dst + width], raw_uq[:, k, :, src:src + width], ACT.Identity,
                                           scale=gain_q(k)).then_inc(w_hi, 1)
            act.wait_ge(tab_turned, 1)
            act.activation(table[:, :], ps[:, 4:6, :].rearrange("p a n -> p (a n)"), ACT.Copy).then_inc(tab_copied, 1)
            act.wait_ge(rot_turned, 1)
            for buf in kbuf:
                act.activation(buf[0][ROT:P, :], ps[ROT:P, 2:4, :].rearrange("p a n -> p (a n)"), ACT.Copy).then_inc(rot_hi, 1)
            for t in range(TILES):
                act.wait_ge(v_done, t + 1)
                act.activation(v[0][:, t, :], ps[:, 6 + t % 2, :], ACT.Copy).then_inc(v_hi, 1)

            def project_hi(h, piece):
                u = 4 * h + piece
                cols = slice((piece % 2) * BANK, (piece % 2 + 1) * BANK)
                if piece < 2:
                    act.wait_ge(proj_roped, 2 * h + piece + 1)
                    act.activation(qbuf[h % 2][0][:, cols], ps[:, 7, :], ACT.Copy).then_inc(proj_hi, 1)
                else:
                    act.wait_ge(proj_done, u + 1)
                    act.activation(kbuf[h % 2][0][0:ROT, cols], ps[0:ROT, 7, :], ACT.Copy).then_inc(proj_hi, 1)

            for piece in range(4):
                project_hi(0, piece)

            def turn_hi(t):
                for b, parts in groups_of(t):
                    g = bank_of[(t, b)]
                    act.wait_ge(pt_turned, g + 1)
                    for n, (first, count) in enumerate(parts):
                        src = ps[:, 4 + g % 2, :].rearrange("p (j c) -> p j c", c=P)[:, first - b:first - b + count, :]
                        last = act.activation(pt_view(pT[0], t, first, count), src, ACT.Copy)
                        last.then_inc(pt_hi, 1) if n == len(parts) - 1 else own(last)

            for m in range(STEPS + LAG + 2):
                t = m - LAG
                fresh = t % BLOCK_ROWS == 0
                for h, piece in projections(m - 1):
                    if piece >= 2:
                        project_hi(h, piece)
                if 0 <= t < STEPS and not fresh:
                    turn_hi(t)
                if m < STEPS:
                    i = m % TILES
                    act.wait_ge(top_ready, m + 1)
                    if m >= ROWS:
                        act.wait_ge(pt_turned, through[m - ROWS])
                    act.activation(prob(m),
                                   ps[:, 2 * (m % 2):2 * (m % 2) + 2, :].rearrange("p a n -> p (a n)")[:, 0:(i + 1) * P],
                                   ACT.Exp, bias=neg_top[:, m % 4:m % 4 + 1], scale=SCALE,
                                   accum_out=total[:, m % 4:m % 4 + 1]).then_inc(exp_done, 1)
                if 0 <= t < STEPS and fresh:
                    if t > 0:
                        act.wait_ge(pv_done, t // BLOCK_ROWS)
                    turn_hi(t)
                for chunk in chunk_of(t - 2):
                    h, qc = divmod(chunk, 2)
                    half = slice(MLA_V_DIM * (h % 2), MLA_V_DIM * (h % 2 + 1))
                    act.wait_ge(pv_done, chunk + 1)
                    act.activation(act_parts[0][half, 4 + h // 2, qc * BANK:(qc + 1) * BANK], ps[half, 6, :], ACT.Copy).then_inc(out_hi, 1)
                for h, piece in projections(m - 1):
                    if piece < 2:
                        project_hi(h, piece)

        @block.vector
        def _(dve):
            own = Own(dve, dve_own)
            for t in range(TILES):
                row = lat[:, t, 0:MLA_Q_RANK]
                dve.tensor_scalar(row, row, keep.rstd_lat[:, 0, t:t + 1], None, ALU.mult).then_inc(lat_normed, 1)
                row = lat[:, t, MLA_Q_RANK:MLA_Q_RANK + MLA_KV_RANK]
                dve.tensor_scalar(row, row, keep.rstd_lat[:, 1, t:t + 1], None, ALU.mult).then_inc(lat_normed, 1)
            dve.wait_ge(w_hi, 1)
            dve.scalar_tensor_tensor(wv[1][:, :].rearrange("p (h n) -> p h n", h=MLA_HEADS), raw_ukv[:, :, MLA_NOPE_DIM:], gain_kv,
                                     wv[0][:, :].rearrange("p (h n) -> p h n", h=MLA_HEADS).bitcast(F32), ALU.mult, ALU.subtract).then_inc(w_lo, 1)
            sin, cos = keep.sin[:, :, HALF:NFREQ], keep.cos[:, :, HALF:NFREQ]
            dve.wait_ge(pool_own, 2)
            for at, src, sign in ((0, cos, 1.0), (1, cos, 1.0), (2, sin, -1.0), (3, sin, 1.0)):
                dve.tensor_scalar(trow[:, :, ROT + at * MHALF:ROT + (at + 1) * MHALF], src, sign, None, ALU.mult).then_inc(trow_ready, 1)
            for t in range(TILES):
                dve.wait_ge(lat_hi, t + 1)
                dve.tensor_tensor(cT[1][:, :, t * P:(t + 1) * P], ps[:, t % 2, 0:(KQ + 1) * P].rearrange("p (k c) -> p k c", c=P),
                                  cT[0][:, :, t * P:(t + 1) * P].bitcast(F32), ALU.subtract).then_inc(lat_lo, 1)
            dve.wait_ge(w_hi, 2)
            dve.scalar_tensor_tensor(wk[1][:, :, :], raw_ukv[:, :, 0:MLA_NOPE_DIM], gain_kv, wk[0][:, :, :].bitcast(F32),
                                     ALU.mult, ALU.subtract).then_inc(w_lo, 1)
            dve.wait_ge(w_hi, 2 + KQ * len(PIECES))
            for k in range(KQ):
                for dst, src, width in PIECES:
                    dve.scalar_tensor_tensor(wq[1][:, k, :, dst:dst + width], raw_uq[:, k, :, src:src + width], gain_q(k),
                                             wq[0][:, k, :, dst:dst + width].bitcast(F32), ALU.mult, ALU.subtract).then_inc(w_lo, 1)
            dve.wait_ge(rot_hi, 2)
            for buf in kbuf:
                dve.tensor_tensor(buf[1][ROT:P, :], ps[ROT:P, 2:4, :].rearrange("p a n -> p (a n)"), buf[0][ROT:P, :].bitcast(F32),
                                  ALU.subtract).then_inc(rot_lo, 1)
            for t in range(TILES):
                dve.wait_ge(v_hi, t + 1)
                dve.tensor_tensor(v[1][:, t, :], ps[:, 6 + t % 2, :], v[0][:, t, :].bitcast(F32), ALU.subtract).then_inc(v_lo, 1)

            def rope_piece(h, piece):
                if piece < 2:
                    cols = slice(piece * BANK, (piece + 1) * BANK)
                    dve.wait_ge(proj_done, 4 * h + piece + 1)
                    if h == 0 and piece == 0:
                        dve.wait_ge(tab_copied, 1)
                    dve.tensor_tensor(ps[:, 7, :], ps[:, 7, :], table[:, cols], ALU.mult).then_inc(proj_roped, 1)

            def project_lo(h, piece):
                cols = slice((piece % 2) * BANK, (piece % 2 + 1) * BANK)
                rows, buf = (slice(0, P), qbuf) if piece < 2 else (slice(0, ROT), kbuf)
                dve.wait_ge(proj_hi, 4 * h + piece + 1)
                dve.tensor_tensor(buf[h % 2][1][rows, cols], ps[rows, 7, :], buf[h % 2][0][rows, cols].bitcast(F32),
                                  ALU.subtract).then_inc(proj_lo, 1)

            for piece in range(4):
                rope_piece(0, piece)
                project_lo(0, piece)
            for m in range(STEPS + LAG + 2):
                if m < STEPS:
                    i, s = m % TILES, m % 4
                    scores = ps[:, 2 * (m % 2):2 * (m % 2) + 2, :].rearrange("p a n -> p (a n)")
                    dve.wait_ge(score_done, m + 1)
                    own(dve.tensor_reduce(top[:, s:s + 1], scores[:, 0:(i + 1) * P], AX, ALU.max))
                    dve.tensor_scalar(neg_top[:, s:s + 1], top[:, s:s + 1], -SCALE, None, ALU.mult).then_inc(top_ready, 1)
                if 1 <= m <= STEPS:
                    s = (m - 1) % 4
                    dve.wait_ge(exp_done, m)
                    dve.reciprocal(inverse[:, s:s + 1], total[:, s:s + 1]).then_inc(inverse_ready, 1)
                for h, piece in projections(m - 1):
                    rope_piece(h, piece)
                    if piece >= 2:
                        project_lo(h, piece)
                t = m - LAG
                if 0 <= t < STEPS:
                    for b, parts in groups_of(t):
                        g = bank_of[(t, b)]
                        dve.wait_ge(pt_hi, g + 1)
                        for n, (first, count) in enumerate(parts):
                            src = ps[:, 4 + g % 2, :].rearrange("p (j c) -> p j c", c=P)[:, first - b:first - b + count, :]
                            last = dve.tensor_tensor(pt_view(pT[1], t, first, count), src,
                                                     pt_view(pT[0], t, first, count).bitcast(F32), ALU.subtract)
                            last.then_inc(pt_lo, 1) if n == len(parts) - 1 else own(last)
                for chunk in chunk_of(t - 2):
                    h, qc = divmod(chunk, 2)
                    half = slice(MLA_V_DIM * (h % 2), MLA_V_DIM * (h % 2 + 1))
                    cols = slice(qc * BANK, (qc + 1) * BANK)
                    dve.wait_ge(out_hi, chunk + 1)
                    dve.tensor_tensor(act_parts[1][half, 4 + h // 2, cols], ps[half, 6, :],
                                      act_parts[0][half, 4 + h // 2, cols].bitcast(F32), ALU.subtract).then_inc(out_lo, 1)
                for h, piece in projections(m - 1):
                    if piece < 2:
                        project_lo(h, piece)

        @block.tensor
        def _(pe):
            for t in range(TILES):
                pe.wait_ge(lat_normed, 2 * t + 2)
                if t >= 2:
                    pe.wait_ge(lat_lo, t - 1)
                for k in range(KQ + 1):
                    last = pe.transpose(ps[:, t % 2, k * P:(k + 1) * P], lat[:, t, k * P:(k + 1) * P], keep.ident)
                last.then_inc(lat_turned, 1)
            pe.wait_ge(trow_ready, 4)
            for t in range(TILES):
                last = pe.transpose(ps[:, 4 + t // 4, (t % 4) * P:(t % 4 + 1) * P], trow[:, t, :], keep.ident)
            last.then_inc(tab_turned, 1)
            pe.wait_ge(krow_ready, 2)
            for t in range(TILES):
                last = pe.transpose(ps[:, 2 + t // 4, (t % 4) * P:(t % 4 + 1) * P], krow[:, t, :], keep.ident)
            last.then_inc(rot_turned, 1)
            pe.wait_ge(w_lo, 1)
            for t in range(TILES):
                pe.wait_ge(lat_lo, t + 1)
                if t >= 2:
                    pe.wait_ge(v_lo, t - 1)
                split_product(pe, ps[:, 6 + t % 2, :], cT[0][:, KQ, t * P:(t + 1) * P], cT[1][:, KQ, t * P:(t + 1) * P],
                              wv[0][:, :], wv[1][:, :], True, True).then_inc(v_done, 1)

            def project(h, piece):
                u = 4 * h + piece
                cols = slice((piece % 2) * BANK, (piece % 2 + 1) * BANK)
                if u >= 1:
                    pe.wait_ge(proj_lo, u)
                if piece < 2:
                    for k in range(KQ):
                        last = split_product(pe, ps[:, 7, :], wq[0][:, k, h, :], wq[1][:, k, h, :],
                                             cT[0][:, k, cols], cT[1][:, k, cols], k == 0, k == KQ - 1)
                else:
                    last = split_product(pe, ps[0:ROT, 7, :], wk[0][:, h, :], wk[1][:, h, :],
                                         cT[0][:, KQ, cols], cT[1][:, KQ, cols], True, True)
                last.then_inc(proj_done, 1)

            pe.wait_ge(v_lo, TILES)
            pe.wait_ge(w_lo, 2 + KQ * len(PIECES))
            for piece in range(4):
                project(0, piece)
            pe.wait_ge(rot_lo, 2)
            pe.wait_ge(mask_ready, 2)
            for m in range(STEPS + LAG + 1):
                if m < STEPS:
                    h, i = divmod(m, TILES)
                    if i == 0:
                        pe.wait_ge(proj_lo, 4 * (h + 1))
                    if m >= 2:
                        pe.wait_ge(exp_done, m - 1)
                    q, k = qbuf[h % 2], kbuf[h % 2]
                    width = (i + 1) * P
                    for c in range(0, width, BANK):
                        n = min(BANK, width - c)
                        last = split_product(pe, ps[:, 2 * (m % 2) + c // BANK, 0:n], q[0][:, i * P:(i + 1) * P], q[1][:, i * P:(i + 1) * P],
                                             k[0][:, c:c + n], k[1][:, c:c + n], True, c + n < width)
                    at = i * P % BANK
                    last = pe.matmul(ps[:, 2 * (m % 2) + i * P // BANK, at:at + P], identR[:, :], maskR[:, :], start=False, stop=True)
                    last.then_inc(score_done, 1)
                t = m - LAG
                if 0 <= t < STEPS:
                    pe.wait_ge(prob_ready, t + 1)
                    for b, parts in groups_of(t):
                        g = bank_of[(t, b)]
                        if g >= 2:
                            pe.wait_ge(pt_lo, g - 1)
                        else:
                            pe.wait_ge(tab_copied, 1)
                        for j in range(b, min(b + 4, t % TILES + 1)):
                            last = pe.transpose(ps[:, 4 + g % 2, (j - b) * P:(j - b + 1) * P], prob(t)[:, j * P:(j + 1) * P], keep.ident)
                        last.then_inc(pt_turned, 1)
                t = m - LAG - 1
                for chunk in chunk_of(t):
                    h, qc = divmod(chunk, 2)
                    pe.wait_ge(pt_lo, through[t])
                    if chunk >= 1:
                        pe.wait_ge(out_lo, chunk)
                    pair = slice(h // 2 * P, (h // 2 + 1) * P)
                    keys = BLOCK_ROWS * (qc + 1)
                    for j in range(keys):
                        ahead = max(j - BLOCK_ROWS * qc, 0) * P
                        at = slice(PT_OFF[j], PT_OFF[j] + BANK - ahead)
                        last = split_product(pe, ps[:, 6, ahead:BANK], v[0][:, j, pair], v[1][:, j, pair],
                                             pT[0][:, at], pT[1][:, at], j == 0, j == keys - 1)
                    last.then_inc(pv_done, 1)
                for h, piece in projections(m):
                    project(h, piece)


def mix_output(nc, io, keep):
    KR = RET_WIDTH // P
    with ExitStack() as ctx:
        def sb(name, shape, dt=F32):
            return ctx.enter_context(nc.sbuf_tensor(name, shape, dt))

        def sem(name):
            return ctx.enter_context(nc.semaphore(name))

        wHi = sb("woHi", [P, KD, D_MODEL], F32R)
        wLo = sb("woLo", [P, KD, D_MODEL], F32R)
        raw = sb("wo_raw", [P, 2, D_MODEL])
        g_post = sb("g_post_row", [P, D_MODEL])
        g_pre = sb("g_pre_row", [P, D_MODEL])
        xrow = sb("xrow", [P, 2, D_MODEL])
        x1 = sb("x1row", [P, 2, D_MODEL])
        stat = sb("statC", [P, 4, TILES])
        rows = keep.latent.rearrange("p t n -> p (t n)")[:, 0:3 * D_MODEL].rearrange("p (b n) -> p b n", b=3)
        mixn, h2, junk = rows[:, 0, :], rows[:, 1, :], rows[:, 2, :]
        ps = ctx.enter_context(nc.psum_tensor("psC", [P, 8, BANK], F32))

        gains_in = sem("gains_in")
        raw_in = [sem("wo_in0"), sem("wo_in1")]
        x_in = [sem("xr_in0"), sem("xr_in1")]
        w_hi = sem("wo_hi")
        w_lo = sem("wo_lo")
        y_turned = sem("y_turned")
        y_hi = sem("y_hi")
        y_lo = sem("y_lo")
        mix_done = sem("mix_done")
        mix_sq = sem("mix_sq")
        mix_rstd = sem("mix_rstd")
        mix_read = sem("mix_read")
        x1_done = sem("x1_done")
        x1_sq = sem("x1_sq")
        x1_rstd = sem("x1_rstd")
        x1_stored = [sem("x1_stored0"), sem("x1_stored1")]
        h2_done = sem("h2_done")
        h2_turned = sem("h2_turned")
        h2_hi = sem("h2_hi")
        h2_lo = sem("h2_lo")
        pool_own = sem("pool_ownC")

        xr = io.x[0].rearrange("(t p) d -> t p d", p=P)
        wr = io.w_o[0].rearrange("(k p) n -> k p n", p=P)
        x1r = io.x1.rearrange("(t p) d -> t p d", p=P)

        def banks(t):
            return ps[:, 2 * (t % 2):2 * (t % 2) + 2, :].rearrange("p a n -> p (a n)")

        def tile_of(a, t, k0, k1):
            return a[:, k0:k1, t * P:(t + 1) * P]

        block = ctx.enter_context(nc.Block())

        @block.sync
        def _(sp):
            def load_x(t):
                if t >= 2:
                    sp.wait_ge(x1_done, t - 1)
                sp.dma_start(xrow[:, t % 2, :], xr[t]).then_inc(x_in[t % 2], 16)

            for k in range(KD):
                if k >= 2:
                    sp.wait_ge(w_lo, k - 1)
                sp.dma_start(raw[:, k % 2, :], wr[k]).then_inc(raw_in[k % 2], 16)
            load_x(0)
            load_x(1)
            sp.dma_start(g_post[:, :], io.g_post_mix[0].partition_broadcast(P)).then_inc(gains_in, 16)
            sp.dma_start(g_pre[:, :], io.g_pre_ffn[0].partition_broadcast(P)).then_inc(gains_in, 16)
            for t in range(TILES):
                sp.wait_ge(x1_done, t + 1)
                sp.dma_start(x1r[t], x1[:, t % 2, :]).then_inc(x1_stored[t % 2], 16)
                if t + 2 < TILES:
                    load_x(t + 2)
            for b in range(2):
                sp.wait_ge(x1_stored[b], 16 * TILES // 2)

        @block.gpsimd
        def _(pool):
            own = Own(pool, pool_own)
            for t in range(TILES):
                for done, ready, i in ((mix_sq, mix_rstd, 0), (x1_sq, x1_rstd, 2)):
                    pool.wait_ge(done, t + 1)
                    own(pool.tensor_scalar(stat[:, i + 1, t:t + 1], stat[:, i, t:t + 1], 1.0 / D_MODEL, EPS, ALU.mult, ALU.add))
                    pool.tensor_tensor(stat[:, i + 1, t:t + 1], stat[:, i + 1, t:t + 1], keep.neghalf[:, 0:1], ALU.pow).then_inc(ready, 1)

        @block.scalar
        def _(act):
            def turn_hi(t):
                act.wait_ge(y_turned, t + 1)
                act.activation(tile_of(keep.actHi, t, 0, KR), ps[:, 4 + t % 4, :].rearrange("p (k c) -> p k c", c=P), ACT.Copy).then_inc(y_hi, 1)

            for k in range(KD):
                act.wait_ge(raw_in[k % 2], 16 * (k // 2 + 1))
                if k < KR:
                    act.activation(wHi[:, k, :], raw[:, k % 2, :], ACT.Identity,
                                   scale=keep.cols[:, COL_RET_GN + k:COL_RET_GN + k + 1]).then_inc(w_hi, 1)
                else:
                    act.activation(wHi[:, k, :], raw[:, k % 2, :], ACT.Copy).then_inc(w_hi, 1)
                turn_hi(k)
            for t in range(TILES + 1):
                if t < TILES:
                    act.wait_ge(mix_done, t + 1)
                    if t >= 1:
                        act.wait_ge(x1_sq, t)
                    act.activation(junk, banks(t), ACT.Square, accum_out=stat[:, 0, t:t + 1]).then_inc(mix_sq, 1)
                    act.wait_ge(x1_done, t + 1)
                    act.wait_ge(mix_sq, t + 1)
                    act.activation(junk, x1[:, t % 2, :], ACT.Square, accum_out=stat[:, 2, t:t + 1]).then_inc(x1_sq, 1)
                if t >= 1:
                    act.wait_ge(h2_turned, t)
                    act.activation(tile_of(keep.actHi, t - 1, 0, KD), ps[:, 6:8, :].rearrange("p a (k c) -> p (a k) c", c=P),
                                   ACT.Copy).then_inc(h2_hi, 1)

        @block.vector
        def _(dve):
            for k in range(KD):
                dve.wait_ge(w_hi, k + 1)
                if k < KR:
                    dve.scalar_tensor_tensor(wLo[:, k, :], raw[:, k % 2, :], keep.cols[:, COL_RET_GN + k:COL_RET_GN + k + 1],
                                             wHi[:, k, :].bitcast(F32), ALU.mult, ALU.subtract).then_inc(w_lo, 1)
                else:
                    dve.tensor_tensor(wLo[:, k, :], raw[:, k % 2, :], wHi[:, k, :].bitcast(F32), ALU.subtract).then_inc(w_lo, 1)
                dve.wait_ge(y_hi, k + 1)
                dve.tensor_tensor(tile_of(keep.actLo, k, 0, KR), ps[:, 4 + k % 4, :].rearrange("p (k c) -> p k c", c=P),
                                  tile_of(keep.actHi, k, 0, KR).bitcast(F32), ALU.subtract).then_inc(y_lo, 1)
            dve.wait_ge(gains_in, 32)
            for t in range(TILES + 1):
                if t < TILES:
                    dve.wait_ge(mix_rstd, t + 1)
                    if t >= 1:
                        dve.wait_ge(x1_done, t)
                    dve.scalar_tensor_tensor(mixn, banks(t), stat[:, 1, t:t + 1], g_post[:, :], ALU.mult, ALU.mult).then_inc(mix_read, 1)
                    dve.wait_ge(mix_read, t + 1)
                    dve.wait_ge(x_in[t % 2], 16 * (t // 2 + 1))
                    if t >= 2:
                        dve.wait_ge(x1_stored[t % 2], 16 * (t // 2))
                    dve.tensor_tensor(x1[:, t % 2, :], mixn, xrow[:, t % 2, :], ALU.add).then_inc(x1_done, 1)
                    dve.wait_ge(x1_rstd, t + 1)
                    if t >= 1:
                        dve.wait_ge(h2_turned, t)
                    dve.scalar_tensor_tensor(h2, x1[:, t % 2, :], stat[:, 3, t:t + 1], g_pre[:, :], ALU.mult, ALU.mult).then_inc(h2_done, 1)
                if t >= 1:
                    dve.wait_ge(h2_hi, t)
                    dve.tensor_tensor(tile_of(keep.actLo, t - 1, 0, KD), ps[:, 6:8, :].rearrange("p a (k c) -> p (a k) c", c=P),
                                      tile_of(keep.actHi, t - 1, 0, KD).bitcast(F32), ALU.subtract).then_inc(h2_lo, 1)

        @block.tensor
        def _(pe):
            for t in range(TILES):
                if t >= 4:
                    pe.wait_ge(y_lo, t - 3)
                for k in range(KR):
                    last = pe.transpose(ps[:, 4 + t % 4, k * P:(k + 1) * P], keep.q_y[:, t, k * P:(k + 1) * P], keep.ident)
                last.then_inc(y_turned, 1)
            for t in range(TILES + 1):
                if t < TILES:
                    pe.wait_ge(y_lo, TILES)
                    if t >= 2:
                        pe.wait_ge(mix_read, t - 1)
                    for half in range(2):
                        cols = slice(half * BANK, (half + 1) * BANK)
                        for k in range(KD):
                            if t == 0 and half == 0:
                                pe.wait_ge(w_lo, k + 1)
                            last = split_product(pe, ps[:, 2 * (t % 2) + half, :], keep.actHi[:, k, t * P:(t + 1) * P],
                                                 keep.actLo[:, k, t * P:(t + 1) * P], wHi[:, k, cols], wLo[:, k, cols], k == 0, k == KD - 1)
                    last.then_inc(mix_done, 1)
                if t >= 1:
                    pe.wait_ge(h2_done, t)
                    if t >= 2:
                        pe.wait_ge(h2_lo, t - 1)
                    for k in range(KD):
                        last = pe.transpose(ps[:, 6 + k // 4, (k % 4) * P:(k % 4 + 1) * P], h2[:, k * P:(k + 1) * P], keep.ident)
                    last.then_inc(h2_turned, 1)


def conv_ffn(nc, io, keep):
    PAIR = 2
    ROUNDS = FF_TILES // PAIR
    OUTS = TILES * (D_MODEL // BANK)
    RING = 4
    with ExitStack() as ctx:
        def sb(name, shape, dt=F32):
            return ctx.enter_context(nc.sbuf_tensor(name, shape, dt))

        def sem(name):
            return ctx.enter_context(nc.semaphore(name))

        raw_up = sb("raw_up", [P, KD, 2, P])
        up = [sb("wupHi", [P, PAIR, KD, 2, P], F32R), sb("wupLo", [P, PAIR, KD, 2, P], F32R)]
        raw_dn = sb("raw_dn", [P, PAIR, D_MODEL])
        dn = [sb("wdnHi", [P, PAIR, D_MODEL], F32R), sb("wdnLo", [P, PAIR, D_MODEL], F32R)]
        f = [sb("fHi", [P, PAIR, SEQ], F32R), sb("fLo", [P, PAIR, SEQ], F32R)]
        conv_g = sb("conv_g", [P, SEQ])
        conv_u = sb("conv_u", [P, SEQ])
        gelu = sb("gelu", [P, SEQ])
        ps = ctx.enter_context(nc.psum_tensor("psD", [P, 8, BANK], F32))
        gate_ps = ps[:, 0:2, :].rearrange("p a n -> p (a n)")
        up_ps = ps[:, 2:4, :].rearrange("p a n -> p (a n)")

        up_in = sem("up_in")
        dn_in = sem("dn_in")
        up_hi = sem("up_hi")
        up_lo = sem("up_lo")
        dn_hi = sem("dn_hi")
        dn_lo = sem("dn_lo")
        gate_done = sem("gateD_done")
        up_done = sem("upD_done")
        gate_tap = sem("gate_tap")
        up_tap = sem("up_tap")
        gate_read = sem("gate_read")
        up_read = sem("up_read")
        gelu_done = sem("gelu_done")
        product = sem("product")
        f_hi = sem("f_hi")
        f_lo = sem("f_lo")
        down_done = sem("down_done")
        down_free = sem("down_free")
        ffn_zero = sem("ffn_zero")
        tap_own = sem("tap_own")

        w_up = io.w_up[0].rearrange("(k p) (z j c) -> p k z j c", p=P, z=2, c=P)
        w_dn = io.w_down[0].rearrange("(j p) n -> p j n", p=P)

        def rounds(eng, body):
            body(0, True, False)
            with eng.Fori(1, ROUNDS - 1) as r:
                body(r, False, False)
            body(ROUNDS - 1, False, True)

        def col(at, n):
            return keep.cols[:, bass.ds(n + at, 1)]

        block = ctx.enter_context(nc.Block())

        @block.sync
        def _(sp):
            def load_up(n, first):
                if not first:
                    sp.wait_ge(up_lo, n)
                for z in range(2):
                    sp.dma_start(raw_up[:, :, z, :], w_up[:, :, z, bass.ds(n, 1), :].squeeze(2)).then_inc(up_in, 16)

            def body(r, first, last):
                load_up(r * PAIR, first)
                if not first:
                    sp.wait_ge(dn_lo, r)
                sp.dma_start(raw_dn[:, :, :], w_dn[:, bass.ds(r * PAIR, PAIR), :]).then_inc(dn_in, 16)
                load_up(r * PAIR + 1, False)

            rounds(sp, body)

        @block.gpsimd
        def _(pool):
            pool.memset(keep.ffn[:, :, :], 0.0).then_inc(ffn_zero, 1)

        @block.scalar
        def _(act):
            def split_up(n, p, early):
                act.wait_ge(up_in, n * 32 + 32)
                if not early:
                    act.wait_ge(up_done, n - 1)
                act.activation(up[0][:, p], raw_up[:, :, :, :], ACT.Copy).then_inc(up_hi, 1)

            def step(n, p, r, first_step, first_round):
                act.wait_ge(gate_done, n + 1)
                if not first_step:
                    act.wait_ge(gelu_done, n)
                act.activation(conv_g[:, :], gate_ps, ACT.Identity, bias=col(COL_BIAS, n), scale=col(COL_W2, n)).then_inc(gate_tap, 1)
                act.wait_ge(gate_read, n + 1)
                if not first_step:
                    act.wait_ge(product, n)
                act.activation(gelu[:, :], conv_g[:, :], ACT.Gelu_apprx_tanh).then_inc(gelu_done, 1)
                act.wait_ge(up_done, n + 1)
                if not first_step:
                    act.wait_ge(f_lo, n)
                act.activation(conv_u[:, :], up_ps, ACT.Identity, bias=col(COL_BIAS + FF_TILES, n),
                               scale=col(COL_W2 + FF_TILES, n)).then_inc(up_tap, 1)
                act.wait_ge(product, n + 1)
                if not first_round:
                    act.wait_ge(down_done, r * OUTS)
                act.activation(f[0][:, p, :], conv_u[:, :], ACT.Copy).then_inc(f_hi, 1)

            def body(r, first, last):
                n = r * PAIR
                if first:
                    split_up(n, 0, True)
                split_up(n + 1, 1, first)
                step(n, 0, r, first, first)
                act.wait_ge(dn_in, r * 16 + 16)
                act.activation(dn[0][:, :, :], raw_dn[:, :, :], ACT.Copy).then_inc(dn_hi, 1)
                if not last:
                    split_up(n + 2, 0, False)
                step(n + 1, 1, r, False, first)

            rounds(act, body)

        @block.vector
        def _(dve):
            def split_up(p, n):
                dve.wait_ge(up_hi, n + 1)
                dve.tensor_tensor(up[1][:, p], raw_up[:, :, :, :], up[0][:, p].bitcast(F32), ALU.subtract).then_inc(up_lo, 1)

            def convolve(n, src, out, tap, tapped, read, at):
                dve.wait_ge(tap, n + 1)
                dve.scalar_tensor_tensor(out[:, 1:SEQ], src[:, 0:SEQ - 1], col(COL_W1 + at, n), out[:, 1:SEQ], ALU.mult, ALU.add).then_inc(tap_own, 1)
                dve.wait_ge(tap_own, tapped)
                dve.scalar_tensor_tensor(out[:, 2:SEQ], src[:, 0:SEQ - 2], col(COL_W0 + at, n), out[:, 2:SEQ], ALU.mult, ALU.add).then_inc(read, 1)

            def step(n):
                convolve(n, gate_ps, conv_g, gate_tap, n * 2 + 1, gate_read, 0)
                convolve(n, up_ps, conv_u, up_tap, n * 2 + 2, up_read, FF_TILES)
                dve.wait_ge(up_read, n + 1)
                dve.wait_ge(gelu_done, n + 1)
                dve.tensor_tensor(conv_u[:, :], gelu[:, :], conv_u[:, :], ALU.mult).then_inc(product, 1)

            def finish(n, p):
                dve.wait_ge(f_hi, n + 1)
                dve.tensor_tensor(f[1][:, p, :], conv_u[:, :], f[0][:, p, :].bitcast(F32), ALU.subtract).then_inc(f_lo, 1)

            def add_round(r):
                for o in range(OUTS):
                    t, half = divmod(o, 2)
                    row = keep.ffn[:, t, half * BANK:(half + 1) * BANK]
                    dve.wait_ge(down_done, r * OUTS + o + 1)
                    dve.tensor_tensor(row, ps[:, 4 + o % RING, :], row, ALU.add).then_inc(down_free, 1)

            def body(r, first, last):
                n = r * PAIR
                if first:
                    split_up(0, n)
                split_up(1, n + 1)
                step(n)
                if not first:
                    add_round(r - 1)
                finish(n, 0)
                dve.wait_ge(dn_hi, r + 1)
                dve.tensor_tensor(dn[1][:, :, :], raw_dn[:, :, :], dn[0][:, :, :].bitcast(F32), ALU.subtract).then_inc(dn_lo, 1)
                if not last:
                    split_up(0, n + 2)
                step(n + 1)
                finish(n + 1, 1)

            dve.sem_inc(down_free, RING)
            dve.wait_ge(ffn_zero, 1)
            rounds(dve, body)
            add_round(ROUNDS - 1)

        @block.tensor
        def _(pe):
            def step(n, p, first):
                pe.wait_ge(up_lo, n + 1)
                for z, read, done in ((0, gate_read, gate_done), (1, up_read, up_done)):
                    if not first:
                        pe.wait_ge(read, n)
                    for c in range(SEQ // BANK):
                        cols = slice(c * BANK, (c + 1) * BANK)
                        for k in range(KD):
                            last = split_product(pe, ps[:, 2 * z + c, :], up[0][:, p, k, z, :], up[1][:, p, k, z, :],
                                                 keep.actHi[:, k, cols], keep.actLo[:, k, cols], k == 0, k == KD - 1)
                    last.then_inc(done, 1)

            def down(r):
                pe.wait_ge(f_lo, r * PAIR + PAIR)
                pe.wait_ge(dn_lo, r + 1)
                for o in range(OUTS):
                    t, half = divmod(o, 2)
                    pe.wait_ge(down_free, r * OUTS + o + 1)
                    for p in range(PAIR):
                        last = split_product(pe, ps[:, 4 + o % RING, :], f[0][:, p, t * P:(t + 1) * P], f[1][:, p, t * P:(t + 1) * P],
                                             dn[0][:, p, half * BANK:(half + 1) * BANK], dn[1][:, p, half * BANK:(half + 1) * BANK],
                                             p == 0, p == PAIR - 1)
                    last.then_inc(down_done, 1)

            def body(r, first, last):
                n = r * PAIR
                step(n, 0, first)
                if not first:
                    down(r - 1)
                step(n + 1, 1, False)

            rounds(pe, body)
            down(ROUNDS - 1)


def layer_embedding(nc, io, keep):
    KE = PLE_DIM // P
    with ExitStack() as ctx:
        def sb(name, shape, dt=F32):
            return ctx.enter_context(nc.sbuf_tensor(name, shape, dt))

        def sem(name):
            return ctx.enter_context(nc.semaphore(name))

        wg = (keep.actHi, keep.actLo)
        wp = [sb("wpHi", [P, KE, D_MODEL], F32R), sb("wpLo", [P, KE, D_MODEL], F32R)]
        raw = sb("ple_raw", [P, 2, D_MODEL])
        xT = [sb("x2Hi", [P, 2, KD, P], F32R), sb("x2Lo", [P, 2, KD, P], F32R)]
        pT = [sb("pHi", [P, 2, KE, P], F32R), sb("pLo", [P, 2, KE, P], F32R)]
        prow = sb("prow", [P, 2, PLE_DIM])
        x1 = sb("x1back", [P, 2, D_MODEL])
        g_ffn = sb("g_ffn_row", [P, D_MODEL])
        g_ple = sb("g_ple_row", [P, D_MODEL])
        bias = sb("bias_row", [P, D_MODEL])
        gate = sb("ple_gate", [P, D_MODEL])
        e = sb("ple_e", [P, D_MODEL])
        junk = sb("junkE", [P, D_MODEL])
        orow = sb("out_row", [P, 2, D_MODEL])
        stat = sb("statE", [P, 4, TILES])
        ps = ctx.enter_context(nc.psum_tensor("psE", [P, 8, BANK], F32))
        gate_ps = ps[:, 0:2, :].rearrange("p a n -> p (a n)")
        e_ps = ps[:, 2:4, :].rearrange("p a n -> p (a n)")

        rows_in = sem("rows_in")
        raw_in = [sem("ple_in0"), sem("ple_in1")]
        x1_in = [sem("x1_in0"), sem("x1_in1")]
        p_in = [sem("p_in0"), sem("p_in1")]
        w_hi = sem("ple_hi")
        w_lo = sem("ple_lo")
        f_sq = sem("f_sq")
        f_rstd = sem("f_rstd")
        x2_part = sem("x2_part")
        x2_done = sem("x2_done")
        x2_turned = sem("x2_turned")
        x2_hi = sem("x2_hi")
        x2_lo = sem("x2_lo")
        gate_done = sem("gateE_done")
        gate_biased = sem("gate_biased")
        gate_sig = sem("gate_sig")
        ple_done = sem("ple_done")
        e_done = sem("e_done")
        e_sq = sem("e_sq")
        e_rstd = sem("e_rstd")
        e_normed = sem("e_normed")
        out_ready = sem("out_ready")
        out_stored = [sem("out_stored0"), sem("out_stored1")]
        pool_own = sem("pool_ownE")

        x1r = io.x1.rearrange("(t p) d -> t p d", p=P)
        outr = io.out[0].rearrange("(t p) d -> t p d", p=P)
        pr = io.p[0, 0].rearrange("(t p) d -> t p d", p=P)
        weights = [io.w_ple_gate[0].rearrange("(k p) n -> k p n", p=P)[k] for k in range(KD)]
        weights += [io.w_ple[0].rearrange("(k p) n -> k p n", p=P)[k] for k in range(KE)]

        def part(i, s):
            return wg[i][:, s, :] if s < KD else wp[i][:, s - KD, :]

        def turned_bank(t):
            return ps[:, 4:6, :].rearrange("p a (k c) -> p (a k) c", c=P)

        block = ctx.enter_context(nc.Block())

        @block.sync
        def _(sp):
            def load_rows(t):
                if t >= 2:
                    sp.wait_ge(x2_done, t - 1)
                    sp.wait_ge(x2_turned, t - 1)
                sp.dma_start(x1[:, t % 2, :], x1r[t]).then_inc(x1_in[t % 2], 16)
                sp.dma_start(prow[:, t % 2, :], pr[t]).then_inc(p_in[t % 2], 16)

            load_rows(0)
            load_rows(1)
            for i, (dst, src) in enumerate(((g_ffn, io.g_post_ffn), (bias, io.b_ple_gate), (g_ple, io.g_post_ple))):
                sp.dma_start(dst[:, :], src[0].partition_broadcast(P)).then_inc(rows_in, 16)
            for s in range(KD + KE):
                if s >= 2:
                    sp.wait_ge(w_lo, s - 1)
                sp.dma_start(raw[:, s % 2, :], weights[s]).then_inc(raw_in[s % 2], 16)
            for t in range(TILES):
                if t + 2 < TILES:
                    load_rows(t + 2)
                sp.wait_ge(out_ready, t + 1)
                sp.dma_start(outr[t], orow[:, t % 2, :]).then_inc(out_stored[t % 2], 16)
            for b in range(2):
                sp.wait_ge(out_stored[b], 16 * TILES // 2)

        @block.gpsimd
        def _(pool):
            own = Own(pool, pool_own)

            def rstd(done, ready, i, t):
                pool.wait_ge(done, t + 1)
                own(pool.tensor_scalar(stat[:, i + 1, t:t + 1], stat[:, i, t:t + 1], 1.0 / D_MODEL, EPS, ALU.mult, ALU.add))
                pool.tensor_tensor(stat[:, i + 1, t:t + 1], stat[:, i + 1, t:t + 1], keep.neghalf[:, 0:1], ALU.pow).then_inc(ready, 1)

            rstd(f_sq, f_rstd, 0, 0)
            rstd(f_sq, f_rstd, 0, 1)
            for t in range(TILES):
                if t + 2 < TILES:
                    rstd(f_sq, f_rstd, 0, t + 2)
                rstd(e_sq, e_rstd, 2, t)

        @block.scalar
        def _(act):
            squares = [0]

            def square(src, accum, done, t):
                if squares[0]:
                    act.wait_ge(*squares[1])
                act.activation(junk[:, :], src, ACT.Square, accum_out=accum).then_inc(done, 1)
                squares[0:] = [1, (done, t + 1)]

            def x2_rows(t):
                square(keep.ffn[:, t, :], stat[:, 0, t:t + 1], f_sq, t)

            def turn_hi(t):
                act.wait_ge(x2_turned, t + 1)
                if t >= 2:
                    act.wait_ge(ple_done, t - 1)
                act.activation(xT[0][:, t % 2], turned_bank(t), ACT.Copy).then_inc(x2_hi, 1)
                act.activation(pT[0][:, t % 2], ps[:, 6, 0:KE * P].rearrange("p (k c) -> p k c", c=P), ACT.Copy).then_inc(x2_hi, 1)

            x2_rows(0)
            for s in range(KD + KE):
                act.wait_ge(raw_in[s % 2], 16 * (s // 2 + 1))
                act.activation(part(0, s), raw[:, s % 2, :], ACT.Copy).then_inc(w_hi, 1)
                if s == 3:
                    turn_hi(0)
                    x2_rows(1)
            for t in range(TILES):
                if t + 1 < TILES:
                    turn_hi(t + 1)
                if t + 2 < TILES:
                    x2_rows(t + 2)
                act.wait_ge(gate_biased, t + 1)
                act.activation(gate[:, :], gate[:, :], ACT.Sigmoid).then_inc(gate_sig, 1)
                act.wait_ge(e_done, t + 1)
                square(e[:, :], stat[:, 2, t:t + 1], e_sq, t)

        @block.vector
        def _(dve):
            def split_w(s):
                dve.wait_ge(w_hi, s + 1)
                dve.tensor_tensor(part(1, s), raw[:, s % 2, :], part(0, s).bitcast(F32), ALU.subtract).then_inc(w_lo, 1)

            def x2_rows(t):
                row = keep.ffn[:, t, :]
                dve.wait_ge(f_rstd, t + 1)
                dve.scalar_tensor_tensor(row, row, stat[:, 1, t:t + 1], g_ffn[:, :], ALU.mult, ALU.mult).then_inc(x2_part, 1)
                dve.wait_ge(x2_part, t + 1)
                dve.wait_ge(x1_in[t % 2], 16 * (t // 2 + 1))
                dve.tensor_tensor(row, row, x1[:, t % 2, :], ALU.add).then_inc(x2_done, 1)

            def turn_lo(t):
                dve.wait_ge(x2_hi, 2 * t + 2)
                dve.tensor_tensor(xT[1][:, t % 2], turned_bank(t), xT[0][:, t % 2].bitcast(F32), ALU.subtract).then_inc(x2_lo, 1)
                dve.tensor_tensor(pT[1][:, t % 2], ps[:, 6, 0:KE * P].rearrange("p (k c) -> p k c", c=P), pT[0][:, t % 2].bitcast(F32),
                                  ALU.subtract).then_inc(x2_lo, 1)

            dve.wait_ge(rows_in, 48)
            x2_rows(0)
            for s in range(KD + KE):
                split_w(s)
                if s == 3:
                    turn_lo(0)
                    x2_rows(1)
            for t in range(TILES):
                if t + 1 < TILES:
                    turn_lo(t + 1)
                if t + 2 < TILES:
                    x2_rows(t + 2)
                dve.wait_ge(gate_done, t + 1)
                if t >= 1:
                    dve.wait_ge(e_done, t)
                dve.tensor_tensor(gate[:, :], gate_ps, bias[:, :], ALU.add).then_inc(gate_biased, 1)
                dve.wait_ge(gate_sig, t + 1)
                dve.wait_ge(ple_done, t + 1)
                if t >= 1:
                    dve.wait_ge(out_ready, t)
                dve.tensor_tensor(e[:, :], e_ps, gate[:, :], ALU.mult).then_inc(e_done, 1)
                dve.wait_ge(e_rstd, t + 1)
                dve.scalar_tensor_tensor(e[:, :], e[:, :], stat[:, 3, t:t + 1], g_ple[:, :], ALU.mult, ALU.mult).then_inc(e_normed, 1)
                dve.wait_ge(e_normed, t + 1)
                if t >= 2:
                    dve.wait_ge(out_stored[t % 2], 16 * (t // 2))
                dve.tensor_tensor(orow[:, t % 2, :], e[:, :], keep.ffn[:, t, :], ALU.add).then_inc(out_ready, 1)

        @block.tensor
        def _(pe):
            def turn(t):
                pe.wait_ge(x2_done, t + 1)
                pe.wait_ge(p_in[t % 2], 16 * (t // 2 + 1))
                if t >= 1:
                    pe.wait_ge(x2_lo, 2 * t)
                for k in range(KD):
                    pe.transpose(ps[:, 4 + k // 4, (k % 4) * P:(k % 4 + 1) * P], keep.ffn[:, t, k * P:(k + 1) * P], keep.ident)
                for k in range(KE):
                    last = pe.transpose(ps[:, 6, k * P:(k + 1) * P], prow[:, t % 2, k * P:(k + 1) * P], keep.ident)
                last.then_inc(x2_turned, 1)

            turn(0)
            for t in range(TILES):
                pe.wait_ge(x2_lo, 2 * t + 2)
                if t >= 1:
                    pe.wait_ge(gate_biased, t)
                for half in range(2):
                    cols = slice(half * BANK, (half + 1) * BANK)
                    for k in range(KD):
                        if t == 0 and half == 0:
                            pe.wait_ge(w_lo, k + 1)
                        last = split_product(pe, ps[:, half, :], xT[0][:, t % 2, k, :], xT[1][:, t % 2, k, :],
                                             wg[0][:, k, cols], wg[1][:, k, cols], k == 0, k == KD - 1)
                last.then_inc(gate_done, 1)
                if t + 1 < TILES:
                    turn(t + 1)
                if t == 0:
                    pe.wait_ge(w_lo, KD + KE)
                else:
                    pe.wait_ge(e_done, t)
                for half in range(2):
                    cols = slice(half * BANK, (half + 1) * BANK)
                    for k in range(KE):
                        last = split_product(pe, ps[:, 2 + half, :], pT[0][:, t % 2, k, :], pT[1][:, t % 2, k, :],
                                             wp[0][:, k, cols], wp[1][:, k, cols], k == 0, k == KE - 1)
                last.then_inc(ple_done, 1)


INPUTS = ["x", "p", "positions", "w_in", "w_uq", "w_ukv", "w_o", "g_pre_mix", "g_post_mix", "g_q_a", "g_kv_a",
          "g_ret_gn", "w_up", "conv_w", "conv_b", "w_down", "g_pre_ffn", "g_post_ffn", "w_ple", "w_ple_gate",
          "b_ple_gate", "g_post_ple"]


def decoder_layer(nc, io):
    with ExitStack() as ctx:
        def sb(name, shape, dt=F32):
            return ctx.enter_context(nc.sbuf_tensor(name, shape, dt))

        keep = Keep()
        keep.ident = sb("ident", [P, P])[:, :]
        keep.neg = sb("neg", [P, P])[:, :]
        keep.cols = sb("cols", [P, COLS])[:, :]
        keep.neghalf = sb("neghalf", [P, 8])[:, :]
        keep.rstd_lat = sb("rstd_lat", [P, 2, TILES])[:, :, :]
        keep.actHi = sb("actHi", [P, KD, SEQ], F32R)[:, :, :]
        keep.actLo = sb("actLo", [P, KD, SEQ], F32R)[:, :, :]
        with ExitStack() as mixer:
            def mb(name, shape, dt=F32):
                return mixer.enter_context(nc.sbuf_tensor(name, shape, dt))

            keep.sin = mb("rope_sin", [P, TILES, NFREQ])[:, :, :]
            keep.cos = mb("rope_cos", [P, TILES, NFREQ])[:, :, :]
            keep.q_y = mb("q_then_y", [P, TILES, RET_WIDTH])[:, :, :]
            keep.latent = mb("latent", [P, TILES, LATENT])[:, :, :]
            retention_and_projection(nc, io, keep)
            latent_attention(nc, io, keep)
            mix_output(nc, io, keep)
        keep.ffn = sb("ffn_rows", [P, TILES, D_MODEL])[:, :, :]
        conv_ffn(nc, io, keep)
        layer_embedding(nc, io, keep)


def kernel(**inputs):
    import concourse.bacc as bacc
    from concourse.bass_utils import run_bass_kernel_spmd

    nc = bacc.Bacc("TRN2", target_bir_lowering=False, num_devices=1)
    arrays = {name: np.ascontiguousarray(inputs[name]) for name in INPUTS}
    arrays["consts"] = shape_constants()
    drams = {name: nc.dram_tensor(f"in_{name}", a.shape, mybir.dt.from_np(a.dtype), kind="ExternalInput").ap()
             for name, a in arrays.items()}
    out = nc.dram_tensor("out", inputs["x"].shape, F32, kind="ExternalOutput").ap()
    x1 = nc.dram_tensor("x1_scratch", (SEQ, D_MODEL), F32, kind="Internal").ap()
    io = Inputs(out=out, x1=x1, **drams)
    decoder_layer(nc, io)
    r = run_bass_kernel_spmd(nc, [{f"in_{name}": a for name, a in arrays.items()}], core_ids=[0])
    return r.results[0]["out"]
```

```python
from contextlib import ExitStack

import numpy as np

import concourse.bass as bass
from concourse import mybir

P = 128
BANK = 512

D_MODEL = 1024
SEQ = 1024
PLE_DIM = 256
RET_HEADS = 8
RET_HEAD_DIM = 64
RET_WIDTH = RET_HEADS * RET_HEAD_DIM
MLA_HEADS = 8
MLA_NOPE_DIM = 64
MLA_ROPE_DIM = 32
MLA_QK_DIM = MLA_NOPE_DIM + MLA_ROPE_DIM
MLA_V_DIM = 64
MLA_Q_RANK = 256
MLA_KV_RANK = 128
LATENT = MLA_Q_RANK + MLA_KV_RANK + MLA_ROPE_DIM
D_FF = 2816
CONV_WIDTH = 3
ROPE_BASE = 10000.0
EPS = 1e-6

TILES = SEQ // P
KD = D_MODEL // P
PAIRS = RET_HEADS // 2
FF_TILES = D_FF // P
HAND1, HAND2 = 3 * SEQ, 4 * SEQ
WO_RING = 4
GATE_RING = 3
GATE_BANKS, UP_BANKS = slice(0, 2), slice(4, 6)
KQ = MLA_Q_RANK // P
HALF = RET_HEAD_DIM // 2
MHALF = MLA_ROPE_DIM // 2
NFREQ = HALF + MHALF
NEG = -3.0e38

F32 = mybir.dt.float32
F32R = mybir.dt.float32r
I32 = mybir.dt.int32
ALU = mybir.AluOpType
ACT = mybir.ActivationFunctionType
AX = mybir.AxisListType.X

COL_W0, COL_W1 = 0, 2 * FF_TILES
COL_PRE_MIX = 4 * FF_TILES
COL_PRE_FFN = COL_PRE_MIX + KD
COL_Q_A = COL_PRE_FFN + KD
COL_KV_A = COL_Q_A + KQ
COL_RET_GN = COL_KV_A + 1
ROWS_1 = COL_RET_GN + RET_WIDTH // P
COL_W2 = P
COL_BIAS = COL_W2 + 2 * FF_TILES
ROWS_2 = 4 * FF_TILES
COL_POS = 2 * P
COLS = COL_POS + TILES

C_IDENT = 0
C_NEG = C_IDENT + P
C_BEFORE = C_NEG + P
C_KSCALE = C_BEFORE + P
C_INNER = C_KSCALE + RET_HEADS
C_DECAY = C_INNER + RET_HEADS
C_FREQ = C_DECAY + PAIRS * P
CONSTS = C_FREQ + NFREQ


def shape_constants():
    c = np.zeros((P, CONSTS), np.float32)
    i = np.arange(P, dtype=np.float64)
    c[:, C_IDENT:C_IDENT + P] = np.eye(P)
    c[:, C_NEG:C_NEG + P] = np.where(i[None, :] > i[:, None], NEG, 0.0)
    c[:, C_BEFORE:C_BEFORE + P] = i[None, :] >= i[:, None]
    log_gamma = np.log1p(-np.exp2(-5.0 - np.arange(RET_HEADS)))
    c[:, C_KSCALE:C_KSCALE + RET_HEADS] = np.exp(-log_gamma[None, :] * (i[:, None] + 1)) * RET_HEAD_DIM ** -0.5
    c[:, C_INNER:C_INNER + RET_HEADS] = np.exp(log_gamma[None, :] * (i[:, None] + 1))
    same = (np.arange(P)[:, None] // RET_HEAD_DIM) == (np.arange(P)[None, :] // RET_HEAD_DIM)
    for pair in range(PAIRS):
        head = 2 * pair + np.arange(P) // RET_HEAD_DIM
        c[:, C_DECAY + pair * P:C_DECAY + (pair + 1) * P] = same * np.exp(log_gamma[head] * P)[:, None]
    ret = (ROPE_BASE ** (-np.arange(0, RET_HEAD_DIM, 2) / RET_HEAD_DIM)).astype(np.float32)
    mla = (ROPE_BASE ** (-np.arange(0, MLA_ROPE_DIM, 2) / MLA_ROPE_DIM)).astype(np.float32)
    c[:, C_FREQ:C_FREQ + NFREQ] = np.concatenate([ret, mla])[None, :]
    return c


def two_pi_pieces():
    rest, out = 2 * np.pi, []
    for _ in range(3):
        scale = 2.0 ** (np.floor(np.log2(rest)) - 7)
        piece = np.floor(rest / scale) * scale
        out.append(float(piece))
        rest -= piece
    return out + [float(np.float32(rest))]


class Inputs:

    def __init__(self, x, p, positions, w_in, w_uq, w_ukv, w_o, g_pre_mix, g_post_mix, g_q_a, g_kv_a, g_ret_gn, w_up,
                 conv_w, conv_b, w_down, g_pre_ffn, g_post_ffn, w_ple, w_ple_gate, b_ple_gate, g_post_ple, consts, out, x1):
        self.x, self.p, self.positions, self.consts, self.out, self.x1 = x, p, positions, consts, out, x1
        self.w_in, self.w_uq, self.w_ukv, self.w_o = w_in, w_uq, w_ukv, w_o
        self.w_up, self.conv_w, self.conv_b, self.w_down = w_up, conv_w, conv_b, w_down
        self.w_ple, self.w_ple_gate, self.b_ple_gate = w_ple, w_ple_gate, b_ple_gate
        self.g_pre_mix, self.g_post_mix, self.g_q_a, self.g_kv_a = g_pre_mix, g_post_mix, g_q_a, g_kv_a
        self.g_ret_gn, self.g_pre_ffn, self.g_post_ffn, self.g_post_ple = g_ret_gn, g_pre_ffn, g_post_ffn, g_post_ple


class Keep:
    pass


class Own:

    def __init__(self, eng, sem):
        self.eng, self.sem, self.n = eng, sem, 0

    def __call__(self, ins):
        self.n += 1
        ins.then_inc(self.sem, 1)
        self.eng.wait_ge(self.sem, self.n)


def split_product(eng, out, hi, lo, whi, wlo, first, last):
    eng.matmul(out, hi, whi, start=first, stop=False)
    eng.matmul(out, hi, wlo, start=False, stop=False)
    return eng.matmul(out, lo, whi, start=False, stop=last)


def retention_and_projection(nc, io, keep):
    groups = [("q", 0, 512), ("k", 512, 512), ("v", 1024, 512), ("latent", 4 * RET_WIDTH, LATENT), ("gate", 3 * RET_WIDTH, 512)]
    SLOTS = len(groups) * TILES
    SLICES = len(groups) * KD
    RAW = 4
    RING = 9
    RET0 = 3 * TILES

    with ExitStack() as ctx:
        def sb(name, shape, dt=F32):
            return ctx.enter_context(nc.sbuf_tensor(name, shape, dt))

        def sem(name):
            return ctx.enter_context(nc.semaphore(name))

        kret = sb("kret", [P, TILES, RET_WIDTH])
        vret = sb("vret", [P, TILES, RET_WIDTH])
        wraw = keep.raw_w_in[:, 0:RAW * 512].rearrange("p (s n) -> p s n", s=RAW)
        wHi = sb("wHi", [P, RING, 512], F32R)
        wLo = sb("wLo", [P, RING, 512], F32R)
        scratch = keep.chunk_room.rearrange("p (s n) -> p s n", s=8)
        mrope = sb("mrope", [P, 2, 2, 512])
        rows1, rows2, posr = (keep.raw_w_in[:, RAW * 512 + i * P:RAW * 512 + (i + 1) * P] for i in range(3))
        posi = sb("posi", [TILES, P], I32)
        small = sb("small", [P, 8, 8])
        junk = sb("junkA", [P, MLA_Q_RANK + MLA_KV_RANK])
        ctab = sb("ctab", [P, CONSTS - C_BEFORE])
        ps = keep.ps

        xt = scratch[:, 0:4, :].rearrange("p (b h) n -> p b (h n)", b=2)
        ht = scratch[:, 4:8, :].rearrange("p (b h) n -> p b (h n)", b=2)
        q_zero = scratch[:, 0:2, :].rearrange("p a n -> p (a n)").rearrange("p (r z c) -> p r z c", r=PAIRS, z=2)
        kT = scratch[:, 2, :].rearrange("p (r c) -> p r c", r=PAIRS)
        qT = scratch[:, 3:5, :].rearrange("p b (r c) -> p b r c", r=PAIRS)
        sT = scratch[:, 5:7, :].rearrange("p a n -> p (a n)").rearrange("p (h c) -> p h c", h=RET_HEADS)
        state = scratch[:, 7, :]
        orow = mrope[:, 0, 0, :]
        osq = mrope[:, 0, 1, :]
        gate = mrope[:, 1, :, :]
        NA = TILES * NFREQ
        angle = mrope[:, 0, 0, 0:NA]
        turns = mrope[:, 0, 1, 0:NA]
        cosin = mrope[:, 1, 0, 0:NA]

        def const(col, n):
            return ctab[:, col - C_BEFORE:col - C_BEFORE + n]

        ident = keep.ident
        ssx = small[:, 0, :]
        rstdx = small[:, 1, :]
        neghalf = keep.neghalf
        meanv = small[:, 3, :]
        varv = small[:, 4, :]
        rstdo = small[:, 5, :]
        scr8 = small[:, 6, :]

        small_in = sem("small_in")
        x_in = [sem("x_in0"), sem("x_in1")]
        raw_in = [sem(f"raw_in{i}") for i in range(RAW)]
        w_hi = sem("w_hi")
        w_lo = sem("w_lo")
        slice_used = sem("slice_used")
        sq_done = sem("sq_done")
        rstd_done = sem("rstd_done")
        h_done = sem("h_done")
        turned = sem("turned")
        hT_hi = sem("hT_hi")
        hT_lo = sem("hT_lo")
        z_ready = sem("z_ready")
        z_dve = sem("z_used_dve")
        z_act = sem("z_used_act")
        rope_out = sem("rope_out")
        setup_turned = sem("setup_turned")
        columns_ready = sem("columns_ready")
        trig_arg = sem("trig_arg")
        trig_done = sem("trig_done")
        dve_own = sem("dve_ownA")
        act_own = sem("act_ownA")
        pool_own = sem("pool_ownA")
        zeros_done = sem("zeros_done")
        qk_turned = sem("qk_turned")
        kT_copied = sem("kT_copied")
        qT_copied = sem("qT_copied")
        qz_copied = sem("qz_copied")
        scores_done = sem("scores_done")
        masked = sem("masked")
        out_done = sem("out_done")
        kv_done = sem("kv_done")
        state_done = sem("state_done")
        out_read = sem("out_read")
        mean_sub = sem("mean_sub")
        osq_done = sem("osq_done")
        var_done = sem("var_done")
        ornorm = sem("rstd_head")
        gate_done = sem("gate_done")
        y_done = sem("y_done")

        w3 = io.w_in[0].rearrange("(k p) n -> p k n", p=P)
        xr = io.x[0].rearrange("(t p) d -> t p d", p=P)

        POOL_BEFORE_Y = 1 + 3 * TILES + 4
        block = ctx.enter_context(nc.Block())

        @block.sync
        def _(sp):
            sp.dma_start(ident, io.consts[:, C_IDENT:C_IDENT + P]).then_inc(small_in, 16)
            cw = io.conv_w[0].rearrange("w (j p) -> w j p", p=P)
            F2 = 2 * FF_TILES
            pieces = [(rows1, COL_W0, cw[0]), (rows1, COL_W1, cw[1]),
                      (rows1, COL_PRE_MIX, io.g_pre_mix.rearrange("a (j p) -> (a j) p", p=P)),
                      (rows1, COL_PRE_FFN, io.g_pre_ffn.rearrange("a (j p) -> (a j) p", p=P)),
                      (rows1, COL_Q_A, io.g_q_a.rearrange("a (j p) -> (a j) p", p=P)),
                      (rows1, COL_KV_A, io.g_kv_a.rearrange("a (j p) -> (a j) p", p=P)),
                      (rows1, COL_RET_GN, io.g_ret_gn.rearrange("a (j p) -> (a j) p", p=P)),
                      (rows2, 0, cw[2]), (rows2, F2, io.conv_b.rearrange("a (j p) -> (a j) p", p=P))]
            for tile, row, src in pieces:
                sp.dma_start(tile[row:row + src.shape[0], :], src).then_inc(small_in, 16)
            sp.dma_start(posi[:, :], io.positions.rearrange("b (t p) -> (b t) p", p=P)).then_inc(small_in, 16)
            sp.dma_start(ctab[:, :], io.consts[:, C_BEFORE:CONSTS]).then_inc(small_in, 16)
            sp.dma_start(keep.neg, io.consts[:, C_NEG:C_NEG + P]).then_inc(small_in, 16)

            def load_x(t):
                if t >= 2:
                    sp.wait_ge(h_done, t - 1)
                sp.dma_start(xt[:, t % 2, :], xr[t]).then_inc(x_in[t % 2], 16)

            def load_w(s):
                name, col, width = groups[s // KD]
                if s >= RAW:
                    sp.wait_ge(w_lo, s - RAW + 1)
                sp.dma_start(wraw[:, s % RAW, 0:width], w3[:, s % KD, col:col + width]).then_inc(raw_in[s % RAW], 16)

            load_x(0)
            load_x(1)
            for s in range(KD):
                load_w(s)
            for t in range(2, TILES):
                load_x(t)
            for s in range(KD, SLICES):
                load_w(s)
            sp.wait_ge(w_lo, SLICES)
            sp.dma_start(keep.raw_uq, io.w_uq[0].rearrange("(k p) n -> p k n", p=P)).then_inc(keep.latent_weights_in, 16)
            sp.dma_start(keep.raw_ukv, io.w_ukv[0]).then_inc(keep.latent_weights_in, 16)

        def slices_before(n, after):
            gi, t = divmod(n, TILES)
            if gi + 1 >= len(groups):
                return []
            spare = RING - KD
            if t == 1 and not after:
                return [(gi + 1) * KD + k for k in range(spare)]
            if t == TILES - 1 and not after:
                return [(gi + 1) * KD + k for k in range(spare, KD)]
            return []

        @block.gpsimd
        def _(pool):
            own = Own(pool, pool_own)
            own(pool.memset(neghalf, -0.5))

            def rope_rows(n):
                t = n % TILES
                rows = keep.q_y if n < TILES else kret
                dst = rows[:, t, :].rearrange("p (h z d) -> p h z d", h=RET_HEADS, z=2)
                cs = mrope[:, n % 2, 0, :].rearrange("p (h z d) -> p h z d", h=RET_HEADS, z=2)
                sn = mrope[:, n % 2, 1, :].rearrange("p (h z d) -> p h z d", h=RET_HEADS, z=2)
                pool.wait_ge(z_dve, n + 1)
                pool.tensor_tensor(dst[:, :, 0, :], cs[:, :, 0, :], sn[:, :, 1, :], ALU.subtract).then_inc(rope_out, 1)
                pool.tensor_tensor(dst[:, :, 1, :], cs[:, :, 1, :], sn[:, :, 0, :], ALU.add).then_inc(rope_out, 1)

            for t in range(TILES):
                pool.wait_ge(sq_done, t + 1)
                own(pool.tensor_scalar(scr8[:, t:t + 1], ssx[:, t:t + 1], 1.0 / D_MODEL, EPS, ALU.mult, ALU.add))
                pool.tensor_tensor(rstdx[:, t:t + 1], scr8[:, t:t + 1], neghalf[:, 0:1], ALU.pow).then_inc(rstd_done, 1)
                if t >= 3:
                    rope_rows(t - 3)
            for n in range(TILES - 3, 2 * TILES):
                rope_rows(n)
            pool.wait_ge(rope_out, 4 * TILES)
            for t in range(TILES):
                dst = kret[:, t, :].rearrange("p (h d) -> p h d", h=RET_HEADS)
                own(pool.tensor_tensor(dst, dst, const(C_KSCALE, RET_HEADS).unsqueeze(2).broadcast_to([P, RET_HEADS, RET_HEAD_DIM]), ALU.mult))
                if t == 0:
                    pool.wait_ge(turned, TILES)
                    pool.memset(q_zero[64:128, :, 0, :], 0.0).then_inc(zeros_done, 1)
                    pool.wait_ge(zeros_done, 1)
                    pool.memset(q_zero[0:64, :, 1, :], 0.0).then_inc(zeros_done, 1)
                    pool.wait_ge(zeros_done, 2)
            for c in range(TILES):
                pool.wait_ge(var_done, c + 1)
                own(pool.tensor_scalar(varv, varv, 1.0 / RET_HEAD_DIM, EPS, ALU.mult, ALU.add))
                pool.tensor_tensor(rstdo, varv, neghalf, ALU.pow).then_inc(ornorm, 1)
            pool.wait_ge(z_act, 2 * TILES)
            for part, width in enumerate((MLA_Q_RANK, MLA_KV_RANK)):
                lat = keep.rstd_lat[:, part, :]
                own(pool.tensor_scalar(lat, lat, 1.0 / width, EPS, ALU.mult, ALU.add))
                own(pool.tensor_tensor(lat, lat, neghalf, ALU.pow))
            for c in range(TILES):
                y = keep.q_y[:, c, :]
                pool.wait_ge(gate_done, c + 1)
                pool.wait_ge(y_done, c + 1)
                own(pool.tensor_tensor(y, y, gate[:, c % 2, :], ALU.mult))

        @block.scalar
        def _(act):
            own = Own(act, act_own)

            def split_hi(s):
                gi, k = divmod(s, KD)
                width = groups[gi][2]
                act.wait_ge(raw_in[s % RAW], 16 * (s // RAW + 1))
                if s == 0:
                    act.wait_ge(columns_ready, 2)
                if s >= RING:
                    before, kb = divmod(s - RING, KD)
                    if kb == KD - 1:
                        act.wait_ge(z_ready, (before + 1) * TILES)
                    else:
                        act.wait_ge(slice_used, before * (KD - 1) + kb + 1)
                act.activation(wHi[:, s % RING, 0:width], wraw[:, s % RAW, 0:width], ACT.Identity,
                               scale=keep.cols[:, COL_PRE_MIX + k:COL_PRE_MIX + k + 1]).then_inc(w_hi, 1)

            def hT_hi_part(t):
                act.wait_ge(turned, t + 1)
                bank = 2 + 2 * (t % 2)
                act.activation(keep.actHi[:, :, t * P:(t + 1) * P],
                               ps[:, bank:bank + 2, :].rearrange("p a (b c) -> p (a b) c", c=P), ACT.Copy).then_inc(hT_hi, 1)

            for t in range(TILES):
                act.wait_ge(x_in[t % 2], 16 * (t // 2 + 1))
                if t >= 2:
                    act.wait_ge(turned, t - 1)
                act.activation(ht[:, t % 2, :], xt[:, t % 2, :], ACT.Square, accum_out=ssx[:, t:t + 1]).then_inc(sq_done, 1)
                if t < 2:
                    for s in range(4 * t, 4 * t + 4):
                        split_hi(s)
                if t >= 1:
                    hT_hi_part(t - 1)
                if t == 1:
                    act.wait_ge(trig_arg, 2)
                    act.activation(keep.sin, angle.rearrange("p (t f) -> p t f", t=TILES), ACT.Sin).then_inc(trig_done, 1)
                    act.activation(keep.cos, cosin.rearrange("p (t f) -> p t f", t=TILES), ACT.Sin, scale=-1.0).then_inc(trig_done, 1)
            hT_hi_part(TILES - 1)
            for s in slices_before(1, False) + slices_before(TILES - 1, False):
                split_hi(s)
            for n in range(TILES, SLOTS + 2):
                if n < SLOTS:
                    gi, t = divmod(n, TILES)
                    for s in slices_before(n, False):
                        split_hi(s)
                    name, col, width = groups[gi]
                    if gi >= 2:
                        act.wait_ge(z_ready, n + 1)
                        z = ps[:, n % 2, 0:width]
                        if name == "v":
                            act.activation(vret[:, t, :], z, ACT.Copy).then_inc(z_act, 1)
                        elif name == "latent":
                            own(act.activation(keep.latent[:, t, :], z, ACT.Copy))
                            own(act.activation(junk[:, 0:MLA_Q_RANK], z[:, 0:MLA_Q_RANK], ACT.Square,
                                               accum_out=keep.rstd_lat[:, 0, t:t + 1]))
                            act.activation(junk[:, MLA_Q_RANK:MLA_Q_RANK + MLA_KV_RANK], z[:, MLA_Q_RANK:MLA_Q_RANK + MLA_KV_RANK],
                                           ACT.Square, accum_out=keep.rstd_lat[:, 1, t:t + 1]).then_inc(z_act, 1)
                            act.wait_ge(z_act, n + 1 - 2 * TILES)
                        else:
                            if t >= 2:
                                act.wait_ge(pool_own, POOL_BEFORE_Y + t - 1)
                            else:
                                act.wait_ge(rope_out, 4 * TILES)
                            act.activation(gate[:, t % 2, :], z, ACT.Silu).then_inc(gate_done, 1)
                c = n - RET0
                if 0 <= c < TILES:
                    act.wait_ge(qk_turned, c + 1)
                    if c >= 1:
                        act.wait_ge(scores_done, c)
                    act.activation(kT, ps[:, 3, :].rearrange("p (r c) -> p r c", r=PAIRS), ACT.Copy).then_inc(kT_copied, 1)
                    if c >= 2:
                        act.wait_ge(out_done, c - 1)
                    act.activation(qT[:, c % 2], ps[:, 2, :].rearrange("p (r c) -> p r c", r=PAIRS), ACT.Copy).then_inc(qT_copied, 1)
                c = n - RET0 - 2
                if 0 <= c < TILES:
                    act.wait_ge(mean_sub, c + 1)
                    act.activation(osq, orow, ACT.Square).then_inc(osq_done, 1)

        @block.vector
        def _(dve):
            own = Own(dve, dve_own)
            dve.wait_ge(small_in, 16 * 13)
            own(dve.tensor_copy(posr[0:TILES, :], posi[:, :]))
            dve.sem_inc(columns_ready, 1)
            dve.wait_ge(setup_turned, 1)
            own(dve.tensor_copy(keep.cols[:, 0:ROWS_1], ps[:, 6, 0:ROWS_1]))
            own(dve.tensor_copy(keep.cols[:, COL_W2:COL_W2 + ROWS_2], ps[:, 6, COL_W2:COL_W2 + ROWS_2]))
            own(dve.tensor_copy(keep.cols[:, COL_POS:COLS], ps[:, 6, COL_POS:COLS]))
            dve.sem_inc(columns_ready, 1)
            def split_lo(s):
                gi, k = divmod(s, KD)
                width = groups[gi][2]
                dve.wait_ge(w_hi, s + 1)
                dve.scalar_tensor_tensor(wLo[:, s % RING, 0:width], wraw[:, s % RAW, 0:width],
                                         keep.cols[:, COL_PRE_MIX + k:COL_PRE_MIX + k + 1],
                                         wHi[:, s % RING, 0:width].bitcast(F32), ALU.mult, ALU.subtract).then_inc(w_lo, 1)

            def norm_x(t):
                dve.wait_ge(rstd_done, t + 1)
                dve.tensor_scalar(ht[:, t % 2, :], xt[:, t % 2, :], rstdx[:, t:t + 1], None, ALU.mult).then_inc(h_done, 1)

            def hT_lo_part(t):
                dve.wait_ge(hT_hi, t + 1)
                bank = 2 + 2 * (t % 2)
                dve.tensor_tensor(keep.actLo[:, :, t * P:(t + 1) * P],
                                  ps[:, bank:bank + 2, :].rearrange("p a (b c) -> p (a b) c", c=P),
                                  keep.actHi[:, :, t * P:(t + 1) * P].bitcast(F32), ALU.subtract).then_inc(hT_lo, 1)

            def rope(n):
                t = n % TILES
                z = ps[:, n % 2, :].rearrange("p (g d) -> p g d", d=HALF)
                dve.wait_ge(z_ready, n + 1)
                if n == 0:
                    dve.wait_ge(trig_done, 2)
                if n >= 2:
                    dve.wait_ge(rope_out, 2 * (n - 1))
                cs = mrope[:, n % 2, 0, :].rearrange("p (g d) -> p g d", d=HALF)
                sn = mrope[:, n % 2, 1, :].rearrange("p (g d) -> p g d", d=HALF)
                own(dve.tensor_tensor(cs, z, keep.cos[:, t, 0:HALF].unsqueeze(1).broadcast_to([P, 2 * RET_HEADS, HALF]), ALU.mult))
                dve.tensor_tensor(sn, z, keep.sin[:, t, 0:HALF].unsqueeze(1).broadcast_to([P, 2 * RET_HEADS, HALF]),
                                  ALU.mult).then_inc(z_dve, 1)

            def zero_padded_q(c):
                dve.wait_ge(qk_turned, c + 1)
                if c == 0:
                    dve.wait_ge(zeros_done, 2)
                if c >= 1:
                    dve.wait_ge(scores_done, c)
                src = ps[:, 2, :].rearrange("p (r c) -> p r c", r=PAIRS)
                dve.wait_ge(qT_copied, c + 1)
                dve.tensor_copy(q_zero[0:64, :, 0, :], src[0:64]).then_inc(qz_copied, 1)
                dve.tensor_copy(q_zero[64:128, :, 1, :], src[64:128]).then_inc(qz_copied, 1)

            def mask_scores(c):
                dve.wait_ge(scores_done, c + 1)
                src = ps[:, 4:6, :].rearrange("p a (h c) -> p (a h) c", c=P)
                dve.tensor_tensor(sT, src, const(C_BEFORE, P).unsqueeze(1).broadcast_to([P, RET_HEADS, P]),
                                  ALU.mult).then_inc(masked, 1)

            def heads(ap):
                return ap.rearrange("p (h d) -> p h d", h=RET_HEADS)

            def each_head(ap):
                return ap.unsqueeze(2).broadcast_to([P, RET_HEADS, RET_HEAD_DIM])

            def finish_chunk(c):
                dve.wait_ge(out_done, c + 1)
                dve.wait_ge(rope_out, 4 * TILES)
                if c >= 1:
                    dve.wait_ge(osq_done, c)
                dve.tensor_tensor(heads(orow), heads(ps[:, 7, :]), each_head(const(C_INNER, RET_HEADS)), ALU.mult).then_inc(out_read, 1)
                if c < TILES - 1:
                    dve.wait_ge(kv_done, c + 1)
                    if c > 0:
                        own(dve.tensor_tensor(state, ps[:, 6, :], state, ALU.add))
                        dve.tensor_tensor(state, state, const(C_DECAY, PAIRS * P), ALU.mult).then_inc(state_done, 1)
                    else:
                        dve.tensor_tensor(state, ps[:, 6, :], const(C_DECAY, PAIRS * P), ALU.mult).then_inc(state_done, 1)
                dve.wait_ge(out_read, c + 1)
                own(dve.tensor_reduce(meanv, heads(orow), AX, ALU.add))
                own(dve.tensor_scalar(meanv, meanv, 1.0 / RET_HEAD_DIM, None, ALU.mult))
                dve.tensor_tensor(heads(orow), heads(orow), each_head(meanv), ALU.subtract).then_inc(mean_sub, 1)
                dve.wait_ge(osq_done, c + 1)
                if c >= 1:
                    dve.wait_ge(ornorm, c)
                dve.tensor_reduce(varv, heads(osq), AX, ALU.add).then_inc(var_done, 1)
                dve.wait_ge(ornorm, c + 1)
                dve.tensor_tensor(heads(keep.q_y[:, c, :]), heads(orow), each_head(rstdo), ALU.mult).then_inc(y_done, 1)
                dve.wait_ge(y_done, c + 1)

            def angles():
                a3 = angle.rearrange("p (t f) -> p t f", t=TILES)
                own(dve.tensor_tensor(a3, keep.cols[:, COL_POS:COLS].unsqueeze(2).broadcast_to([P, TILES, NFREQ]),
                                      const(C_FREQ, NFREQ).unsqueeze(1).broadcast_to([P, TILES, NFREQ]), ALU.mult))
                magic = 1.5 * 2.0 ** 23
                for unit in (4096.0, 1.0):
                    own(dve.tensor_scalar(turns, angle, 1.0 / (2 * np.pi * unit), magic, ALU.mult, ALU.add))
                    own(dve.tensor_scalar(turns, turns, -magic, unit, ALU.add, ALU.mult))
                    for piece in two_pi_pieces():
                        own(dve.scalar_tensor_tensor(angle, turns, -piece, angle, ALU.mult, ALU.add))
                pi_below = 3.1415925
                own(dve.tensor_scalar(angle, angle, pi_below, -pi_below, ALU.min, ALU.max))
                dve.sem_inc(trig_arg, 1)
                own(dve.scalar_tensor_tensor(turns, angle, -1.0, angle, ALU.mult, ALU.max))
                dve.tensor_scalar(cosin, turns, -float(np.pi / 2), None, ALU.add).then_inc(trig_arg, 1)

            norm_x(0)
            for s in range(4):
                split_lo(s)
            for t in range(1, TILES):
                norm_x(t)
                if t == 1:
                    for s in range(4, KD):
                        split_lo(s)
                hT_lo_part(t - 1)
                if t == 1:
                    angles()
                if t >= 2:
                    rope(t - 2)
            hT_lo_part(TILES - 1)
            rope(TILES - 2)
            for s in slices_before(1, False) + slices_before(TILES - 1, False):
                split_lo(s)
            rope(TILES - 1)
            for n in range(TILES, SLOTS + 2):
                if n < SLOTS:
                    for s in slices_before(n, False):
                        split_lo(s)
                    if n < 2 * TILES:
                        rope(n)
                if 0 <= n - RET0 - 2 < TILES:
                    finish_chunk(n - RET0 - 2)
                if 0 <= n - RET0 - 1 < TILES:
                    mask_scores(n - RET0 - 1)
                if 0 <= n - RET0 < TILES:
                    zero_padded_q(n - RET0)

        @block.tensor
        def _(pe):
            pe.wait_ge(small_in, 16 * 13)
            pe.transpose(ps[:, 6, 0:ROWS_1], rows1[0:ROWS_1, :], ident[0:ROWS_1, 0:ROWS_1])
            pe.transpose(ps[:, 6, COL_W2:COL_W2 + ROWS_2], rows2[0:ROWS_2, :], ident[0:ROWS_2, 0:ROWS_2])
            pe.wait_ge(columns_ready, 1)
            pe.transpose(ps[:, 6, COL_POS:COLS], posr[0:TILES, :], ident[0:TILES, 0:TILES]).then_inc(setup_turned, 1)

            def turn_x(t):
                pe.wait_ge(h_done, t + 1)
                if t >= 2:
                    pe.wait_ge(hT_lo, t - 1)
                bank = 2 + 2 * (t % 2)
                for k in range(KD):
                    last = pe.transpose(ps[:, bank + k // 4, (k % 4) * P:(k % 4 + 1) * P], ht[:, t % 2, k * P:(k + 1) * P], ident)
                last.then_inc(turned, 1)

            def product(n):
                gi, t = divmod(n, TILES)
                width = groups[gi][2]
                if gi == 0:
                    pe.wait_ge(hT_lo, t + 1)
                if n >= 2:
                    if n - 2 < 2 * TILES:
                        pe.wait_ge(z_dve, n - 1)
                    elif n - 2 < 4 * TILES:
                        pe.wait_ge(z_act, n - 1 - 2 * TILES)
                    else:
                        pe.wait_ge(gate_done, n - 1 - 4 * TILES)
                for k in range(KD):
                    s = gi * KD + k
                    if t == 0:
                        pe.wait_ge(w_lo, s + 1)
                    last = split_product(pe, ps[:, n % 2, 0:width],
                                         keep.actHi[:, k, t * P:(t + 1) * P], keep.actLo[:, k, t * P:(t + 1) * P],
                                         wHi[:, s % RING, 0:width], wLo[:, s % RING, 0:width], k == 0, k == KD - 1)
                    if t == TILES - 1 and k < KD - 1:
                        last.then_inc(slice_used, 1)
                last.then_inc(z_ready, 1)

            def turn_chunk(c):
                if c == 0:
                    pe.wait_ge(pool_own, 1 + TILES + 1)
                    pe.wait_ge(hT_lo, TILES)
                else:
                    pe.wait_ge(pool_own, 1 + TILES + 1 + c)
                    pe.wait_ge(kT_copied, c)
                    pe.wait_ge(qz_copied, 2 * c)
                for pair in range(PAIRS):
                    pe.transpose(ps[:, 2, pair * P:(pair + 1) * P], keep.q_y[:, c, pair * P:(pair + 1) * P], ident)
                for pair in range(PAIRS):
                    last = pe.transpose(ps[:, 3, pair * P:(pair + 1) * P], kret[:, c, pair * P:(pair + 1) * P], ident)
                last.then_inc(qk_turned, 1)

            def score_chunk(c):
                pe.wait_ge(kT_copied, c + 1)
                pe.wait_ge(qz_copied, 2 * c + 2)
                if c >= 1:
                    pe.wait_ge(masked, c)
                for pair in range(PAIRS):
                    last = pe.matmul(ps[:, 4 + pair // 2, (pair % 2) * 256:(pair % 2 + 1) * 256], kT[:, pair, :],
                                     q_zero[:, pair, :, :], start=True, stop=True)
                last.then_inc(scores_done, 1)

            def finish_chunk(c):
                pe.wait_ge(masked, c + 1)
                if c >= 1:
                    pe.wait_ge(state_done, c)
                    pe.wait_ge(out_read, c)
                else:
                    pe.wait_ge(z_act, TILES)
                for pair in range(PAIRS):
                    cols = slice(pair * P, (pair + 1) * P)
                    if c >= 1:
                        pe.matmul(ps[:, 7, cols], qT[:, c % 2, pair, :], state[:, cols], start=True, stop=False, skip_group_check=True)
                    for z in range(2):
                        h = 2 * pair + z
                        hc = slice(h * RET_HEAD_DIM, (h + 1) * RET_HEAD_DIM)
                        last = pe.matmul(ps[:, 7, hc], sT[:, h, :], vret[:, c, hc], start=(c == 0), stop=True,
                                         skip_group_check=True)
                last.then_inc(out_done, 1)
                if c < TILES - 1:
                    for pair in range(PAIRS):
                        cols = slice(pair * P, (pair + 1) * P)
                        last = pe.matmul(ps[:, 6, cols], kret[:, c, cols], vret[:, c, cols], start=True, stop=True)
                    last.then_inc(kv_done, 1)

            turn_x(0)
            turn_x(1)
            for n in range(SLOTS + 2):
                if n < SLOTS:
                    product(n)
                if 2 <= n + 2 < TILES:
                    turn_x(n + 2)
                if 0 <= n - RET0 - 2 < TILES:
                    finish_chunk(n - RET0 - 2)
                if 0 <= n - RET0 - 1 < TILES:
                    score_chunk(n - RET0 - 1)
                if 0 <= n - RET0 < TILES:
                    turn_chunk(n - RET0)


def latent_attention(nc, io, keep):
    SCALE = MLA_QK_DIM ** -0.5
    BLOCK_ROWS = 4
    STEPS = MLA_HEADS * TILES
    LAG = 3
    ROT = MLA_NOPE_DIM
    PT_OFF = [j * BANK for j in range(5)] + [5 * BANK, 5 * BANK + 384, 5 * BANK + 768]
    PT_COLS = PT_OFF[-1] + P

    def groups_of(m):
        i = m % TILES
        if i < BLOCK_ROWS:
            return [(0, [(0, i + 1)])]
        tail = [(4, 1)] + ([(5, i - 4)] if i > 4 else [])
        return [(0, [(0, 4)]), (4, tail)]

    def pt_view(buf, m, first, count):
        i = m % TILES
        if i < BLOCK_ROWS:
            start, step = i * P, BANK - P
        elif first == 0:
            start, step = (i - BLOCK_ROWS) * P, BANK
        elif first == 4:
            start, step = PT_OFF[4] + (i - 4) * P, P
        else:
            start, step = PT_OFF[5] + (i - 5) * P, PT_OFF[6] - PT_OFF[5] - P
        if count == 1:
            return buf[:, start:start + P].unsqueeze(1)
        return bass_view(buf, start, step, count)

    def bass_view(buf, start, step, count):
        width = count * step
        if start + width <= buf.shape[1]:
            return buf[:, start:start + width].rearrange("p (j s) -> p j s", s=step)[:, :, 0:P]
        lead = start + width - buf.shape[1]
        return buf[:, start - lead:start - lead + width].rearrange("p (j s) -> p j s", s=step)[:, :, lead:lead + P]

    ROW_AT = [21, 15, 8, 0, 21, 15, 8, 0]
    ROWS = 4

    bank_of = {}
    for m in range(STEPS):
        for b, _ in groups_of(m):
            bank_of[(m, b)] = len(bank_of)
    through = [max(v for (mm, _), v in bank_of.items() if mm == m) + 1 for m in range(STEPS)]

    with ExitStack() as ctx:
        def sb(name, shape, dt=F32):
            return ctx.enter_context(nc.sbuf_tensor(name, shape, dt))

        def sem(name):
            return ctx.enter_context(nc.semaphore(name))

        wq = [keep.wq[:, i * 2 * SEQ:(i + 1) * 2 * SEQ].rearrange("p (k h c) -> p k h c", k=KQ, h=MLA_HEADS) for i in range(2)]
        wk = [sb("wkHi", [P, MLA_HEADS, MLA_NOPE_DIM], F32R), sb("wkLo", [P, MLA_HEADS, MLA_NOPE_DIM], F32R)]
        v = [sb("vHi", [P, TILES, MLA_HEADS * MLA_V_DIM], F32R), sb("vLo", [P, TILES, MLA_HEADS * MLA_V_DIM], F32R)]
        table = sb("rope_table", [P, SEQ])
        q1 = [keep.q1k1[:, 0:SEQ], keep.q1k1[:, SEQ:2 * SEQ]]
        k0 = [sb("k0Hi", [P, SEQ], F32R), sb("k0Lo", [P, SEQ], F32R)]
        k1 = [keep.q1k1[:, 2 * SEQ:3 * SEQ], sb("k1Lo", [P, SEQ], F32R)]
        identR = sb("identR", [P, P], F32R)
        maskR = sb("maskR", [P, P], F32R)
        st = sb("softmax_small", [P, 4, 4])
        act_parts = (keep.actHi, keep.actLo)
        wv = [a[:, KD - 1, 0:MLA_HEADS * MLA_V_DIM] for a in act_parts]
        raw_uq = keep.raw_uq.rearrange("p k (h n) -> p k h n", h=MLA_HEADS)
        raw_ukv = keep.raw_ukv.rearrange("p (h n) -> p h n", h=MLA_HEADS)
        cT = [a[:, 0:KQ + 1, :] for a in act_parts]
        qbuf = [[a[:, KQ + 1, :] for a in act_parts], [a[:, :] for a in q1]]
        kbuf = [[a[:, :] for a in k0], [a[:, :] for a in k1]]
        prob_rows = keep.latent.rearrange("p t n -> p (t n)")

        def prob(m):
            i = m % TILES
            return prob_rows[:, ROW_AT[i] * P:(ROW_AT[i] + i + 1) * P]

        lat = keep.latent
        top, neg_top, total, inverse = (st[:, i, :] for i in range(4))

        with ExitStack() as early:
            def eb(name, shape, dt=F32):
                return early.enter_context(nc.sbuf_tensor(name, shape, dt))
            krow = eb("krow", [P, TILES, P])
            trow = eb("trow", [P, TILES, P])
            ktmp = eb("ktmp", [P, 2, TILES, MLA_ROPE_DIM])
        pT = [sb("pTHi", [P, PT_COLS], F32R)[:, :], sb("pTLo", [P, PT_COLS], F32R)[:, :]]
        ps = keep.ps

        q_normed = sem("q_normed")
        kv_normed = sem("kv_normed")
        krow_ready = sem("krow_ready")
        trow_ready = sem("trow_ready")
        lat_turned = sem("lat_turned")
        lat_hi = sem("lat_hi")
        lat_lo = sem("lat_lo")
        rot_turned = sem("rot_turned")
        tab_turned = sem("tab_turned")
        rot_hi = sem("rot_hi")
        rot_lo = sem("rot_lo")
        tab_copied = sem("tab_copied")
        mask_ready = sem("mask_ready")
        w_hi = sem("w_hiB")
        w_lo = sem("w_loB")
        v_done = sem("v_done")
        v_hi = sem("v_hi")
        v_lo = sem("v_lo")
        proj_done = sem("proj_done")
        proj_roped = sem("proj_roped")
        proj_hi = sem("proj_hi")
        proj_lo = sem("proj_lo")
        score_done = sem("score_done")
        top_ready = sem("top_ready")
        exp_done = sem("exp_done")
        inverse_ready = sem("inverse_ready")
        prob_ready = sem("prob_ready")
        pt_turned = sem("pt_turned")
        pt_hi = sem("pt_hi")
        pt_lo = sem("pt_lo")
        pv_done = sem("pv_done")
        out_hi = sem("out_hi")
        out_lo = sem("out_lo")
        y_turned = sem("y_turned")
        y_hi = sem("y_hi")
        y_lo = sem("y_lo")
        dve_own = sem("dve_ownB")
        act_own = sem("act_ownB")
        pool_own = sem("pool_ownB")

        PIECES = [(0, 0, MLA_QK_DIM), (MLA_QK_DIM, MLA_QK_DIM - MHALF, MHALF), (MLA_QK_DIM + MHALF, MLA_NOPE_DIM, MHALF)]
        PIECE_AT = [0, 2, 4, 6]
        gain_kv = keep.cols[:, COL_KV_A:COL_KV_A + 1]

        def by_head(ap):
            return ap.rearrange("p (h n) -> p h n", h=MLA_HEADS)

        def gain_q(k):
            return keep.cols[:, COL_Q_A + k:COL_Q_A + k + 1]

        def projections(m):
            h, i = divmod(m, TILES)
            return [(h + 1, PIECE_AT.index(i))] if 0 <= h < MLA_HEADS - 1 and i in PIECE_AT else []

        WEIGHT_PIECES = [[(wq[0][:, k, :, dst:dst + width], wq[1][:, k, :, dst:dst + width], raw_uq[:, k, :, src:src + width], gain_q(k))]
                         for k in range(KQ) for dst, src, width in PIECES]
        for (hi, lo), first in (((wk[0][:, :, :], wk[1][:, :, :]), 0),
                                ((by_head(wv[0]), by_head(wv[1])), MLA_NOPE_DIM)):
            WEIGHT_PIECES.append([(hi, lo, raw_ukv[:, :, first:first + MLA_NOPE_DIM], gain_kv)])
        KR = RET_WIDTH // P
        Y0 = STEPS - TILES
        LAT_BANK = [0, 1, 6, 7]

        def chunk_of(t):
            return [t // BLOCK_ROWS] if 0 <= t < STEPS and t % BLOCK_ROWS == BLOCK_ROWS - 1 else []

        block = ctx.enter_context(nc.Block())

        @block.sync
        def _(sp):
            sp.wait_ge(proj_done, 4 * (MLA_HEADS - 1) + 2)
            for k in range(WO_RING):
                sp.dma_start(keep.raw_wo[:, k, :], io.w_o[0][k * P:(k + 1) * P, :]).then_inc(keep.wo_in[k], 16)

        @block.gpsimd
        def _(pool):
            own = Own(pool, pool_own)
            own(pool.memset(trow[:, :, 0:ROT], 1.0))
            own(pool.memset(krow[:, :, 0:ROT], 0.0))
            kpe = lat[:, :, MLA_Q_RANK + MLA_KV_RANK:LATENT].rearrange("p t (z d) -> p t z d", z=2)
            shape = [P, TILES, 2, MHALF]
            cs, sn = (ktmp[:, j].rearrange("p t (z d) -> p t z d", z=2) for j in range(2))
            for z in range(2):
                own(pool.tensor_tensor(cs[:, :, z, :], kpe[:, :, z, :], keep.cos[:, :, HALF:NFREQ], ALU.mult))
                own(pool.tensor_tensor(sn[:, :, z, :], kpe[:, :, z, :], keep.sin[:, :, HALF:NFREQ], ALU.mult))
            for copy in range(2):
                at = ROT + copy * MLA_ROPE_DIM
                own(pool.tensor_tensor(krow[:, :, at:at + MHALF], cs[:, :, 0, :], sn[:, :, 1, :], ALU.subtract))
                pool.tensor_tensor(krow[:, :, at + MHALF:at + 2 * MHALF], cs[:, :, 1, :], sn[:, :, 0, :], ALU.add).then_inc(krow_ready, 1)
            for m in range(STEPS):
                pool.wait_ge(inverse_ready, m + 1)
                row = prob(m)
                pool.tensor_scalar(row, row, inverse[:, m % 4:m % 4 + 1], 1.0, ALU.mult, ALU.mult).then_inc(prob_ready, 1)

        @block.scalar
        def _(act):
            own = Own(act, act_own)
            for t in range(TILES):
                row = lat[:, t, MLA_Q_RANK:MLA_Q_RANK + MLA_KV_RANK]
                act.activation(row, row, ACT.Copy, scale=keep.rstd_lat[:, 1, t:t + 1]).then_inc(kv_normed, 1)
            act.wait_ge(keep.latent_weights_in, 32)
            for t in range(TILES):
                act.wait_ge(lat_turned, t + 1)
                act.activation(cT[0][:, :, t * P:(t + 1) * P], ps[:, LAT_BANK[t % 4], 0:(KQ + 1) * P].rearrange("p (k c) -> p k c", c=P),
                               ACT.Copy).then_inc(lat_hi, 1)
                for dst, _, src, gain in WEIGHT_PIECES[t]:
                    act.activation(dst, src, ACT.Identity, scale=gain).then_inc(w_hi, 1)
            act.wait_ge(tab_turned, 1)
            act.activation(table[:, :], ps[:, 4:6, :].rearrange("p a n -> p (a n)"), ACT.Copy).then_inc(tab_copied, 1)

            def value_hi(t):
                act.wait_ge(v_done, t + 1)
                act.activation(v[0][:, t, :], ps[:, 6, :], ACT.Copy).then_inc(v_hi, 1)

            def project_hi(h, piece):
                u = 4 * h + piece
                cols = slice((piece % 2) * BANK, (piece % 2 + 1) * BANK)
                if piece < 2:
                    act.wait_ge(proj_roped, 2 * h + piece + 1)
                    act.activation(qbuf[h % 2][0][:, cols], ps[:, 7, :], ACT.Copy).then_inc(proj_hi, 1)
                else:
                    act.wait_ge(proj_done, u + 1)
                    act.activation(kbuf[h % 2][0][0:ROT, cols], ps[0:ROT, 7, :], ACT.Copy).then_inc(proj_hi, 1)

            for piece in range(4):
                if piece == 2:
                    act.wait_ge(rot_turned, 1)
                    act.activation(kbuf[0][0][ROT:P, :], ps[ROT:P, 2:4, :].rearrange("p a n -> p (a n)"), ACT.Copy).then_inc(rot_hi, 1)
                project_hi(0, piece)
                value_hi(piece)
            act.activation(identR[:, :], keep.ident, ACT.Copy).then_inc(mask_ready, 1)
            act.activation(maskR[:, :], keep.neg, ACT.Copy).then_inc(mask_ready, 1)

            def turn_hi(t):
                for b, parts in groups_of(t):
                    g = bank_of[(t, b)]
                    act.wait_ge(pt_turned, g + 1)
                    for n, (first, count) in enumerate(parts):
                        src = ps[:, 4 + g % 2, :].rearrange("p (j c) -> p j c", c=P)[:, first - b:first - b + count, :]
                        last = act.activation(pt_view(pT[0], t, first, count), src, ACT.Copy)
                        last.then_inc(pt_hi, 1) if n == len(parts) - 1 else own(last)

            for m in range(STEPS + LAG + 2):
                t = m - LAG
                fresh = t % BLOCK_ROWS == 0
                if 0 <= m - 1 - Y0 < TILES:
                    j = m - 1 - Y0
                    act.wait_ge(y_turned, j + 1)
                    act.activation(act_parts[0][:, 0:KR, j * P:(j + 1) * P], ps[:, 7, :].rearrange("p (k c) -> p k c", c=P), ACT.Copy).then_inc(y_hi, 1)
                for h, piece in projections(m - 1):
                    if piece >= 2:
                        project_hi(h, piece)
                if 0 <= t < STEPS and not fresh:
                    turn_hi(t)
                if m < STEPS:
                    i = m % TILES
                    act.wait_ge(top_ready, m + 1)
                    if m >= ROWS:
                        act.wait_ge(pt_turned, through[m - ROWS])
                    act.activation(prob(m),
                                   ps[:, 2 * (m % 2):2 * (m % 2) + 2, :].rearrange("p a n -> p (a n)")[:, 0:(i + 1) * P],
                                   ACT.Exp, bias=neg_top[:, m % 4:m % 4 + 1], scale=SCALE,
                                   accum_out=total[:, m % 4:m % 4 + 1]).then_inc(exp_done, 1)
                if 0 <= t < STEPS and fresh:
                    if t > 0:
                        act.wait_ge(pv_done, t // BLOCK_ROWS)
                    turn_hi(t)
                for chunk in chunk_of(t - 2):
                    h, qc = divmod(chunk, 2)
                    half = slice(MLA_V_DIM * (h % 2), MLA_V_DIM * (h % 2 + 1))
                    act.wait_ge(pv_done, chunk + 1)
                    act.activation(act_parts[0][half, 4 + h // 2, qc * BANK:(qc + 1) * BANK], ps[half, 6, :], ACT.Copy).then_inc(out_hi, 1)
                for h, piece in projections(m - 1):
                    if piece < 2:
                        project_hi(h, piece)
                if 0 <= m - 1 < TILES - 4:
                    value_hi(m + 3)
                if m == 1:
                    act.activation(kbuf[1][0][ROT:P, :], kbuf[0][0][ROT:P, :].bitcast(F32), ACT.Copy).then_inc(rot_hi, 1)

        @block.vector
        def _(dve):
            own = Own(dve, dve_own)
            sin, cos = keep.sin[:, :, HALF:NFREQ], keep.cos[:, :, HALF:NFREQ]
            for t in range(TILES):
                row = lat[:, t, 0:MLA_Q_RANK]
                dve.tensor_scalar(row, row, keep.rstd_lat[:, 0, t:t + 1], None, ALU.mult).then_inc(q_normed, 1)
                if t == 3:
                    dve.wait_ge(pool_own, 1)
                    for at, src, sign in ((0, cos, 1.0), (1, cos, 1.0), (2, sin, -1.0), (3, sin, 1.0)):
                        dve.tensor_scalar(trow[:, :, ROT + at * MHALF:ROT + (at + 1) * MHALF], src, sign, None, ALU.mult).then_inc(trow_ready, 1)
            pieces = 0
            for t in range(TILES):
                dve.wait_ge(lat_hi, t + 1)
                dve.tensor_tensor(cT[1][:, :, t * P:(t + 1) * P], ps[:, LAT_BANK[t % 4], 0:(KQ + 1) * P].rearrange("p (k c) -> p k c", c=P),
                                  cT[0][:, :, t * P:(t + 1) * P].bitcast(F32), ALU.subtract).then_inc(lat_lo, 1)
                for hi, lo, src, gain in WEIGHT_PIECES[t]:
                    pieces += 1
                    dve.wait_ge(w_hi, pieces)
                    dve.scalar_tensor_tensor(lo, src, gain, hi.bitcast(F32), ALU.mult, ALU.subtract).then_inc(w_lo, 1)

            def value_lo(t):
                dve.wait_ge(v_hi, t + 1)
                dve.tensor_tensor(v[1][:, t, :], ps[:, 6, :], v[0][:, t, :].bitcast(F32), ALU.subtract).then_inc(v_lo, 1)

            def rope_piece(h, piece):
                if piece < 2:
                    cols = slice(piece * BANK, (piece + 1) * BANK)
                    dve.wait_ge(proj_done, 4 * h + piece + 1)
                    if h == 0 and piece == 0:
                        dve.wait_ge(tab_copied, 1)
                    dve.tensor_tensor(ps[:, 7, :], ps[:, 7, :], table[:, cols], ALU.mult).then_inc(proj_roped, 1)

            def project_lo(h, piece):
                cols = slice((piece % 2) * BANK, (piece % 2 + 1) * BANK)
                rows, buf = (slice(0, P), qbuf) if piece < 2 else (slice(0, ROT), kbuf)
                dve.wait_ge(proj_hi, 4 * h + piece + 1)
                dve.tensor_tensor(buf[h % 2][1][rows, cols], ps[rows, 7, :], buf[h % 2][0][rows, cols].bitcast(F32),
                                  ALU.subtract).then_inc(proj_lo, 1)

            for piece in range(4):
                rope_piece(0, piece)
                if piece == 2:
                    dve.wait_ge(rot_hi, 1)
                    dve.tensor_tensor(kbuf[0][1][ROT:P, :], ps[ROT:P, 2:4, :].rearrange("p a n -> p (a n)"),
                                      kbuf[0][0][ROT:P, :].bitcast(F32), ALU.subtract).then_inc(rot_lo, 1)
                project_lo(0, piece)
                value_lo(piece)
            for m in range(STEPS + LAG + 2):
                if m < STEPS:
                    i, s = m % TILES, m % 4
                    scores = ps[:, 2 * (m % 2):2 * (m % 2) + 2, :].rearrange("p a n -> p (a n)")
                    dve.wait_ge(score_done, m + 1)
                    own(dve.tensor_reduce(top[:, s:s + 1], scores[:, 0:(i + 1) * P], AX, ALU.max))
                    dve.tensor_scalar(neg_top[:, s:s + 1], top[:, s:s + 1], -SCALE, None, ALU.mult).then_inc(top_ready, 1)
                if 0 <= m - 1 - Y0 < TILES:
                    j = m - 1 - Y0
                    dve.wait_ge(y_hi, j + 1)
                    dve.tensor_tensor(act_parts[1][:, 0:KR, j * P:(j + 1) * P], ps[:, 7, :].rearrange("p (k c) -> p k c", c=P),
                                      act_parts[0][:, 0:KR, j * P:(j + 1) * P].bitcast(F32), ALU.subtract).then_inc(y_lo, 1)
                if 1 <= m <= STEPS:
                    s = (m - 1) % 4
                    dve.wait_ge(exp_done, m)
                    dve.reciprocal(inverse[:, s:s + 1], total[:, s:s + 1]).then_inc(inverse_ready, 1)
                for h, piece in projections(m - 1):
                    rope_piece(h, piece)
                    if piece >= 2:
                        project_lo(h, piece)
                t = m - LAG
                if 0 <= t < STEPS:
                    for b, parts in groups_of(t):
                        g = bank_of[(t, b)]
                        dve.wait_ge(pt_hi, g + 1)
                        for n, (first, count) in enumerate(parts):
                            src = ps[:, 4 + g % 2, :].rearrange("p (j c) -> p j c", c=P)[:, first - b:first - b + count, :]
                            last = dve.tensor_tensor(pt_view(pT[1], t, first, count), src,
                                                     pt_view(pT[0], t, first, count).bitcast(F32), ALU.subtract)
                            last.then_inc(pt_lo, 1) if n == len(parts) - 1 else own(last)
                for chunk in chunk_of(t - 2):
                    h, qc = divmod(chunk, 2)
                    half = slice(MLA_V_DIM * (h % 2), MLA_V_DIM * (h % 2 + 1))
                    cols = slice(qc * BANK, (qc + 1) * BANK)
                    dve.wait_ge(out_hi, chunk + 1)
                    dve.tensor_tensor(act_parts[1][half, 4 + h // 2, cols], ps[half, 6, :],
                                      act_parts[0][half, 4 + h // 2, cols].bitcast(F32), ALU.subtract).then_inc(out_lo, 1)
                for h, piece in projections(m - 1):
                    if piece < 2:
                        project_lo(h, piece)
                if 0 <= m - 1 < TILES - 4:
                    value_lo(m + 3)
                if m == 1:
                    dve.wait_ge(rot_lo, 1)
                    dve.tensor_copy(kbuf[1][1][ROT:P, :], kbuf[0][1][ROT:P, :].bitcast(F32)).then_inc(rot_lo, 1)

        @block.tensor
        def _(pe):
            for t in range(TILES):
                pe.wait_ge(kv_normed, t + 1)
                pe.wait_ge(q_normed, t + 1)
                if t >= 4:
                    pe.wait_ge(lat_lo, t - 3)
                for k in range(KQ + 1):
                    last = pe.transpose(ps[:, LAT_BANK[t % 4], k * P:(k + 1) * P], lat[:, t, k * P:(k + 1) * P], keep.ident)
                last.then_inc(lat_turned, 1)
                if t == 3:
                    pe.wait_ge(trow_ready, 4)
                    for j in range(TILES):
                        last = pe.transpose(ps[:, 4 + j // 4, (j % 4) * P:(j % 4 + 1) * P], trow[:, j, :], keep.ident)
                    last.then_inc(tab_turned, 1)
            pe.wait_ge(krow_ready, 2)
            for t in range(TILES):
                last = pe.transpose(ps[:, 2 + t // 4, (t % 4) * P:(t % 4 + 1) * P], krow[:, t, :], keep.ident)
            last.then_inc(rot_turned, 1)

            def value(t):
                if t >= 1:
                    pe.wait_ge(v_lo, t)
                split_product(pe, ps[:, 6, :], cT[0][:, KQ, t * P:(t + 1) * P], cT[1][:, KQ, t * P:(t + 1) * P],
                              wv[0], wv[1], True, True).then_inc(v_done, 1)

            def project(h, piece):
                u = 4 * h + piece
                cols = slice((piece % 2) * BANK, (piece % 2 + 1) * BANK)
                if u >= 1:
                    pe.wait_ge(proj_lo, u)
                if piece < 2:
                    for k in range(KQ):
                        last = split_product(pe, ps[:, 7, :], wq[0][:, k, h, :], wq[1][:, k, h, :],
                                             cT[0][:, k, cols], cT[1][:, k, cols], k == 0, k == KQ - 1)
                else:
                    last = split_product(pe, ps[0:ROT, 7, :], wk[0][:, h, :], wk[1][:, h, :],
                                         cT[0][:, KQ, cols], cT[1][:, KQ, cols], True, True)
                last.then_inc(proj_done, 1)

            pe.wait_ge(lat_lo, TILES)
            pe.wait_ge(w_lo, sum(len(some) for some in WEIGHT_PIECES))
            for piece in range(4):
                project(0, piece)
                value(piece)
            pe.wait_ge(rot_lo, 1)
            pe.wait_ge(mask_ready, 2)
            for m in range(STEPS + LAG + 1):
                if m < STEPS:
                    h, i = divmod(m, TILES)
                    if i == 0:
                        pe.wait_ge(proj_lo, 4 * (h + 1))
                    if m == TILES:
                        pe.wait_ge(rot_lo, 2)
                    if m >= 2:
                        pe.wait_ge(exp_done, m - 1)
                    q, k = qbuf[h % 2], kbuf[h % 2]
                    width = (i + 1) * P
                    for c in range(0, width, BANK):
                        n = min(BANK, width - c)
                        last = split_product(pe, ps[:, 2 * (m % 2) + c // BANK, 0:n], q[0][:, i * P:(i + 1) * P], q[1][:, i * P:(i + 1) * P],
                                             k[0][:, c:c + n], k[1][:, c:c + n], True, c + n < width)
                    at = i * P % BANK
                    last = pe.matmul(ps[:, 2 * (m % 2) + i * P // BANK, at:at + P], identR[:, :], maskR[:, :], start=False, stop=True)
                    last.then_inc(score_done, 1)
                t = m - LAG
                if 0 <= t < STEPS:
                    pe.wait_ge(prob_ready, t + 1)
                    for b, parts in groups_of(t):
                        g = bank_of[(t, b)]
                        if g >= 2:
                            pe.wait_ge(pt_lo, g - 1)
                        else:
                            pe.wait_ge(tab_copied, 1)
                        for j in range(b, min(b + 4, t % TILES + 1)):
                            last = pe.transpose(ps[:, 4 + g % 2, (j - b) * P:(j - b + 1) * P], prob(t)[:, j * P:(j + 1) * P], keep.ident)
                        last.then_inc(pt_turned, 1)
                t = m - LAG - 1
                for chunk in chunk_of(t):
                    h, qc = divmod(chunk, 2)
                    pe.wait_ge(pt_lo, through[t])
                    if chunk >= 1:
                        pe.wait_ge(out_lo, chunk)
                    else:
                        pe.wait_ge(v_lo, TILES)
                    pair = slice(h // 2 * P, (h // 2 + 1) * P)
                    keys = BLOCK_ROWS * (qc + 1)
                    for j in range(keys):
                        ahead = max(j - BLOCK_ROWS * qc, 0) * P
                        at = slice(PT_OFF[j], PT_OFF[j] + BANK - ahead)
                        last = split_product(pe, ps[:, 6, ahead:BANK], v[0][:, j, pair], v[1][:, j, pair],
                                             pT[0][:, at], pT[1][:, at], j == 0, j == keys - 1)
                    last.then_inc(pv_done, 1)
                for h, piece in projections(m):
                    project(h, piece)
                if m < TILES - 4:
                    value(m + 4)
                if 0 <= m - Y0 < TILES:
                    j = m - Y0
                    if j >= 1:
                        pe.wait_ge(y_lo, j)
                    else:
                        pe.wait_ge(proj_lo, 4 * MLA_HEADS)
                    for k in range(KR):
                        last = pe.transpose(ps[:, 7, k * P:(k + 1) * P], keep.q_y[:, j, k * P:(k + 1) * P], keep.ident)
                    last.then_inc(y_turned, 1)


def up_product(pe, keep, up, z, c):
    cols = slice(c * BANK, (c + 1) * BANK)
    bank = (GATE_BANKS, UP_BANKS)[z].start + c
    for k in range(KD):
        last = split_product(pe, keep.ps[:, bank, :], up[0][:, k, z, :], up[1][:, k, z, :],
                             keep.actHi[:, k, cols], keep.actLo[:, k, cols], k == 0, k == KD - 1)
    return last


def mix_output(nc, io, keep):
    KR = RET_WIDTH // P
    with ExitStack() as ctx:
        def sb(name, shape, dt=F32):
            return ctx.enter_context(nc.sbuf_tensor(name, shape, dt))

        def sem(name):
            return ctx.enter_context(nc.semaphore(name))

        wHi = sb("woHi", [P, KD, D_MODEL], F32R)
        wLo = sb("woLo", [P, KD, D_MODEL], F32R)
        raw = keep.raw_wo
        four_rows = keep.q_y.rearrange("p t n -> p (t n)").rearrange("p (b n) -> p b n", b=4)
        g_post, g_pre, xrow = four_rows[:, 0, :], four_rows[:, 1, :], four_rows[:, 2:4, :]
        x1 = sb("x1row", [P, 2, D_MODEL])
        stat = sb("statC", [P, 4, TILES])
        rows = keep.latent.rearrange("p t n -> p (t n)")[:, 0:3 * D_MODEL].rearrange("p (b n) -> p b n", b=3)
        mixn, h2, junk = rows[:, 0, :], rows[:, 1, :], rows[:, 2, :]
        ps = keep.ps

        gains_in = sem("gains_in")
        x_in = [sem("xr_in0"), sem("xr_in1")]
        w_hi = sem("wo_hi")
        w_lo = sem("wo_lo")
        mix_done = sem("mix_done")
        mix_sq = sem("mix_sq")
        mix_rstd = sem("mix_rstd")
        mix_read = sem("mix_read")
        x1_done = sem("x1_done")
        x1_sq = sem("x1_sq")
        x1_rstd = sem("x1_rstd")
        x1_stored = [sem("x1_stored0"), sem("x1_stored1")]
        h2_done = sem("h2_done")
        h2_turned = sem("h2_turned")
        h2_hi = sem("h2_hi")
        h2_lo = sem("h2_lo")
        pool_own = sem("pool_ownC")

        xr = io.x[0].rearrange("(t p) d -> t p d", p=P)
        wr = io.w_o[0].rearrange("(k p) n -> k p n", p=P)
        x1r = io.x1.rearrange("(t p) d -> t p d", p=P)

        def banks(t):
            return ps[:, 2 * (t % 2):2 * (t % 2) + 2, :].rearrange("p a n -> p (a n)")

        def tile_of(a, t, k0, k1):
            return a[:, k0:k1, t * P:(t + 1) * P]

        block = ctx.enter_context(nc.Block())

        @block.sync
        def _(sp):
            def load_x(t):
                if t >= 2:
                    sp.wait_ge(x1_done, t - 1)
                sp.dma_start(xrow[:, t % 2, :], xr[t]).then_inc(x_in[t % 2], 16)

            load_x(0)
            sp.dma_start(g_post, io.g_post_mix[0].partition_broadcast(P)).then_inc(gains_in, 16)
            for k in range(WO_RING, KD):
                sp.wait_ge(w_lo, k - WO_RING + 1)
                sp.dma_start(raw[:, k % WO_RING, :], wr[k]).then_inc(keep.wo_in[k % WO_RING], 16)
            sp.dma_start(g_pre, io.g_pre_ffn[0].partition_broadcast(P)).then_inc(gains_in, 16)
            load_x(1)
            w_up = io.w_up[0].rearrange("(k p) (z j c) -> p k z j c", p=P, z=2, c=P)
            for z in range(2):
                sp.dma_start(keep.raw_up[:, :, z, :], w_up[:, :, z, 0, :]).then_inc(keep.up_in, 16)
            for t in range(TILES):
                sp.wait_ge(x1_done, t + 1)
                sp.dma_start(x1r[t], x1[:, t % 2, :]).then_inc(x1_stored[t % 2], 16)
                if t + 2 < TILES:
                    load_x(t + 2)
            for b in range(2):
                sp.wait_ge(x1_stored[b], 16 * TILES // 2)

        @block.gpsimd
        def _(pool):
            own = Own(pool, pool_own)
            for t in range(TILES):
                for done, ready, i in ((mix_sq, mix_rstd, 0), (x1_sq, x1_rstd, 2)):
                    pool.wait_ge(done, t + 1)
                    own(pool.tensor_scalar(stat[:, i + 1, t:t + 1], stat[:, i, t:t + 1], 1.0 / D_MODEL, EPS, ALU.mult, ALU.add))
                    pool.tensor_tensor(stat[:, i + 1, t:t + 1], stat[:, i + 1, t:t + 1], keep.neghalf[:, 0:1], ALU.pow).then_inc(ready, 1)

        @block.scalar
        def _(act):
            for k in range(KD):
                act.wait_ge(keep.wo_in[k % WO_RING], 16 * (k // WO_RING + 1))
                if k < KR:
                    act.activation(wHi[:, k, :], raw[:, k % WO_RING, :], ACT.Identity,
                                   scale=keep.cols[:, COL_RET_GN + k:COL_RET_GN + k + 1]).then_inc(w_hi, 1)
                else:
                    act.activation(wHi[:, k, :], raw[:, k % WO_RING, :], ACT.Copy).then_inc(w_hi, 1)
            act.wait_ge(keep.up_in, 32)
            act.wait_ge(w_lo, KD)
            act.activation(keep.up0[0], keep.raw_up, ACT.Copy).then_inc(keep.up_hi, 1)
            for t in range(TILES + 1):
                if t < TILES:
                    act.wait_ge(mix_done, t + 1)
                    if t >= 1:
                        act.wait_ge(x1_sq, t)
                    act.activation(junk, banks(t), ACT.Square, accum_out=stat[:, 0, t:t + 1]).then_inc(mix_sq, 1)
                    act.wait_ge(x1_done, t + 1)
                    act.wait_ge(mix_sq, t + 1)
                    act.activation(junk, x1[:, t % 2, :], ACT.Square, accum_out=stat[:, 2, t:t + 1]).then_inc(x1_sq, 1)
                if t >= 1:
                    act.wait_ge(h2_turned, t)
                    act.activation(tile_of(keep.actHi, t - 1, 0, KD), ps[:, 6:8, :].rearrange("p a (k c) -> p (a k) c", c=P),
                                   ACT.Copy).then_inc(h2_hi, 1)

        @block.vector
        def _(dve):
            for k in range(KD):
                dve.wait_ge(w_hi, k + 1)
                if k < KR:
                    dve.scalar_tensor_tensor(wLo[:, k, :], raw[:, k % WO_RING, :], keep.cols[:, COL_RET_GN + k:COL_RET_GN + k + 1],
                                             wHi[:, k, :].bitcast(F32), ALU.mult, ALU.subtract).then_inc(w_lo, 1)
                else:
                    dve.tensor_tensor(wLo[:, k, :], raw[:, k % WO_RING, :], wHi[:, k, :].bitcast(F32), ALU.subtract).then_inc(w_lo, 1)
            dve.wait_ge(keep.up_hi, 1)
            dve.tensor_tensor(keep.up0[1], keep.raw_up, keep.up0[0].bitcast(F32), ALU.subtract).then_inc(keep.up_lo, 1)
            dve.wait_ge(gains_in, 32)
            for t in range(TILES + 1):
                if t < TILES:
                    dve.wait_ge(mix_rstd, t + 1)
                    if t >= 1:
                        dve.wait_ge(x1_done, t)
                    dve.scalar_tensor_tensor(mixn, banks(t), stat[:, 1, t:t + 1], g_post, ALU.mult, ALU.mult).then_inc(mix_read, 1)
                    dve.wait_ge(mix_read, t + 1)
                    dve.wait_ge(x_in[t % 2], 16 * (t // 2 + 1))
                    if t >= 2:
                        dve.wait_ge(x1_stored[t % 2], 16 * (t // 2))
                    dve.tensor_tensor(x1[:, t % 2, :], mixn, xrow[:, t % 2, :], ALU.add).then_inc(x1_done, 1)
                    dve.wait_ge(x1_rstd, t + 1)
                    if t >= 1:
                        dve.wait_ge(h2_turned, t)
                    dve.scalar_tensor_tensor(h2, x1[:, t % 2, :], stat[:, 3, t:t + 1], g_pre, ALU.mult, ALU.mult).then_inc(h2_done, 1)
                if t >= 1:
                    dve.wait_ge(h2_hi, t)
                    dve.tensor_tensor(tile_of(keep.actLo, t - 1, 0, KD), ps[:, 6:8, :].rearrange("p a (k c) -> p (a k) c", c=P),
                                      tile_of(keep.actHi, t - 1, 0, KD).bitcast(F32), ALU.subtract).then_inc(h2_lo, 1)

        @block.tensor
        def _(pe):
            for t in range(TILES + 1):
                if t < TILES:
                    if t >= 2:
                        pe.wait_ge(mix_read, t - 1)
                    for k in range(KD):
                        if t == 0:
                            pe.wait_ge(w_lo, k + 1)
                        for half in range(2):
                            cols = slice(half * BANK, (half + 1) * BANK)
                            last = split_product(pe, ps[:, 2 * (t % 2) + half, :], keep.actHi[:, k, t * P:(t + 1) * P],
                                                 keep.actLo[:, k, t * P:(t + 1) * P], wHi[:, k, cols], wLo[:, k, cols], k == 0, k == KD - 1)
                    last.then_inc(mix_done, 1)
                if t >= 1:
                    pe.wait_ge(h2_done, t)
                    if t >= 2:
                        pe.wait_ge(h2_lo, t - 1)
                    for k in range(KD):
                        last = pe.transpose(ps[:, 6 + k // 4, (k % 4) * P:(k % 4 + 1) * P], h2[:, k * P:(k + 1) * P], keep.ident)
                    last.then_inc(h2_turned, 1)
                if t >= TILES - 1:
                    if t == TILES - 1:
                        pe.wait_ge(keep.up_lo, 1)
                        pe.wait_ge(h2_lo, BANK // P)
                        pe.wait_ge(mix_read, TILES - 1)
                    up_product(pe, keep, keep.up0, t - TILES + 1, 0)


def conv_ffn(nc, io, keep):
    PAIR = 2
    ROUNDS = FF_TILES // PAIR
    OUTS = TILES * (D_MODEL // BANK)
    DOWN_BANKS = [2, 3, 6, 7]
    RING = len(DOWN_BANKS)
    with ExitStack() as ctx:
        def sb(name, shape, dt=F32):
            return ctx.enter_context(nc.sbuf_tensor(name, shape, dt))

        def sem(name):
            return ctx.enter_context(nc.semaphore(name))

        raw_up = keep.raw_up
        up1 = [sb("wupHi", [P, KD, 2, P], F32R)[:, :, :, :], sb("wupLo", [P, KD, 2, P], F32R)[:, :, :, :]]
        up = [keep.up0, up1]
        raw_dn = sb("raw_dn", [P, PAIR, D_MODEL])
        dn = [sb("wdnHi", [P, PAIR, D_MODEL], F32R), sb("wdnLo", [P, PAIR, D_MODEL], F32R)]
        f = [sb("fHi", [P, PAIR, SEQ], F32R), sb("fLo", [P, PAIR, SEQ], F32R)]
        conv_g = sb("conv_g", [P, SEQ])
        conv_u = sb("conv_u", [P, SEQ])
        gelu = sb("gelu", [P, SEQ])
        ps = keep.ps
        gate_ps = ps[:, GATE_BANKS, :].rearrange("p a n -> p (a n)")
        up_ps = ps[:, UP_BANKS, :].rearrange("p a n -> p (a n)")

        dn_in = sem("dn_in")
        up_in, up_hi, up_lo = keep.up_in, keep.up_hi, keep.up_lo
        dn_hi = sem("dn_hi")
        dn_lo = sem("dn_lo")
        gate_done = sem("gateD_done")
        up_done = sem("upD_done")
        gate_tap = sem("gate_tap")
        up_tap = sem("up_tap")
        gate_read = sem("gate_read")
        up_read = sem("up_read")
        gelu_done = sem("gelu_done")
        product = sem("product")
        f_hi = sem("f_hi")
        f_lo = sem("f_lo")
        down_done = sem("down_done")
        down_free = sem("down_free")
        ffn_zero = sem("ffn_zero")
        tap_own = sem("tap_own")

        w_up = io.w_up[0].rearrange("(k p) (z j c) -> p k z j c", p=P, z=2, c=P)
        w_dn = io.w_down[0].rearrange("(j p) n -> p j n", p=P)

        def rounds(eng, body):
            body(0, True, False)
            with eng.Fori(1, ROUNDS - 1) as r:
                body(r, False, False)
            body(ROUNDS - 1, False, True)

        def col(at, n):
            return keep.cols[:, bass.ds(n + at, 1)]

        block = ctx.enter_context(nc.Block())

        @block.sync
        def _(sp):
            def load_up(n):
                sp.wait_ge(up_lo, n)
                for z in range(2):
                    sp.dma_start(raw_up[:, :, z, :], w_up[:, :, z, bass.ds(n, 1), :].squeeze(2)).then_inc(up_in, 16)

            def body(r, first, last):
                if not first:
                    load_up(r * PAIR)
                    sp.wait_ge(dn_lo, r)
                else:
                    load_up(1)
                sp.dma_start(raw_dn[:, :, :], w_dn[:, bass.ds(r * PAIR, PAIR), :]).then_inc(dn_in, 16)
                if not first:
                    load_up(r * PAIR + 1)

            rounds(sp, body)
            sp.wait_ge(up_done, FF_TILES - 1)
            x1r = io.x1.rearrange("(t p) d -> t p d", p=P)
            for s in range(KD + PLE_DIM // P):
                if s == 0:
                    sp.wait_ge(up_lo, FF_TILES)
                if s >= GATE_RING:
                    sp.wait_ge(keep.gate_lo, s - GATE_RING + 1)
                src = io.w_ple_gate[0][s * P:(s + 1) * P, :] if s < KD else io.w_ple[0][(s - KD) * P:(s - KD + 1) * P, :]
                sp.dma_start(keep.raw_gate[:, s % GATE_RING, :], src).then_inc(keep.gate_in[s % GATE_RING], 16)
                if s == GATE_RING:
                    for t in range(2):
                        sp.dma_start(keep.four_rows[:, t, :], x1r[t]).then_inc(keep.x1_in[t], 16)
                    for row, gain in ((2, io.g_post_ffn), (3, io.b_ple_gate)):
                        sp.dma_start(keep.four_rows[:, row, :], gain[0].partition_broadcast(P)).then_inc(keep.rows_in, 16)
            sp.wait_ge(keep.rows_in, 32)

        @block.gpsimd
        def _(pool):
            pool.memset(keep.ffn[:, :, :], 0.0).then_inc(ffn_zero, 1)

        @block.scalar
        def _(act):
            def split_up(n, p, early):
                act.wait_ge(up_in, n * 32 + 32)
                if not early:
                    act.wait_ge(up_done, n - 1)
                act.activation(up[p][0], raw_up, ACT.Copy).then_inc(up_hi, 1)

            def step(n, p, r, first_step, first_round):
                act.wait_ge(gate_done, n + 1)
                if not first_step:
                    act.wait_ge(gelu_done, n)
                act.activation(conv_g[:, :], gate_ps, ACT.Identity, bias=col(COL_BIAS, n), scale=col(COL_W2, n)).then_inc(gate_tap, 1)
                act.wait_ge(gate_read, n + 1)
                if not first_step:
                    act.wait_ge(product, n)
                act.activation(gelu[:, :], conv_g[:, :], ACT.Gelu_apprx_tanh).then_inc(gelu_done, 1)
                act.wait_ge(up_done, n + 1)
                if not first_step:
                    act.wait_ge(f_lo, n)
                act.activation(conv_u[:, :], up_ps, ACT.Identity, bias=col(COL_BIAS + FF_TILES, n),
                               scale=col(COL_W2 + FF_TILES, n)).then_inc(up_tap, 1)
                act.wait_ge(product, n + 1)
                if not first_round:
                    act.wait_ge(down_done, r * OUTS)
                act.activation(f[0][:, p, :], conv_u[:, :], ACT.Copy).then_inc(f_hi, 1)

            def body(r, first, last):
                n = r * PAIR
                split_up(n + 1, 1, first)
                step(n, 0, r, first, first)
                act.wait_ge(dn_in, r * 16 + 16)
                act.activation(dn[0][:, :, :], raw_dn[:, :, :], ACT.Copy).then_inc(dn_hi, 1)
                if not last:
                    split_up(n + 2, 0, False)
                step(n + 1, 1, r, False, first)

            rounds(act, body)
            for t in range(TILES):
                if t == 0:
                    act.wait_ge(up_done, FF_TILES)
                act.wait_ge(keep.gate_in[t % GATE_RING], 16 * (t // GATE_RING + 1))
                act.activation(keep.actHi[:, t, :], keep.raw_gate[:, t % GATE_RING, :], ACT.Copy).then_inc(keep.gate_hi, 1)
                act.wait_ge(down_free, RING + (ROUNDS - 1) * OUTS + 2 * t + 2)
                if t >= 1:
                    act.wait_ge(keep.f_sq, t)
                act.activation(gelu[:, :], keep.ffn[:, t, :], ACT.Square, accum_out=keep.rstd_lat[:, 0, t:t + 1]).then_inc(keep.f_sq, 1)

        @block.vector
        def _(dve):
            def split_up(p, n):
                dve.wait_ge(up_hi, n + 1)
                dve.tensor_tensor(up[p][1], raw_up, up[p][0].bitcast(F32), ALU.subtract).then_inc(up_lo, 1)

            def convolve(n, src, out, tap, tapped, read, at):
                dve.wait_ge(tap, n + 1)
                dve.scalar_tensor_tensor(out[:, 1:SEQ], src[:, 0:SEQ - 1], col(COL_W1 + at, n), out[:, 1:SEQ], ALU.mult, ALU.add).then_inc(tap_own, 1)
                dve.wait_ge(tap_own, tapped)
                dve.scalar_tensor_tensor(out[:, 2:SEQ], src[:, 0:SEQ - 2], col(COL_W0 + at, n), out[:, 2:SEQ], ALU.mult, ALU.add).then_inc(read, 1)

            def step(n):
                convolve(n, gate_ps, conv_g, gate_tap, n * 2 + 1, gate_read, 0)
                convolve(n, up_ps, conv_u, up_tap, n * 2 + 2, up_read, FF_TILES)
                dve.wait_ge(up_read, n + 1)
                dve.wait_ge(gelu_done, n + 1)
                dve.tensor_tensor(conv_u[:, :], gelu[:, :], conv_u[:, :], ALU.mult).then_inc(product, 1)

            def finish(n, p):
                dve.wait_ge(f_hi, n + 1)
                dve.tensor_tensor(f[1][:, p, :], conv_u[:, :], f[0][:, p, :].bitcast(F32), ALU.subtract).then_inc(f_lo, 1)

            def split_gate(s):
                dve.wait_ge(keep.gate_hi, s + 1)
                dve.tensor_tensor(keep.actLo[:, s, :], keep.raw_gate[:, s % GATE_RING, :], keep.actHi[:, s, :].bitcast(F32),
                                  ALU.subtract).then_inc(keep.gate_lo, 1)

            def add_round(r, last=False):
                for o in range(OUTS):
                    t, half = divmod(o, 2)
                    row = keep.ffn[:, t, half * BANK:(half + 1) * BANK]
                    dve.wait_ge(down_done, r * OUTS + o + 1)
                    dve.tensor_tensor(row, ps[:, DOWN_BANKS[o % RING], :], row, ALU.add).then_inc(down_free, 1)
                    if last and half == 1:
                        split_gate(t)

            def body(r, first, last):
                n = r * PAIR
                split_up(1, n + 1)
                step(n)
                if not first:
                    add_round(r - 1)
                finish(n, 0)
                dve.wait_ge(dn_hi, r + 1)
                dve.tensor_tensor(dn[1][:, :, :], raw_dn[:, :, :], dn[0][:, :, :].bitcast(F32), ALU.subtract).then_inc(dn_lo, 1)
                if not last:
                    split_up(0, n + 2)
                step(n + 1)
                finish(n + 1, 1)

            dve.sem_inc(down_free, RING)
            dve.wait_ge(ffn_zero, 1)
            rounds(dve, body)
            add_round(ROUNDS - 1, True)

        @block.tensor
        def _(pe):
            def step(n, p, first):
                pe.wait_ge(up_lo, n + 1)
                for z, read, done in ((0, gate_read, gate_done), (1, up_read, up_done)):
                    if not first:
                        pe.wait_ge(read, n)
                    for c in range(1 if first else 0, SEQ // BANK):
                        last = up_product(pe, keep, up[p], z, c)
                    last.then_inc(done, 1)

            def down(r):
                pe.wait_ge(f_lo, r * PAIR + PAIR)
                pe.wait_ge(dn_lo, r + 1)
                for o in range(OUTS):
                    t, half = divmod(o, 2)
                    pe.wait_ge(down_free, r * OUTS + o + 1)
                    for p in range(PAIR):
                        last = split_product(pe, ps[:, DOWN_BANKS[o % RING], :], f[0][:, p, t * P:(t + 1) * P], f[1][:, p, t * P:(t + 1) * P],
                                             dn[0][:, p, half * BANK:(half + 1) * BANK], dn[1][:, p, half * BANK:(half + 1) * BANK],
                                             p == 0, p == PAIR - 1)
                    last.then_inc(down_done, 1)

            def body(r, first, last):
                n = r * PAIR
                step(n, 0, first)
                if not first:
                    down(r - 1)
                step(n + 1, 1, False)

            rounds(pe, body)
            down(ROUNDS - 1)


def layer_embedding(nc, io, keep):
    KE = PLE_DIM // P
    with ExitStack() as ctx:
        def sb(name, shape, dt=F32):
            return ctx.enter_context(nc.sbuf_tensor(name, shape, dt))

        def sem(name):
            return ctx.enter_context(nc.semaphore(name))

        wg = (keep.actHi, keep.actLo)
        wp = [sb("wpHi", [P, KE, D_MODEL], F32R), sb("wpLo", [P, KE, D_MODEL], F32R)]
        x1, g_ffn, bias = keep.four_rows[:, 0:2, :], keep.four_rows[:, 2, :], keep.four_rows[:, 3, :]
        xT = [sb("x2Hi", [P, 2, KD, P], F32R), sb("x2Lo", [P, 2, KD, P], F32R)]
        pT = [sb("pHi", [P, 2, KE, P], F32R), sb("pLo", [P, 2, KE, P], F32R)]
        prow = sb("prow", [P, 2, PLE_DIM])
        orow = sb("out_row", [P, 2, D_MODEL])
        g_ple = sb("g_ple_row", [P, D_MODEL])
        gate = sb("ple_gate", [P, D_MODEL])
        e = sb("ple_e", [P, D_MODEL])
        junk = sb("junkE", [P, D_MODEL])
        stat = sb("statE", [P, 4, TILES])
        ps = keep.ps
        gate_ps = ps[:, 0:2, :].rearrange("p a n -> p (a n)")
        e_ps = ps[:, 2:4, :].rearrange("p a n -> p (a n)")

        rows_in = keep.rows_in
        x1_in = keep.x1_in
        p_in = [sem("p_in0"), sem("p_in1")]
        f_rstd = sem("f_rstd")
        x2_part = sem("x2_part")
        x2_done = sem("x2_done")
        x2_turned = sem("x2_turned")
        x2_hi = sem("x2_hi")
        x2_lo = sem("x2_lo")
        gate_done = sem("gateE_done")
        gate_biased = sem("gate_biased")
        gate_sig = sem("gate_sig")
        ple_done = sem("ple_done")
        e_done = sem("e_done")
        e_sq = sem("e_sq")
        e_rstd = sem("e_rstd")
        e_normed = sem("e_normed")
        out_ready = sem("out_ready")
        out_stored = [sem("out_stored0"), sem("out_stored1")]
        pool_own = sem("pool_ownE")

        x1r = io.x1.rearrange("(t p) d -> t p d", p=P)
        outr = io.out[0].rearrange("(t p) d -> t p d", p=P)
        pr = io.p[0, 0].rearrange("(t p) d -> t p d", p=P)

        def turned_bank(t):
            return ps[:, 4:6, :].rearrange("p a (k c) -> p (a k) c", c=P)

        block = ctx.enter_context(nc.Block())

        @block.sync
        def _(sp):
            def load_rows(t):
                if t >= 2:
                    sp.wait_ge(x2_done, t - 1)
                    sp.wait_ge(x2_turned, t - 1)
                    sp.dma_start(x1[:, t % 2, :], x1r[t]).then_inc(x1_in[t % 2], 16)
                sp.dma_start(prow[:, t % 2, :], pr[t]).then_inc(p_in[t % 2], 16)

            load_rows(0)
            load_rows(1)
            sp.dma_start(g_ple[:, :], io.g_post_ple[0].partition_broadcast(P)).then_inc(rows_in, 16)
            for t in range(TILES):
                if t + 2 < TILES:
                    load_rows(t + 2)
                sp.wait_ge(out_ready, t + 1)
                sp.dma_start(outr[t], orow[:, t % 2, :]).then_inc(out_stored[t % 2], 16)
            for b in range(2):
                sp.wait_ge(out_stored[b], 16 * TILES // 2)

        @block.gpsimd
        def _(pool):
            own = Own(pool, pool_own)

            def rstd(done, ready, i, t):
                pool.wait_ge(done, t + 1)
                own(pool.tensor_scalar(stat[:, i + 1, t:t + 1], stat[:, i, t:t + 1], 1.0 / D_MODEL, EPS, ALU.mult, ALU.add))
                pool.tensor_tensor(stat[:, i + 1, t:t + 1], stat[:, i + 1, t:t + 1], keep.neghalf[:, 0:1], ALU.pow).then_inc(ready, 1)

            pool.wait_ge(keep.f_sq, TILES)
            own(pool.tensor_scalar(keep.rstd_lat[:, 1, :], keep.rstd_lat[:, 0, :], 1.0 / D_MODEL, EPS, ALU.mult, ALU.add))
            pool.tensor_tensor(keep.rstd_lat[:, 1, :], keep.rstd_lat[:, 1, :], keep.neghalf, ALU.pow).then_inc(f_rstd, 1)
            for t in range(TILES):
                rstd(e_sq, e_rstd, 2, t)

        @block.scalar
        def _(act):
            squares = [0]

            def square(src, accum, done, t):
                if squares[0]:
                    act.wait_ge(*squares[1])
                act.activation(junk[:, :], src, ACT.Square, accum_out=accum).then_inc(done, 1)
                squares[0:] = [1, (done, t + 1)]

            def turn_hi(t):
                act.wait_ge(x2_turned, t + 1)
                if t >= 2:
                    act.wait_ge(ple_done, t - 1)
                act.activation(xT[0][:, t % 2], turned_bank(t), ACT.Copy).then_inc(x2_hi, 1)
                act.activation(pT[0][:, t % 2], ps[:, 6, 0:KE * P].rearrange("p (k c) -> p k c", c=P), ACT.Copy).then_inc(x2_hi, 1)

            for s in range(KE):
                act.wait_ge(keep.gate_in[(KD + s) % GATE_RING], 16 * ((KD + s) // GATE_RING + 1))
                act.activation(wp[0][:, s, :], keep.raw_gate[:, (KD + s) % GATE_RING, :], ACT.Copy).then_inc(keep.gate_hi, 1)
            turn_hi(0)
            for t in range(TILES):
                if t + 1 < TILES:
                    turn_hi(t + 1)
                act.wait_ge(gate_biased, t + 1)
                act.activation(gate[:, :], gate[:, :], ACT.Sigmoid).then_inc(gate_sig, 1)
                act.wait_ge(e_done, t + 1)
                square(e[:, :], stat[:, 2, t:t + 1], e_sq, t)

        @block.vector
        def _(dve):
            def x2_rows(t):
                row = keep.ffn[:, t, :]
                dve.scalar_tensor_tensor(row, row, keep.rstd_lat[:, 1, t:t + 1], g_ffn, ALU.mult, ALU.mult).then_inc(x2_part, 1)
                dve.wait_ge(x2_part, t + 1)
                dve.wait_ge(x1_in[t % 2], 16 * (t // 2 + 1))
                dve.tensor_tensor(row, row, x1[:, t % 2, :], ALU.add).then_inc(x2_done, 1)

            def turn_lo(t):
                dve.wait_ge(x2_hi, 2 * t + 2)
                dve.tensor_tensor(xT[1][:, t % 2], turned_bank(t), xT[0][:, t % 2].bitcast(F32), ALU.subtract).then_inc(x2_lo, 1)
                dve.tensor_tensor(pT[1][:, t % 2], ps[:, 6, 0:KE * P].rearrange("p (k c) -> p k c", c=P), pT[0][:, t % 2].bitcast(F32),
                                  ALU.subtract).then_inc(x2_lo, 1)

            dve.wait_ge(f_rstd, 1)
            x2_rows(0)
            for s in range(KE):
                dve.wait_ge(keep.gate_hi, KD + s + 1)
                dve.tensor_tensor(wp[1][:, s, :], keep.raw_gate[:, (KD + s) % GATE_RING, :], wp[0][:, s, :].bitcast(F32),
                                  ALU.subtract).then_inc(keep.gate_lo, 1)
            turn_lo(0)
            x2_rows(1)
            dve.wait_ge(rows_in, 48)
            for t in range(TILES):
                if t + 1 < TILES:
                    turn_lo(t + 1)
                if t + 2 < TILES:
                    x2_rows(t + 2)
                dve.wait_ge(gate_done, t + 1)
                if t >= 1:
                    dve.wait_ge(e_done, t)
                dve.tensor_tensor(gate[:, :], gate_ps, bias, ALU.add).then_inc(gate_biased, 1)
                dve.wait_ge(gate_sig, t + 1)
                dve.wait_ge(ple_done, t + 1)
                if t >= 1:
                    dve.wait_ge(out_ready, t)
                dve.tensor_tensor(e[:, :], e_ps, gate[:, :], ALU.mult).then_inc(e_done, 1)
                dve.wait_ge(e_rstd, t + 1)
                dve.scalar_tensor_tensor(e[:, :], e[:, :], stat[:, 3, t:t + 1], g_ple[:, :], ALU.mult, ALU.mult).then_inc(e_normed, 1)
                dve.wait_ge(e_normed, t + 1)
                if t >= 2:
                    dve.wait_ge(out_stored[t % 2], 16 * (t // 2))
                dve.tensor_tensor(orow[:, t % 2, :], e[:, :], keep.ffn[:, t, :], ALU.add).then_inc(out_ready, 1)

        @block.tensor
        def _(pe):
            def turn(t):
                pe.wait_ge(x2_done, t + 1)
                pe.wait_ge(p_in[t % 2], 16 * (t // 2 + 1))
                if t >= 1:
                    pe.wait_ge(x2_lo, 2 * t)
                for k in range(KD):
                    pe.transpose(ps[:, 4 + k // 4, (k % 4) * P:(k % 4 + 1) * P], keep.ffn[:, t, k * P:(k + 1) * P], keep.ident)
                for k in range(KE):
                    last = pe.transpose(ps[:, 6, k * P:(k + 1) * P], prow[:, t % 2, k * P:(k + 1) * P], keep.ident)
                last.then_inc(x2_turned, 1)

            turn(0)
            for t in range(TILES):
                pe.wait_ge(x2_lo, 2 * t + 2)
                if t >= 1:
                    pe.wait_ge(gate_biased, t)
                for half in range(2):
                    cols = slice(half * BANK, (half + 1) * BANK)
                    for k in range(KD):
                        last = split_product(pe, ps[:, half, :], xT[0][:, t % 2, k, :], xT[1][:, t % 2, k, :],
                                             wg[0][:, k, cols], wg[1][:, k, cols], k == 0, k == KD - 1)
                    if half == 0 and t + 1 < TILES:
                        turn(t + 1)
                last.then_inc(gate_done, 1)
                if t == 0:
                    pe.wait_ge(keep.gate_lo, KD + KE)
                else:
                    pe.wait_ge(e_done, t)
                for half in range(2):
                    cols = slice(half * BANK, (half + 1) * BANK)
                    for k in range(KE):
                        last = split_product(pe, ps[:, 2 + half, :], pT[0][:, t % 2, k, :], pT[1][:, t % 2, k, :],
                                             wp[0][:, k, cols], wp[1][:, k, cols], k == 0, k == KE - 1)
                last.then_inc(ple_done, 1)


INPUTS = ["x", "p", "positions", "w_in", "w_uq", "w_ukv", "w_o", "g_pre_mix", "g_post_mix", "g_q_a", "g_kv_a",
          "g_ret_gn", "w_up", "conv_w", "conv_b", "w_down", "g_pre_ffn", "g_post_ffn", "w_ple", "w_ple_gate",
          "b_ple_gate", "g_post_ple"]


def decoder_layer(nc, io):
    with ExitStack() as ctx:
        def sb(name, shape, dt=F32):
            return ctx.enter_context(nc.sbuf_tensor(name, shape, dt))

        def sem(name):
            return ctx.enter_context(nc.semaphore(name))

        keep = Keep()
        keep.ident = sb("ident", [P, P])[:, :]
        keep.neg = sb("neg", [P, P])[:, :]
        keep.cols = sb("cols", [P, COLS])[:, :]
        keep.neghalf = sb("neghalf", [P, 8])[:, :]
        keep.rstd_lat = sb("rstd_lat", [P, 2, TILES])[:, :, :]
        keep.actHi = sb("actHi", [P, KD, SEQ], F32R)[:, :, :]
        keep.actLo = sb("actLo", [P, KD, SEQ], F32R)[:, :, :]
        hand_base = nc.sbuf_base
        sb("handover", [P, HAND1 + HAND2])

        def hand(name, first, count, dt=F32):
            return nc.alloc_sbuf_tensor_at(name, [P, count], dt, offset=hand_base + 4 * first)[:, :]

        keep.raw_w_in = hand("raw_w_in", 0, HAND1)
        keep.chunk_room = hand("chunk_room", HAND1, HAND2)
        raw_latent = hand("raw_latent", 0, HAND1)
        keep.q1k1 = hand("q1k1", 0, HAND1, F32R)
        keep.wq = hand("wq", HAND1, HAND2, F32R)
        keep.raw_wo = hand("raw_wo", HAND1, HAND2).rearrange("p (s n) -> p s n", s=WO_RING)
        keep.raw_up = hand("raw_up", 0, 2 * D_MODEL).rearrange("p (k z c) -> p k z c", k=KD, z=2)
        keep.up0 = [hand(name, HAND1 + i * 2 * D_MODEL, 2 * D_MODEL, F32R).rearrange("p (k z c) -> p k z c", k=KD, z=2)
                    for i, name in enumerate(("wup0Hi", "wup0Lo"))]
        keep.latent_weights_in = sem("latent_weights_in")
        keep.wo_in = [sem(f"wo_in{i}") for i in range(WO_RING)]
        keep.up_in = sem("up_in")
        keep.up_hi = sem("up_hi")
        keep.up_lo = sem("up_lo")
        keep.raw_gate = hand("raw_gate", 0, HAND1).rearrange("p (s n) -> p s n", s=GATE_RING)
        keep.four_rows = hand("four_rows", HAND1, HAND2).rearrange("p (b n) -> p b n", b=4)
        keep.gate_in = [sem(f"gate_in{i}") for i in range(GATE_RING)]
        keep.gate_hi = sem("gate_hi")
        keep.gate_lo = sem("gate_lo")
        keep.x1_in = [sem("x1_in0"), sem("x1_in1")]
        keep.rows_in = sem("rows_in")
        keep.f_sq = sem("f_sq")
        keep.ps = ctx.enter_context(nc.psum_tensor("banks", [P, 8, BANK], F32))
        with ExitStack() as mixer:
            def mb(name, shape, dt=F32):
                return mixer.enter_context(nc.sbuf_tensor(name, shape, dt))

            keep.sin = mb("rope_sin", [P, TILES, NFREQ])[:, :, :]
            keep.cos = mb("rope_cos", [P, TILES, NFREQ])[:, :, :]
            keep.q_y = mb("q_then_y", [P, TILES, RET_WIDTH])[:, :, :]
            keep.latent = mb("latent", [P, TILES, LATENT])[:, :, :]
            uq_cols = KQ * MLA_HEADS * MLA_QK_DIM
            ukv_cols = MLA_HEADS * (MLA_NOPE_DIM + MLA_V_DIM)
            keep.raw_uq = raw_latent[:, 0:uq_cols].rearrange("p (k n) -> p k n", k=KQ)
            keep.raw_ukv = raw_latent[:, uq_cols:uq_cols + ukv_cols]
            retention_and_projection(nc, io, keep)
            latent_attention(nc, io, keep)
            mix_output(nc, io, keep)
        keep.ffn = sb("ffn_rows", [P, TILES, D_MODEL])[:, :, :]
        conv_ffn(nc, io, keep)
        layer_embedding(nc, io, keep)


def kernel(**inputs):
    import concourse.bacc as bacc
    from concourse.bass_utils import run_bass_kernel_spmd

    nc = bacc.Bacc("TRN2", target_bir_lowering=False, num_devices=1)
    arrays = {name: np.ascontiguousarray(inputs[name]) for name in INPUTS}
    arrays["consts"] = shape_constants()
    drams = {name: nc.dram_tensor(f"in_{name}", a.shape, mybir.dt.from_np(a.dtype), kind="ExternalInput").ap()
             for name, a in arrays.items()}
    out = nc.dram_tensor("out", inputs["x"].shape, F32, kind="ExternalOutput").ap()
    x1 = nc.dram_tensor("x1_scratch", (SEQ, D_MODEL), F32, kind="Internal").ap()
    io = Inputs(out=out, x1=x1, **drams)
    decoder_layer(nc, io)
    r = run_bass_kernel_spmd(nc, [{f"in_{name}": a for name, a in arrays.items()}], core_ids=[0])
    return r.results[0]["out"]
```

```python
from contextlib import ExitStack

import numpy as np

import concourse.bass as bass
from concourse import mybir

P = 128
BANK = 512

D_MODEL = 1024
SEQ = 1024
PLE_DIM = 256
RET_HEADS = 8
RET_HEAD_DIM = 64
RET_WIDTH = RET_HEADS * RET_HEAD_DIM
MLA_HEADS = 8
MLA_NOPE_DIM = 64
MLA_ROPE_DIM = 32
MLA_QK_DIM = MLA_NOPE_DIM + MLA_ROPE_DIM
MLA_V_DIM = 64
MLA_Q_RANK = 256
MLA_KV_RANK = 128
LATENT = MLA_Q_RANK + MLA_KV_RANK + MLA_ROPE_DIM
D_FF = 2816
CONV_WIDTH = 3
ROPE_BASE = 10000.0
EPS = 1e-6

TILES = SEQ // P
KD = D_MODEL // P
PAIRS = RET_HEADS // 2
FF_TILES = D_FF // P
HAND1, HAND2 = 3 * SEQ, 4 * SEQ
WO_RING = 4
WK_COLS = MLA_HEADS * MLA_NOPE_DIM
GATE_RING = 3
GATE_BANKS, UP_BANKS = slice(0, 2), slice(4, 6)
KQ = MLA_Q_RANK // P
HALF = RET_HEAD_DIM // 2
MHALF = MLA_ROPE_DIM // 2
NFREQ = HALF + MHALF
NEG = -3.0e38

F32 = mybir.dt.float32
F32R = mybir.dt.float32r
I32 = mybir.dt.int32
ALU = mybir.AluOpType
ACT = mybir.ActivationFunctionType
AX = mybir.AxisListType.X

COL_W0, COL_W1 = 0, 2 * FF_TILES
COL_Q_A = 4 * FF_TILES
COL_KV_A = COL_Q_A + KQ
COL_RET_GN = COL_KV_A + 1
ROWS_1 = COL_RET_GN + RET_WIDTH // P
COL_W2 = P
COL_BIAS = COL_W2 + 2 * FF_TILES
ROWS_2 = 4 * FF_TILES
COL_POS = 2 * P
COL_PRE_MIX = COL_POS + TILES
COLS = COL_PRE_MIX + KD

C_IDENT = 0
C_NEG = C_IDENT + P
C_FREQ = C_NEG + P
C_BEFORE = C_FREQ + NFREQ
C_KSCALE = C_BEFORE + P
C_INNER = C_KSCALE + RET_HEADS
C_DECAY = C_INNER + RET_HEADS
CONSTS = C_DECAY + PAIRS * P


def shape_constants():
    c = np.zeros((P, CONSTS), np.float32)
    i = np.arange(P, dtype=np.float64)
    c[:, C_IDENT:C_IDENT + P] = np.eye(P)
    c[:, C_NEG:C_NEG + P] = np.where(i[None, :] > i[:, None], NEG, 0.0)
    c[:, C_BEFORE:C_BEFORE + P] = i[None, :] >= i[:, None]
    log_gamma = np.log1p(-np.exp2(-5.0 - np.arange(RET_HEADS)))
    c[:, C_KSCALE:C_KSCALE + RET_HEADS] = np.exp(-log_gamma[None, :] * (i[:, None] + 1)) * RET_HEAD_DIM ** -0.5
    c[:, C_INNER:C_INNER + RET_HEADS] = np.exp(log_gamma[None, :] * (i[:, None] + 1))
    same = (np.arange(P)[:, None] // RET_HEAD_DIM) == (np.arange(P)[None, :] // RET_HEAD_DIM)
    for pair in range(PAIRS):
        head = 2 * pair + np.arange(P) // RET_HEAD_DIM
        c[:, C_DECAY + pair * P:C_DECAY + (pair + 1) * P] = same * np.exp(log_gamma[head] * P)[:, None]
    ret = (ROPE_BASE ** (-np.arange(0, RET_HEAD_DIM, 2) / RET_HEAD_DIM)).astype(np.float32)
    mla = (ROPE_BASE ** (-np.arange(0, MLA_ROPE_DIM, 2) / MLA_ROPE_DIM)).astype(np.float32)
    c[:, C_FREQ:C_FREQ + NFREQ] = np.concatenate([ret, mla])[None, :]
    return c


def two_pi_pieces():
    rest, out = 2 * np.pi, []
    for _ in range(3):
        scale = 2.0 ** (np.floor(np.log2(rest)) - 7)
        piece = np.floor(rest / scale) * scale
        out.append(float(piece))
        rest -= piece
    return out + [float(np.float32(rest))]


def pt_columns():
    offsets = [j * BANK for j in range(5)] + [5 * BANK, 5 * BANK + 384, 5 * BANK + 768]
    return offsets, offsets[-1] + P


def query_key_pieces(keep):
    pieces = []
    for k in range(KQ):
        gain = keep.cols[:, COL_Q_A + k:COL_Q_A + k + 1]
        for dst, src, width in ((0, 0, MLA_QK_DIM), (MLA_QK_DIM, MLA_QK_DIM - MHALF, MHALF), (MLA_QK_DIM + MHALF, MLA_NOPE_DIM, MHALF)):
            pieces.append((keep.wq_parts[0][:, k, :, dst:dst + width], keep.wq_parts[1][:, k, :, dst:dst + width],
                           keep.raw_uq[:, k, :, src:src + width], gain))
    pieces.append((keep.wk[0], keep.wk[1], keep.raw_ukv[:, :, 0:MLA_NOPE_DIM], keep.cols[:, COL_KV_A:COL_KV_A + 1]))
    return pieces


class Inputs:

    def __init__(self, x, p, positions, w_in, w_uq, w_ukv, w_o, g_pre_mix, g_post_mix, g_q_a, g_kv_a, g_ret_gn, w_up,
                 conv_w, conv_b, w_down, g_pre_ffn, g_post_ffn, w_ple, w_ple_gate, b_ple_gate, g_post_ple, consts, out, x1):
        self.x, self.p, self.positions, self.consts, self.out, self.x1 = x, p, positions, consts, out, x1
        self.w_in, self.w_uq, self.w_ukv, self.w_o = w_in, w_uq, w_ukv, w_o
        self.w_up, self.conv_w, self.conv_b, self.w_down = w_up, conv_w, conv_b, w_down
        self.w_ple, self.w_ple_gate, self.b_ple_gate = w_ple, w_ple_gate, b_ple_gate
        self.g_pre_mix, self.g_post_mix, self.g_q_a, self.g_kv_a = g_pre_mix, g_post_mix, g_q_a, g_kv_a
        self.g_ret_gn, self.g_pre_ffn, self.g_post_ffn, self.g_post_ple = g_ret_gn, g_pre_ffn, g_post_ffn, g_post_ple


class Keep:
    pass


class Own:

    def __init__(self, eng, sem):
        self.eng, self.sem, self.n = eng, sem, 0

    def __call__(self, ins):
        self.n += 1
        ins.then_inc(self.sem, 1)
        self.eng.wait_ge(self.sem, self.n)


def split_product(eng, out, hi, lo, whi, wlo, first, last):
    eng.matmul(out, hi, whi, start=first, stop=False)
    eng.matmul(out, hi, wlo, start=False, stop=False)
    return eng.matmul(out, lo, whi, start=False, stop=last)


def retention_and_projection(nc, io, keep):
    groups = [("q", 0, 512), ("k", 512, 512), ("v", 1024, 512), ("latent", 4 * RET_WIDTH, LATENT), ("gate", 3 * RET_WIDTH, 512)]
    SLOTS = len(groups) * TILES
    SLICES = len(groups) * KD
    RAW = 4
    RING = 9
    RET0 = 3 * TILES

    with ExitStack() as ctx:
        def sb(name, shape, dt=F32):
            return ctx.enter_context(nc.sbuf_tensor(name, shape, dt))

        def sem(name):
            return ctx.enter_context(nc.semaphore(name))

        kret = sb("kret", [P, TILES, RET_WIDTH])
        vret = sb("vret", [P, TILES, RET_WIDTH])
        wraw = keep.raw_w_in[:, 0:RAW * 512].rearrange("p (s n) -> p s n", s=RAW)
        wHi = sb("wHi", [P, RING, 512], F32R)
        wLo = sb("wLo", [P, RING, 512], F32R)
        scratch = keep.chunk_room.rearrange("p (s n) -> p s n", s=8)
        mrope = sb("mrope", [P, 2, 2, 512])
        rows1, rows2, first_rows = (keep.raw_w_in[:, RAW * 512 + i * P:RAW * 512 + (i + 1) * P] for i in range(3))
        posi = sb("posi", [TILES, P], I32)
        small = sb("small", [P, 8, 8])
        junk = sb("junkA", [P, MLA_Q_RANK + MLA_KV_RANK])
        ctab = sb("ctab", [P, CONSTS - C_FREQ])
        ps = keep.ps

        xt = scratch[:, 0:4, :].rearrange("p (b h) n -> p b (h n)", b=2)
        ht = scratch[:, 4:8, :].rearrange("p (b h) n -> p b (h n)", b=2)
        q_zero = scratch[:, 0:2, :].rearrange("p a n -> p (a n)").rearrange("p (r z c) -> p r z c", r=PAIRS, z=2)
        kT = scratch[:, 2, :].rearrange("p (r c) -> p r c", r=PAIRS)
        qT = scratch[:, 3:5, :].rearrange("p b (r c) -> p b r c", r=PAIRS)
        sT = scratch[:, 5:7, :].rearrange("p a n -> p (a n)").rearrange("p (h c) -> p h c", h=RET_HEADS)
        state = scratch[:, 7, :]
        orow = mrope[:, 0, 0, :]
        osq = mrope[:, 0, 1, :]
        gate = mrope[:, 1, :, :]
        NA = TILES * NFREQ
        angle = mrope[:, 0, 0, 0:NA]
        turns = mrope[:, 0, 1, 0:NA]
        cosin = mrope[:, 1, 0, 0:NA]

        def const(col, n):
            return ctab[:, col - C_FREQ:col - C_FREQ + n]

        ident = keep.ident
        ssx = small[:, 0, :]
        rstdx = small[:, 1, :]
        neghalf = keep.neghalf
        meanv = small[:, 3, :]
        varv = small[:, 4, :]
        rstdo = small[:, 5, :]
        scr8 = small[:, 6, :]

        first_in = sem("first_in")
        small_in = sem("small_in")
        x_in = [sem("x_in0"), sem("x_in1")]
        raw_in = [sem(f"raw_in{i}") for i in range(RAW)]
        w_hi = sem("w_hi")
        w_lo = sem("w_lo")
        slice_used = sem("slice_used")
        sq_done = sem("sq_done")
        rstd_done = sem("rstd_done")
        h_done = sem("h_done")
        turned = sem("turned")
        hT_hi = sem("hT_hi")
        hT_lo = sem("hT_lo")
        z_ready = sem("z_ready")
        z_dve = sem("z_used_dve")
        z_act = sem("z_used_act")
        rope_out = sem("rope_out")
        setup_turned = sem("setup_turned")
        columns_ready = sem("columns_ready")
        trig_arg = sem("trig_arg")
        trig_done = sem("trig_done")
        dve_own = sem("dve_ownA")
        act_own = sem("act_ownA")
        pool_own = sem("pool_ownA")
        zeros_done = sem("zeros_done")
        qk_turned = sem("qk_turned")
        kT_copied = sem("kT_copied")
        qT_copied = sem("qT_copied")
        qz_copied = sem("qz_copied")
        scores_done = sem("scores_done")
        masked = sem("masked")
        out_done = sem("out_done")
        kv_done = sem("kv_done")
        state_done = sem("state_done")
        out_read = sem("out_read")
        mean_sub = sem("mean_sub")
        osq_done = sem("osq_done")
        var_done = sem("var_done")
        ornorm = sem("rstd_head")
        gate_done = sem("gate_done")
        y_done = sem("y_done")
        y_gated = sem("y_gated")

        w3 = io.w_in[0].rearrange("(k p) n -> p k n", p=P)
        xr = io.x[0].rearrange("(t p) d -> t p d", p=P)

        POOL_LATENT = 1 + 3 * TILES + 4
        LATENT0 = RET0 + TILES + 2
        KEY_AT = 3
        latent_pieces = query_key_pieces(keep)
        block = ctx.enter_context(nc.Block())

        @block.sync
        def _(sp):
            def load_x(t):
                if t >= 2:
                    sp.wait_ge(h_done, t - 1)
                sp.dma_start(xt[:, t % 2, :], xr[t]).then_inc(x_in[t % 2], 16)

            def load_w(s):
                name, col, width = groups[s // KD]
                if s >= RAW:
                    sp.wait_ge(w_lo, s - RAW + 1)
                sp.dma_start(wraw[:, s % RAW, 0:width], w3[:, s % KD, col:col + width]).then_inc(raw_in[s % RAW], 16)

            sp.dma_start(posi[:, :], io.positions.rearrange("b (t p) -> (b t) p", p=P)).then_inc(first_in, 16)
            sp.dma_start(first_rows[TILES:TILES + KD, :], io.g_pre_mix.rearrange("a (j p) -> (a j) p", p=P)).then_inc(first_in, 16)
            sp.dma_start(ident, io.consts[:, C_IDENT:C_IDENT + P]).then_inc(first_in, 16)
            load_x(0)
            sp.dma_start(const(C_FREQ, NFREQ), io.consts[:, C_FREQ:C_FREQ + NFREQ]).then_inc(first_in, 16)
            for s in range(2):
                load_w(s)
            load_x(1)
            for s in range(2, RAW):
                load_w(s)
            cw = io.conv_w[0].rearrange("w (j p) -> (w j) p", p=P)
            F2 = 2 * FF_TILES
            pieces = [(rows1, COL_W0, cw[0:2 * F2]), (rows1, COL_Q_A, io.g_q_a.rearrange("a (j p) -> (a j) p", p=P)),
                      (rows1, COL_KV_A, io.g_kv_a.rearrange("a (j p) -> (a j) p", p=P)),
                      (rows1, COL_RET_GN, io.g_ret_gn.rearrange("a (j p) -> (a j) p", p=P)),
                      (rows2, 0, cw[2 * F2:3 * F2]), (rows2, F2, io.conv_b.rearrange("a (j p) -> (a j) p", p=P))]
            for tile, row, src in pieces:
                sp.dma_start(tile[row:row + src.shape[0], :], src).then_inc(small_in, 16)
            for s in range(RAW, KD):
                load_w(s)
            sp.dma_start(const(C_BEFORE, CONSTS - C_BEFORE), io.consts[:, C_BEFORE:CONSTS]).then_inc(small_in, 16)
            sp.dma_start(keep.neg, io.consts[:, C_NEG:C_NEG + P]).then_inc(small_in, 16)
            for t in range(2, TILES):
                load_x(t)
            for s in range(KD, SLICES):
                load_w(s)
            sp.wait_ge(w_lo, SLICES)
            sp.dma_start(keep.raw_uq, io.w_uq[0].rearrange("(k p) (h n) -> p k h n", p=P, h=MLA_HEADS)).then_inc(keep.latent_weights_in, 16)
            sp.dma_start(keep.raw_ukv, io.w_ukv[0].rearrange("p (h n) -> p h n", h=MLA_HEADS)).then_inc(keep.latent_weights_in, 16)

        def slices_before(n, after):
            gi, t = divmod(n, TILES)
            if gi + 1 >= len(groups):
                return []
            spare = RING - KD
            if t == 1 and not after:
                return [(gi + 1) * KD + k for k in range(spare)]
            if t == TILES - 1 and not after:
                return [(gi + 1) * KD + k for k in range(spare, KD)]
            return []

        @block.gpsimd
        def _(pool):
            own = Own(pool, pool_own)
            own(pool.memset(neghalf, -0.5))

            def rope_rows(n):
                t = n % TILES
                rows = keep.q_y if n < TILES else kret
                dst = rows[:, t, :].rearrange("p (h z d) -> p h z d", h=RET_HEADS, z=2)
                cs = mrope[:, n % 2, 0, :].rearrange("p (h z d) -> p h z d", h=RET_HEADS, z=2)
                sn = mrope[:, n % 2, 1, :].rearrange("p (h z d) -> p h z d", h=RET_HEADS, z=2)
                pool.wait_ge(z_dve, n + 1)
                pool.tensor_tensor(dst[:, :, 0, :], cs[:, :, 0, :], sn[:, :, 1, :], ALU.subtract).then_inc(rope_out, 1)
                pool.tensor_tensor(dst[:, :, 1, :], cs[:, :, 1, :], sn[:, :, 0, :], ALU.add).then_inc(rope_out, 1)

            for t in range(TILES):
                pool.wait_ge(sq_done, t + 1)
                own(pool.tensor_scalar(scr8[:, t:t + 1], ssx[:, t:t + 1], 1.0 / D_MODEL, EPS, ALU.mult, ALU.add))
                pool.tensor_tensor(rstdx[:, t:t + 1], scr8[:, t:t + 1], neghalf[:, 0:1], ALU.pow).then_inc(rstd_done, 1)
                if t >= 3:
                    rope_rows(t - 3)
            for n in range(TILES - 3, 2 * TILES):
                rope_rows(n)
            pool.wait_ge(rope_out, 4 * TILES)
            for t in range(TILES):
                dst = kret[:, t, :].rearrange("p (h d) -> p h d", h=RET_HEADS)
                own(pool.tensor_tensor(dst, dst, const(C_KSCALE, RET_HEADS).unsqueeze(2).broadcast_to([P, RET_HEADS, RET_HEAD_DIM]), ALU.mult))
                if t == 0:
                    pool.wait_ge(turned, TILES)
                    pool.memset(q_zero[64:128, :, 0, :], 0.0).then_inc(zeros_done, 1)
                    pool.wait_ge(zeros_done, 1)
                    pool.memset(q_zero[0:64, :, 1, :], 0.0).then_inc(zeros_done, 1)
                    pool.wait_ge(zeros_done, 2)
            def rotate_key():
                at = MLA_NOPE_DIM
                pool.wait_ge(out_done, TILES)
                pool.wait_ge(kv_done, TILES - 1)
                own(pool.memset(keep.krow[:, :, 0:at], 0.0))
                kpe = keep.latent[:, :, MLA_Q_RANK + MLA_KV_RANK:LATENT].rearrange("p t (z d) -> p t z d", z=2)
                cs, sn = (keep.krow_products[:, j].rearrange("p t (z d) -> p t z d", z=2) for j in range(2))
                for z in range(2):
                    own(pool.tensor_tensor(cs[:, :, z, :], kpe[:, :, z, :], keep.cos[:, :, HALF:NFREQ], ALU.mult))
                    own(pool.tensor_tensor(sn[:, :, z, :], kpe[:, :, z, :], keep.sin[:, :, HALF:NFREQ], ALU.mult))
                for copy in range(2):
                    own(pool.tensor_tensor(keep.krow[:, :, at:at + MHALF], cs[:, :, 0, :], sn[:, :, 1, :], ALU.subtract))
                    own(pool.tensor_tensor(keep.krow[:, :, at + MHALF:at + 2 * MHALF], cs[:, :, 1, :], sn[:, :, 0, :], ALU.add))
                    at += MLA_ROPE_DIM

            def gate_rows(c):
                y = keep.q_y[:, c, :]
                pool.wait_ge(gate_done, c + 1)
                pool.wait_ge(y_done, c + 1)
                pool.tensor_tensor(y, y, gate[:, c % 2, :], ALU.mult).then_inc(y_gated, 1)

            for c in range(TILES):
                if c == TILES - 1:
                    gate_rows(0)
                pool.wait_ge(var_done, c + 1)
                own(pool.tensor_scalar(varv, varv, 1.0 / RET_HEAD_DIM, EPS, ALU.mult, ALU.add))
                pool.tensor_tensor(rstdo, varv, neghalf, ALU.pow).then_inc(ornorm, 1)
            pool.wait_ge(z_act, 2 * TILES)
            for part, width in enumerate((MLA_Q_RANK, MLA_KV_RANK)):
                lat = keep.rstd_lat[:, part, :]
                own(pool.tensor_scalar(lat, lat, 1.0 / width, EPS, ALU.mult, ALU.add))
                own(pool.tensor_tensor(lat, lat, neghalf, ALU.pow))
            for c in range(1, TILES):
                gate_rows(c)
                if c == KEY_AT:
                    rotate_key()

        @block.scalar
        def _(act):
            own = Own(act, act_own)

            def split_hi(s):
                gi, k = divmod(s, KD)
                width = groups[gi][2]
                act.wait_ge(raw_in[s % RAW], 16 * (s // RAW + 1))
                if s == 0:
                    act.wait_ge(columns_ready, 2)
                if s >= RING:
                    before, kb = divmod(s - RING, KD)
                    if kb == KD - 1:
                        act.wait_ge(z_ready, (before + 1) * TILES)
                    else:
                        act.wait_ge(slice_used, before * (KD - 1) + kb + 1)
                act.activation(wHi[:, s % RING, 0:width], wraw[:, s % RAW, 0:width], ACT.Identity,
                               scale=keep.cols[:, COL_PRE_MIX + k:COL_PRE_MIX + k + 1]).then_inc(w_hi, 1)

            def hT_hi_part(t):
                act.wait_ge(turned, t + 1)
                bank = 2 + 2 * (t % 2)
                act.activation(keep.actHi[:, :, t * P:(t + 1) * P],
                               ps[:, bank:bank + 2, :].rearrange("p a (b c) -> p (a b) c", c=P), ACT.Copy).then_inc(hT_hi, 1)

            for t in range(TILES):
                act.wait_ge(x_in[t % 2], 16 * (t // 2 + 1))
                if t >= 2:
                    act.wait_ge(turned, t - 1)
                act.activation(ht[:, t % 2, :], xt[:, t % 2, :], ACT.Square, accum_out=ssx[:, t:t + 1]).then_inc(sq_done, 1)
                if t == 1:
                    hT_hi_part(0)
                if t < 2:
                    for s in range(4 * t, 4 * t + 4):
                        split_hi(s)
                if t >= 2:
                    hT_hi_part(t - 1)
                if t == 1:
                    act.wait_ge(trig_arg, 2)
                    act.activation(keep.sin, angle.rearrange("p (t f) -> p t f", t=TILES), ACT.Sin).then_inc(trig_done, 1)
                    act.activation(keep.cos, cosin.rearrange("p (t f) -> p t f", t=TILES), ACT.Sin, scale=-1.0).then_inc(trig_done, 1)
            hT_hi_part(TILES - 1)
            for s in slices_before(1, False) + slices_before(TILES - 1, False):
                split_hi(s)
            for n in range(TILES, SLOTS + 2):
                if n < SLOTS:
                    gi, t = divmod(n, TILES)
                    for s in slices_before(n, False):
                        split_hi(s)
                    name, col, width = groups[gi]
                    if gi >= 2:
                        act.wait_ge(z_ready, n + 1)
                        z = ps[:, n % 2, 0:width]
                        if name == "v":
                            act.activation(vret[:, t, :], z, ACT.Copy).then_inc(z_act, 1)
                        elif name == "latent":
                            own(act.activation(keep.latent[:, t, :], z, ACT.Copy))
                            own(act.activation(junk[:, 0:MLA_Q_RANK], z[:, 0:MLA_Q_RANK], ACT.Square,
                                               accum_out=keep.rstd_lat[:, 0, t:t + 1]))
                            act.activation(junk[:, MLA_Q_RANK:MLA_Q_RANK + MLA_KV_RANK], z[:, MLA_Q_RANK:MLA_Q_RANK + MLA_KV_RANK],
                                           ACT.Square, accum_out=keep.rstd_lat[:, 1, t:t + 1]).then_inc(z_act, 1)
                            act.wait_ge(z_act, n + 1 - 2 * TILES)
                        else:
                            if t >= 2:
                                act.wait_ge(y_gated, t - 1)
                            else:
                                act.wait_ge(rope_out, 4 * TILES)
                            act.activation(gate[:, t % 2, :], z, ACT.Silu).then_inc(gate_done, 1)
                c = n - RET0
                if 0 <= c < TILES:
                    act.wait_ge(qk_turned, c + 1)
                    if c >= 1:
                        act.wait_ge(scores_done, c)
                    act.activation(kT, ps[:, 3, :].rearrange("p (r c) -> p r c", r=PAIRS), ACT.Copy).then_inc(kT_copied, 1)
                    if c >= 2:
                        act.wait_ge(out_done, c - 1)
                    act.activation(qT[:, c % 2], ps[:, 2, :].rearrange("p (r c) -> p r c", r=PAIRS), ACT.Copy).then_inc(qT_copied, 1)
                c = n - RET0 - 2
                if 0 <= c < TILES:
                    act.wait_ge(mean_sub, c + 1)
                    act.activation(osq, orow, ACT.Square).then_inc(osq_done, 1)
                if n == LATENT0:
                    act.wait_ge(y_done, TILES)
                    act.wait_ge(out_done, TILES)
                    act.wait_ge(keep.latent_weights_in, 32)
                    act.wait_ge(pool_own, POOL_LATENT)
                    for t in range(TILES):
                        row = keep.latent[:, t, MLA_Q_RANK:MLA_Q_RANK + MLA_KV_RANK]
                        own(act.activation(row, row, ACT.Copy, scale=keep.rstd_lat[:, 1, t:t + 1]))
                if 0 <= n - LATENT0 < len(latent_pieces):
                    hi, lo, src, gain = latent_pieces[n - LATENT0]
                    act.activation(hi, src, ACT.Identity, scale=gain).then_inc(w_hi, 1)

        @block.vector
        def _(dve):
            own = Own(dve, dve_own)
            dve.wait_ge(first_in, 16 * 4)
            dve.tensor_copy(first_rows[0:TILES, :], posi[:, :]).then_inc(columns_ready, 1)
            dve.wait_ge(setup_turned, 1)
            dve.tensor_copy(keep.cols[:, COL_POS:COLS], ps[:, 6, COL_POS:COLS]).then_inc(columns_ready, 1)
            dve.wait_ge(columns_ready, 2)

            def other_columns():
                dve.wait_ge(small_in, 16 * 8)
                dve.wait_ge(setup_turned, 2)
                own(dve.tensor_copy(keep.cols[:, 0:ROWS_1], ps[:, 6, 0:ROWS_1]))
                own(dve.tensor_scalar(keep.cols[:, COL_Q_A:COL_Q_A + KQ], keep.cols[:, COL_Q_A:COL_Q_A + KQ], MLA_QK_DIM ** -0.5, None, ALU.mult))
                own(dve.tensor_copy(keep.cols[:, COL_W2:COL_W2 + ROWS_2], ps[:, 6, COL_W2:COL_W2 + ROWS_2]))

            def split_lo(s):
                gi, k = divmod(s, KD)
                width = groups[gi][2]
                dve.wait_ge(w_hi, s + 1)
                dve.scalar_tensor_tensor(wLo[:, s % RING, 0:width], wraw[:, s % RAW, 0:width],
                                         keep.cols[:, COL_PRE_MIX + k:COL_PRE_MIX + k + 1],
                                         wHi[:, s % RING, 0:width].bitcast(F32), ALU.mult, ALU.subtract).then_inc(w_lo, 1)

            def norm_x(t):
                dve.wait_ge(rstd_done, t + 1)
                dve.tensor_scalar(ht[:, t % 2, :], xt[:, t % 2, :], rstdx[:, t:t + 1], None, ALU.mult).then_inc(h_done, 1)

            def hT_lo_part(t):
                dve.wait_ge(hT_hi, t + 1)
                bank = 2 + 2 * (t % 2)
                dve.tensor_tensor(keep.actLo[:, :, t * P:(t + 1) * P],
                                  ps[:, bank:bank + 2, :].rearrange("p a (b c) -> p (a b) c", c=P),
                                  keep.actHi[:, :, t * P:(t + 1) * P].bitcast(F32), ALU.subtract).then_inc(hT_lo, 1)

            def rope(n):
                t = n % TILES
                z = ps[:, n % 2, :].rearrange("p (g d) -> p g d", d=HALF)
                dve.wait_ge(z_ready, n + 1)
                if n == 0:
                    dve.wait_ge(trig_done, 2)
                if n >= 2:
                    dve.wait_ge(rope_out, 2 * (n - 1))
                cs = mrope[:, n % 2, 0, :].rearrange("p (g d) -> p g d", d=HALF)
                sn = mrope[:, n % 2, 1, :].rearrange("p (g d) -> p g d", d=HALF)
                own(dve.tensor_tensor(cs, z, keep.cos[:, t, 0:HALF].unsqueeze(1).broadcast_to([P, 2 * RET_HEADS, HALF]), ALU.mult))
                dve.tensor_tensor(sn, z, keep.sin[:, t, 0:HALF].unsqueeze(1).broadcast_to([P, 2 * RET_HEADS, HALF]),
                                  ALU.mult).then_inc(z_dve, 1)

            def zero_padded_q(c):
                dve.wait_ge(qk_turned, c + 1)
                if c == 0:
                    dve.wait_ge(zeros_done, 2)
                if c >= 1:
                    dve.wait_ge(scores_done, c)
                src = ps[:, 2, :].rearrange("p (r c) -> p r c", r=PAIRS)
                dve.wait_ge(qT_copied, c + 1)
                dve.tensor_copy(q_zero[0:64, :, 0, :], src[0:64]).then_inc(qz_copied, 1)
                dve.tensor_copy(q_zero[64:128, :, 1, :], src[64:128]).then_inc(qz_copied, 1)

            def mask_scores(c):
                dve.wait_ge(scores_done, c + 1)
                src = ps[:, 4:6, :].rearrange("p a (h c) -> p (a h) c", c=P)
                dve.tensor_tensor(sT, src, const(C_BEFORE, P).unsqueeze(1).broadcast_to([P, RET_HEADS, P]),
                                  ALU.mult).then_inc(masked, 1)

            def heads(ap):
                return ap.rearrange("p (h d) -> p h d", h=RET_HEADS)

            def each_head(ap):
                return ap.unsqueeze(2).broadcast_to([P, RET_HEADS, RET_HEAD_DIM])

            def prepare_latent():
                dve.wait_ge(pool_own, POOL_LATENT)
                for t in range(TILES):
                    row = keep.latent[:, t, 0:MLA_Q_RANK]
                    own(dve.tensor_scalar(row, row, keep.rstd_lat[:, 0, t:t + 1], None, ALU.mult))
                own(dve.memset(keep.trow[:, :, 0:MLA_NOPE_DIM], 1.0))
                sin, cos = keep.sin[:, :, HALF:NFREQ], keep.cos[:, :, HALF:NFREQ]
                for i, (src, sign) in enumerate(((cos, 1.0), (cos, 1.0), (sin, -1.0), (sin, 1.0))):
                    at = MLA_NOPE_DIM + i * MHALF
                    own(dve.tensor_scalar(keep.trow[:, :, at:at + MHALF], src, sign, None, ALU.mult))

            def take_output(c):
                dve.wait_ge(out_done, c + 1)
                dve.wait_ge(rope_out, 4 * TILES)
                if c >= 1:
                    dve.wait_ge(osq_done, c)
                dve.tensor_tensor(heads(orow), heads(ps[:, 7, :]), each_head(const(C_INNER, RET_HEADS)), ALU.mult).then_inc(out_read, 1)
                if c < TILES - 1:
                    dve.wait_ge(kv_done, c + 1)
                    if c > 0:
                        own(dve.tensor_tensor(state, ps[:, 6, :], state, ALU.add))
                        dve.tensor_tensor(state, state, const(C_DECAY, PAIRS * P), ALU.mult).then_inc(state_done, 1)
                    else:
                        dve.tensor_tensor(state, ps[:, 6, :], const(C_DECAY, PAIRS * P), ALU.mult).then_inc(state_done, 1)

            def subtract_mean(c):
                dve.wait_ge(out_read, c + 1)
                own(dve.tensor_reduce(meanv, heads(orow), AX, ALU.add))
                own(dve.tensor_scalar(meanv, meanv, 1.0 / RET_HEAD_DIM, None, ALU.mult))
                dve.tensor_tensor(heads(orow), heads(orow), each_head(meanv), ALU.subtract).then_inc(mean_sub, 1)

            def norm_heads(c):
                dve.wait_ge(osq_done, c + 1)
                if c >= 1:
                    dve.wait_ge(ornorm, c)
                dve.tensor_reduce(varv, heads(osq), AX, ALU.add).then_inc(var_done, 1)
                dve.wait_ge(ornorm, c + 1)
                dve.tensor_tensor(heads(keep.q_y[:, c, :]), heads(orow), each_head(rstdo), ALU.mult).then_inc(y_done, 1)
                dve.wait_ge(y_done, c + 1)

            def multiply_angles():
                a3 = angle.rearrange("p (t f) -> p t f", t=TILES)
                own(dve.tensor_tensor(a3, keep.cols[:, COL_POS:COL_PRE_MIX].unsqueeze(2).broadcast_to([P, TILES, NFREQ]),
                                      const(C_FREQ, NFREQ).unsqueeze(1).broadcast_to([P, TILES, NFREQ]), ALU.mult))

            def reduce_angles(unit):
                magic = 1.5 * 2.0 ** 23
                own(dve.tensor_scalar(turns, angle, 1.0 / (2 * np.pi * unit), magic, ALU.mult, ALU.add))
                own(dve.tensor_scalar(turns, turns, -magic, unit, ALU.add, ALU.mult))
                for piece in two_pi_pieces():
                    own(dve.scalar_tensor_tensor(angle, turns, -piece, angle, ALU.mult, ALU.add))

            def fold_angles():
                pi_below = 3.1415925
                dve.tensor_scalar(angle, angle, pi_below, -pi_below, ALU.min, ALU.max).then_inc(trig_arg, 1)
                dve.wait_ge(trig_arg, 1)
                own(dve.scalar_tensor_tensor(turns, angle, -1.0, angle, ALU.mult, ALU.max))
                dve.tensor_scalar(cosin, turns, -float(np.pi / 2), None, ALU.add).then_inc(trig_arg, 1)

            multiply_angles()
            reduce_angles(4096.0)
            norm_x(0)
            for s in range(4):
                split_lo(s)
            for t in range(1, TILES):
                norm_x(t)
                hT_lo_part(t - 1)
                if t == 1:
                    reduce_angles(1.0)
                    fold_angles()
                    for s in range(4, KD):
                        split_lo(s)
                if t == 2:
                    other_columns()
                if t >= 2:
                    rope(t - 2)
            hT_lo_part(TILES - 1)
            rope(TILES - 2)
            for s in slices_before(1, False) + slices_before(TILES - 1, False):
                split_lo(s)
            rope(TILES - 1)
            for n in range(TILES, SLOTS + 2):
                if n < SLOTS:
                    for s in slices_before(n, False):
                        split_lo(s)
                    if n < 2 * TILES:
                        rope(n)
                c = n - RET0 - 2
                if 0 <= c < TILES:
                    take_output(c)
                if 0 <= c + 1 < TILES:
                    mask_scores(c + 1)
                if 0 <= c < TILES:
                    subtract_mean(c)
                if 0 <= c + 2 < TILES:
                    zero_padded_q(c + 2)
                if 0 <= c < TILES:
                    norm_heads(c)
                if n == LATENT0:
                    prepare_latent()
                if 0 <= n - LATENT0 < len(latent_pieces):
                    hi, lo, src, gain = latent_pieces[n - LATENT0]
                    dve.wait_ge(w_hi, SLICES + n - LATENT0 + 1)
                    dve.scalar_tensor_tensor(lo, src, gain, hi.bitcast(F32), ALU.mult, ALU.subtract).then_inc(w_lo, 1)

        @block.tensor
        def _(pe):
            pe.wait_ge(first_in, 16 * 4)
            pe.wait_ge(columns_ready, 1)
            pe.transpose(ps[:, 6, COL_POS:COLS], first_rows[0:TILES + KD, :], ident[0:TILES + KD, 0:TILES + KD]).then_inc(setup_turned, 1)

            def turn_small_vectors():
                pe.wait_ge(small_in, 16 * 8)
                pe.transpose(ps[:, 6, 0:ROWS_1], rows1[0:ROWS_1, :], ident[0:ROWS_1, 0:ROWS_1])
                pe.transpose(ps[:, 6, COL_W2:COL_W2 + ROWS_2], rows2[0:ROWS_2, :], ident[0:ROWS_2, 0:ROWS_2]).then_inc(setup_turned, 1)

            def turn_x(t):
                pe.wait_ge(h_done, t + 1)
                if t >= 2:
                    pe.wait_ge(hT_lo, t - 1)
                bank = 2 + 2 * (t % 2)
                for k in range(KD):
                    last = pe.transpose(ps[:, bank + k // 4, (k % 4) * P:(k % 4 + 1) * P], ht[:, t % 2, k * P:(k + 1) * P], ident)
                last.then_inc(turned, 1)

            def product(n):
                gi, t = divmod(n, TILES)
                width = groups[gi][2]
                if gi == 0:
                    pe.wait_ge(hT_lo, t + 1)
                if n >= 2:
                    if n - 2 < 2 * TILES:
                        pe.wait_ge(z_dve, n - 1)
                    elif n - 2 < 4 * TILES:
                        pe.wait_ge(z_act, n - 1 - 2 * TILES)
                    else:
                        pe.wait_ge(gate_done, n - 1 - 4 * TILES)
                for k in range(KD):
                    s = gi * KD + k
                    if t == 0:
                        pe.wait_ge(w_lo, s + 1)
                    last = split_product(pe, ps[:, n % 2, 0:width],
                                         keep.actHi[:, k, t * P:(t + 1) * P], keep.actLo[:, k, t * P:(t + 1) * P],
                                         wHi[:, s % RING, 0:width], wLo[:, s % RING, 0:width], k == 0, k == KD - 1)
                    if t == TILES - 1 and k < KD - 1:
                        last.then_inc(slice_used, 1)
                last.then_inc(z_ready, 1)

            def turn_chunk(c):
                if c == 0:
                    pe.wait_ge(pool_own, 1 + TILES + 1)
                    pe.wait_ge(hT_lo, TILES)
                else:
                    pe.wait_ge(pool_own, 1 + TILES + 1 + c)
                    pe.wait_ge(kT_copied, c)
                    pe.wait_ge(qz_copied, 2 * c)
                for pair in range(PAIRS):
                    pe.transpose(ps[:, 2, pair * P:(pair + 1) * P], keep.q_y[:, c, pair * P:(pair + 1) * P], ident)
                for pair in range(PAIRS):
                    last = pe.transpose(ps[:, 3, pair * P:(pair + 1) * P], kret[:, c, pair * P:(pair + 1) * P], ident)
                last.then_inc(qk_turned, 1)

            def score_chunk(c):
                pe.wait_ge(kT_copied, c + 1)
                pe.wait_ge(qz_copied, 2 * c + 2)
                if c >= 1:
                    pe.wait_ge(masked, c)
                for pair in range(PAIRS):
                    last = pe.matmul(ps[:, 4 + pair // 2, (pair % 2) * 256:(pair % 2 + 1) * 256], kT[:, pair, :],
                                     q_zero[:, pair, :, :], start=True, stop=True)
                last.then_inc(scores_done, 1)

            def finish_chunk(c):
                pe.wait_ge(masked, c + 1)
                if c >= 1:
                    pe.wait_ge(state_done, c)
                    pe.wait_ge(out_read, c)
                else:
                    pe.wait_ge(z_act, TILES)
                for pair in range(PAIRS):
                    cols = slice(pair * P, (pair + 1) * P)
                    if c >= 1:
                        pe.matmul(ps[:, 7, cols], qT[:, c % 2, pair, :], state[:, cols], start=True, stop=False, skip_group_check=True)
                    for z in range(2):
                        h = 2 * pair + z
                        hc = slice(h * RET_HEAD_DIM, (h + 1) * RET_HEAD_DIM)
                        last = pe.matmul(ps[:, 7, hc], sT[:, h, :], vret[:, c, hc], start=(c == 0), stop=True,
                                         skip_group_check=True)
                last.then_inc(out_done, 1)
                if c < TILES - 1:
                    for pair in range(PAIRS):
                        cols = slice(pair * P, (pair + 1) * P)
                        last = pe.matmul(ps[:, 6, cols], kret[:, c, cols], vret[:, c, cols], start=True, stop=True)
                    last.then_inc(kv_done, 1)

            turn_x(0)
            turn_x(1)
            for n in range(SLOTS + 2):
                if n < SLOTS:
                    product(n)
                if n == 0:
                    turn_small_vectors()
                if 2 <= n + 2 < TILES:
                    turn_x(n + 2)
                if 0 <= n - RET0 - 2 < TILES:
                    finish_chunk(n - RET0 - 2)
                if 0 <= n - RET0 - 1 < TILES:
                    score_chunk(n - RET0 - 1)
                if 0 <= n - RET0 < TILES:
                    turn_chunk(n - RET0)


def latent_attention(nc, io, keep):
    BLOCK_ROWS = 4
    STEPS = MLA_HEADS * TILES
    FULL_RATE = 2 * P
    LAG = 3
    ROT = MLA_NOPE_DIM
    PT_OFF, PT_COLS = pt_columns()

    def groups_of(m):
        i = m % TILES
        if i < BLOCK_ROWS:
            return [(0, [(0, i + 1)])]
        tail = [(4, 1)] + ([(5, i - 4)] if i > 4 else [])
        return [(0, [(0, 4)]), (4, tail)]

    def pt_view(buf, m, first, count):
        i = m % TILES
        if i < BLOCK_ROWS:
            start, step = i * P, BANK - P
        elif first == 0:
            start, step = (i - BLOCK_ROWS) * P, BANK
        elif first == 4:
            start, step = PT_OFF[4] + (i - 4) * P, P
        else:
            start, step = PT_OFF[5] + (i - 5) * P, PT_OFF[6] - PT_OFF[5] - P
        if count == 1:
            return buf[:, start:start + P].unsqueeze(1)
        return bass_view(buf, start, step, count)

    def bass_view(buf, start, step, count):
        width = count * step
        if start + width <= buf.shape[1]:
            return buf[:, start:start + width].rearrange("p (j s) -> p j s", s=step)[:, :, 0:P]
        lead = start + width - buf.shape[1]
        return buf[:, start - lead:start - lead + width].rearrange("p (j s) -> p j s", s=step)[:, :, lead:lead + P]

    ROW_AT = [21, 15, 8, 0, 21, 15, 8, 0]
    ROWS = 4

    bank_of = {}
    for m in range(STEPS):
        for b, _ in groups_of(m):
            bank_of[(m, b)] = len(bank_of)
    through = [max(v for (mm, _), v in bank_of.items() if mm == m) + 1 for m in range(STEPS)]

    with ExitStack() as ctx:
        def sb(name, shape, dt=F32):
            return ctx.enter_context(nc.sbuf_tensor(name, shape, dt))

        def sem(name):
            return ctx.enter_context(nc.semaphore(name))

        pT = [sb("pTHi", [P, PT_COLS], F32R)[:, :], sb("pTLo", [P, PT_COLS], F32R)[:, :]]
        sb("wk_room", [P, 2 * WK_COLS])
        wq, wk = keep.wq_parts, keep.wk
        v = [sb("vHi", [P, TILES, MLA_HEADS * MLA_V_DIM], F32R), sb("vLo", [P, TILES, MLA_HEADS * MLA_V_DIM], F32R)]
        table = sb("rope_table", [P, SEQ])
        q1 = [keep.q1k1[:, 0:SEQ], keep.q1k1[:, SEQ:2 * SEQ]]
        k0 = [sb("k0Hi", [P, SEQ], F32R), sb("k0Lo", [P, SEQ], F32R)]
        k1 = [keep.q1k1[:, 2 * SEQ:3 * SEQ], sb("k1Lo", [P, SEQ], F32R)]
        identR = sb("identR", [P, P], F32R)
        maskR = sb("maskR", [P, 3 * P], F32R)
        st = sb("softmax_small", [P, 4, 4])
        act_parts = (keep.actHi, keep.actLo)
        wv = [a[:, KD - 1, 0:MLA_HEADS * MLA_V_DIM] for a in act_parts]
        raw_wv = keep.raw_ukv[:, :, MLA_NOPE_DIM:]
        cT = [a[:, 0:KQ + 1, :] for a in act_parts]
        qbuf = [[a[:, KQ + 1, :] for a in act_parts], [a[:, :] for a in q1]]
        kbuf = [[a[:, :] for a in k0], [a[:, :] for a in k1]]
        prob_rows = keep.latent.rearrange("p t n -> p (t n)")

        def prob(m):
            i = m % TILES
            return prob_rows[:, ROW_AT[i] * P:(ROW_AT[i] + i + 1) * P]

        lat = keep.latent
        neg_top, total, inverse = (st[:, i, :] for i in range(3))

        ps = keep.ps

        lat_turned = sem("lat_turned")
        lat_hi = sem("lat_hi")
        lat_lo = sem("lat_lo")
        rot_turned = sem("rot_turned")
        tab_turned = sem("tab_turned")
        rot_hi = sem("rot_hi")
        rot_lo = sem("rot_lo")
        tab_copied = sem("tab_copied")
        mask_ready = sem("mask_ready")
        w_hi = sem("w_hiB")
        w_lo = sem("w_loB")
        v_done = sem("v_done")
        v_hi = sem("v_hi")
        v_lo = sem("v_lo")
        proj_done = sem("proj_done")
        proj_roped = sem("proj_roped")
        proj_hi = sem("proj_hi")
        proj_lo = sem("proj_lo")
        score_done = sem("score_done")
        top_ready = sem("top_ready")
        exp_done = sem("exp_done")
        inverse_ready = sem("inverse_ready")
        prob_ready = sem("prob_ready")
        pt_turned = sem("pt_turned")
        pt_hi = sem("pt_hi")
        pt_lo = sem("pt_lo")
        pv_done = sem("pv_done")
        out_hi = sem("out_hi")
        out_lo = sem("out_lo")
        y_turned = sem("y_turned")
        y_hi = sem("y_hi")
        y_lo = sem("y_lo")
        dve_own = sem("dve_ownB")
        act_own = sem("act_ownB")
        pool_own = sem("pool_ownB")

        PIECE_AT = [0, 2, 4, 6]
        gain_kv = keep.cols[:, COL_KV_A:COL_KV_A + 1]

        def by_head(ap):
            return ap.rearrange("p (h n) -> p h n", h=MLA_HEADS)

        def project_bank(h, piece):
            return [7, 0, 1, 7][piece] if h == 0 else 7

        def value_bank(t):
            return 6 - t % 2

        def projections(m):
            h, i = divmod(m, TILES)
            return [(h + 1, PIECE_AT.index(i))] if 0 <= h < MLA_HEADS - 1 and i in PIECE_AT else []

        KR = RET_WIDTH // P
        Y0 = STEPS - TILES
        V_FIRST = 6
        K1_AT = 4
        LAT_BANK = [0, 1, 6, 7]

        def chunk_of(t):
            return [t // BLOCK_ROWS] if 0 <= t < STEPS and t % BLOCK_ROWS == BLOCK_ROWS - 1 else []

        block = ctx.enter_context(nc.Block())

        @block.sync
        def _(sp):
            sp.wait_ge(proj_done, 4 * (MLA_HEADS - 1) + 2)
            for k in range(WO_RING):
                sp.dma_start(keep.raw_wo[:, k, :], io.w_o[0][k * P:(k + 1) * P, :]).then_inc(keep.wo_in[k], 16)

        @block.gpsimd
        def _(pool):
            own = Own(pool, pool_own)
            for m in range(STEPS):
                pool.wait_ge(inverse_ready, m + 1)
                row = prob(m)
                pool.tensor_scalar(row, row, inverse[:, m % 4:m % 4 + 1], 1.0, ALU.mult, ALU.mult).then_inc(prob_ready, 1)

        @block.scalar
        def _(act):
            own = Own(act, act_own)
            act.activation(by_head(wv[0]), raw_wv, ACT.Identity, scale=gain_kv).then_inc(w_hi, 1)
            for t in range(TILES):
                act.wait_ge(lat_turned, t + 1)
                act.activation(cT[0][:, :, t * P:(t + 1) * P], ps[:, LAT_BANK[t % 4], 0:(KQ + 1) * P].rearrange("p (k c) -> p k c", c=P),
                               ACT.Copy).then_inc(lat_hi, 1)
            act.wait_ge(tab_turned, 1)
            act.activation(table[:, :], ps[:, 4:6, :].rearrange("p a n -> p (a n)"), ACT.Copy).then_inc(tab_copied, 1)

            def value_hi(t):
                act.wait_ge(v_done, t + 1)
                act.activation(v[0][:, t, :], ps[:, value_bank(t), :], ACT.Copy).then_inc(v_hi, 1)

            def project_hi(h, piece):
                u = 4 * h + piece
                cols = slice((piece % 2) * BANK, (piece % 2 + 1) * BANK)
                if piece < 2:
                    act.wait_ge(proj_roped, 2 * h + piece + 1)
                    act.activation(qbuf[h % 2][0][:, cols], ps[:, project_bank(h, piece), :], ACT.Copy).then_inc(proj_hi, 1)
                else:
                    act.wait_ge(proj_done, u + 1)
                    act.activation(kbuf[h % 2][0][0:ROT, cols], ps[0:ROT, project_bank(h, piece), :], ACT.Copy).then_inc(proj_hi, 1)

            for piece in range(4):
                if piece == 2:
                    act.wait_ge(rot_turned, 1)
                    act.activation(kbuf[0][0][ROT:P, :], ps[ROT:P, 2:4, :].rearrange("p a n -> p (a n)"), ACT.Copy).then_inc(rot_hi, 1)
                project_hi(0, piece)
                value_hi(piece)
            for t in range(4, V_FIRST):
                value_hi(t)
            act.activation(identR[:, :], keep.ident, ACT.Copy).then_inc(mask_ready, 1)
            for at, scale in ((0, 0.0), (P, 1.0), (2 * P, 0.0)):
                act.activation(maskR[:, at:at + P], keep.neg, ACT.Copy, scale=scale).then_inc(mask_ready, 1)

            def turn_hi(t):
                for b, parts in groups_of(t):
                    g = bank_of[(t, b)]
                    act.wait_ge(pt_turned, g + 1)
                    for n, (first, count) in enumerate(parts):
                        src = ps[:, 4 + g % 2, :].rearrange("p (j c) -> p j c", c=P)[:, first - b:first - b + count, :]
                        last = act.activation(pt_view(pT[0], t, first, count), src, ACT.Copy)
                        last.then_inc(pt_hi, 1) if n == len(parts) - 1 else own(last)

            for m in range(STEPS + LAG + 2):
                t = m - LAG
                fresh = t % BLOCK_ROWS == 0
                if 0 <= m - 1 - Y0 < TILES:
                    j = m - 1 - Y0
                    act.wait_ge(y_turned, j + 1)
                    act.activation(act_parts[0][:, 0:KR, j * P:(j + 1) * P], ps[:, 7, :].rearrange("p (k c) -> p k c", c=P), ACT.Copy).then_inc(y_hi, 1)
                for h, piece in projections(m - 1):
                    if piece >= 2:
                        project_hi(h, piece)
                if 0 <= t < STEPS and not fresh:
                    turn_hi(t)
                if m < STEPS:
                    i = m % TILES
                    act.wait_ge(top_ready, m + 1)
                    if m >= ROWS:
                        act.wait_ge(pt_turned, through[m - ROWS])
                    act.activation(prob(m),
                                   ps[:, 2 * (m % 2):2 * (m % 2) + 2, :].rearrange("p a n -> p (a n)")[:, 0:(i + 1) * P],
                                   ACT.Exp, bias=neg_top[:, m % 4:m % 4 + 1],
                                   accum_out=total[:, m % 4:m % 4 + 1]).then_inc(exp_done, 1)
                if 0 <= t < STEPS and fresh:
                    if t > 0:
                        act.wait_ge(pv_done, t // BLOCK_ROWS)
                    turn_hi(t)
                for chunk in chunk_of(t - 2):
                    h, qc = divmod(chunk, 2)
                    half = slice(MLA_V_DIM * (h % 2), MLA_V_DIM * (h % 2 + 1))
                    act.wait_ge(pv_done, chunk + 1)
                    act.activation(act_parts[0][half, 4 + h // 2, qc * BANK:(qc + 1) * BANK], ps[half, 6, :], ACT.Copy).then_inc(out_hi, 1)
                for h, piece in projections(m - 1):
                    if piece < 2:
                        project_hi(h, piece)
                if 0 <= m - 1 < TILES - V_FIRST:
                    value_hi(m - 1 + V_FIRST)
                if m == K1_AT:
                    act.activation(kbuf[1][0][ROT:P, :], kbuf[0][0][ROT:P, :].bitcast(F32), ACT.Copy).then_inc(rot_hi, 1)

        @block.vector
        def _(dve):
            own = Own(dve, dve_own)
            dve.wait_ge(w_hi, 1)
            dve.scalar_tensor_tensor(by_head(wv[1]), raw_wv, gain_kv, by_head(wv[0]).bitcast(F32), ALU.mult, ALU.subtract).then_inc(w_lo, 1)
            for t in range(TILES):
                dve.wait_ge(lat_hi, t + 1)
                dve.tensor_tensor(cT[1][:, :, t * P:(t + 1) * P], ps[:, LAT_BANK[t % 4], 0:(KQ + 1) * P].rearrange("p (k c) -> p k c", c=P),
                                  cT[0][:, :, t * P:(t + 1) * P].bitcast(F32), ALU.subtract).then_inc(lat_lo, 1)

            def value_lo(t):
                dve.wait_ge(v_hi, t + 1)
                dve.tensor_tensor(v[1][:, t, :], ps[:, value_bank(t), :], v[0][:, t, :].bitcast(F32), ALU.subtract).then_inc(v_lo, 1)

            def rope_piece(h, piece):
                if piece < 2:
                    cols = slice(piece * BANK, (piece + 1) * BANK)
                    dve.wait_ge(proj_done, 4 * h + piece + 1)
                    if h == 0 and piece == 0:
                        dve.wait_ge(tab_copied, 1)
                    z = ps[:, project_bank(h, piece), :]
                    dve.tensor_tensor(z, z, table[:, cols], ALU.mult).then_inc(proj_roped, 1)

            def project_lo(h, piece):
                cols = slice((piece % 2) * BANK, (piece % 2 + 1) * BANK)
                rows, buf = (slice(0, P), qbuf) if piece < 2 else (slice(0, ROT), kbuf)
                dve.wait_ge(proj_hi, 4 * h + piece + 1)
                dve.tensor_tensor(buf[h % 2][1][rows, cols], ps[rows, project_bank(h, piece), :], buf[h % 2][0][rows, cols].bitcast(F32),
                                  ALU.subtract).then_inc(proj_lo, 1)

            rope_piece(0, 0)
            for piece in range(4):
                if piece + 1 < 4:
                    rope_piece(0, piece + 1)
                if piece == 2:
                    dve.wait_ge(rot_hi, 1)
                    dve.tensor_tensor(kbuf[0][1][ROT:P, :], ps[ROT:P, 2:4, :].rearrange("p a n -> p (a n)"),
                                      kbuf[0][0][ROT:P, :].bitcast(F32), ALU.subtract).then_inc(rot_lo, 1)
                project_lo(0, piece)
                value_lo(piece)
            for t in range(4, V_FIRST):
                value_lo(t)
            for m in range(STEPS + LAG + 2):
                if m < STEPS:
                    i, s = m % TILES, m % 4
                    scores = ps[:, 2 * (m % 2):2 * (m % 2) + 2, :].rearrange("p a n -> p (a n)")
                    dve.wait_ge(score_done, m + 1)
                    dve.tensor_reduce(neg_top[:, s:s + 1], scores[:, 0:(i + 1) * P], AX, ALU.max, negate=True).then_inc(top_ready, 1)
                if 0 <= m - 1 - Y0 < TILES:
                    j = m - 1 - Y0
                    dve.wait_ge(y_hi, j + 1)
                    dve.tensor_tensor(act_parts[1][:, 0:KR, j * P:(j + 1) * P], ps[:, 7, :].rearrange("p (k c) -> p k c", c=P),
                                      act_parts[0][:, 0:KR, j * P:(j + 1) * P].bitcast(F32), ALU.subtract).then_inc(y_lo, 1)
                if 1 <= m <= STEPS:
                    s = (m - 1) % 4
                    dve.wait_ge(exp_done, m)
                    dve.reciprocal(inverse[:, s:s + 1], total[:, s:s + 1]).then_inc(inverse_ready, 1)
                for h, piece in projections(m - 1):
                    rope_piece(h, piece)
                    if piece >= 2:
                        project_lo(h, piece)
                t = m - LAG
                if 0 <= t < STEPS:
                    for b, parts in groups_of(t):
                        g = bank_of[(t, b)]
                        dve.wait_ge(pt_hi, g + 1)
                        for n, (first, count) in enumerate(parts):
                            src = ps[:, 4 + g % 2, :].rearrange("p (j c) -> p j c", c=P)[:, first - b:first - b + count, :]
                            last = dve.tensor_tensor(pt_view(pT[1], t, first, count), src,
                                                     pt_view(pT[0], t, first, count).bitcast(F32), ALU.subtract)
                            last.then_inc(pt_lo, 1) if n == len(parts) - 1 else own(last)
                for chunk in chunk_of(t - 2):
                    h, qc = divmod(chunk, 2)
                    half = slice(MLA_V_DIM * (h % 2), MLA_V_DIM * (h % 2 + 1))
                    cols = slice(qc * BANK, (qc + 1) * BANK)
                    dve.wait_ge(out_hi, chunk + 1)
                    dve.tensor_tensor(act_parts[1][half, 4 + h // 2, cols], ps[half, 6, :],
                                      act_parts[0][half, 4 + h // 2, cols].bitcast(F32), ALU.subtract).then_inc(out_lo, 1)
                for h, piece in projections(m - 1):
                    if piece < 2:
                        project_lo(h, piece)
                if 0 <= m - 1 < TILES - V_FIRST:
                    value_lo(m - 1 + V_FIRST)
                if m == K1_AT:
                    dve.wait_ge(rot_lo, 1)
                    dve.tensor_copy(kbuf[1][1][ROT:P, :], kbuf[0][1][ROT:P, :].bitcast(F32)).then_inc(rot_lo, 1)

        @block.tensor
        def _(pe):
            for t in range(TILES):
                if t >= 4:
                    pe.wait_ge(lat_lo, t - 3)
                for k in range(KQ + 1):
                    last = pe.transpose(ps[:, LAT_BANK[t % 4], k * P:(k + 1) * P], lat[:, t, k * P:(k + 1) * P], keep.ident)
                last.then_inc(lat_turned, 1)
                if t == 3:
                    for j in range(TILES):
                        last = pe.transpose(ps[:, 4 + j // 4, (j % 4) * P:(j % 4 + 1) * P], keep.trow[:, j, :], keep.ident)
                    last.then_inc(tab_turned, 1)
            for t in range(TILES):
                last = pe.transpose(ps[:, 2 + t // 4, (t % 4) * P:(t % 4 + 1) * P], keep.krow[:, t, :], keep.ident)
            last.then_inc(rot_turned, 1)

            def value(t):
                if t == 1:
                    pe.wait_ge(tab_copied, 1)
                elif t >= 2:
                    pe.wait_ge(v_lo, t - 1)
                split_product(pe, ps[:, value_bank(t), :], cT[0][:, KQ, t * P:(t + 1) * P], cT[1][:, KQ, t * P:(t + 1) * P],
                              wv[0], wv[1], True, True).then_inc(v_done, 1)

            def project(h, piece):
                u = 4 * h + piece
                cols = slice((piece % 2) * BANK, (piece % 2 + 1) * BANK)
                if h >= 1:
                    pe.wait_ge(proj_lo, u)
                elif piece == 3:
                    pe.wait_ge(proj_lo, 1)
                if piece < 2:
                    for k in range(KQ):
                        last = split_product(pe, ps[:, project_bank(h, piece), :], wq[0][:, k, h, :], wq[1][:, k, h, :],
                                             cT[0][:, k, cols], cT[1][:, k, cols], k == 0, k == KQ - 1)
                else:
                    last = split_product(pe, ps[0:ROT, project_bank(h, piece), :], wk[0][:, h, :], wk[1][:, h, :],
                                         cT[0][:, KQ, cols], cT[1][:, KQ, cols], True, True)
                last.then_inc(proj_done, 1)

            pe.wait_ge(lat_lo, TILES)
            pe.wait_ge(w_lo, 1)
            for piece in range(4):
                project(0, piece)
                value(piece)
            for t in range(4, V_FIRST):
                value(t)
            pe.wait_ge(rot_lo, 1)
            pe.wait_ge(mask_ready, 4)
            for m in range(STEPS + LAG + 1):
                if m < STEPS:
                    h, i = divmod(m, TILES)
                    if i == 0:
                        pe.wait_ge(proj_lo, 4 * (h + 1))
                    if m == TILES:
                        pe.wait_ge(rot_lo, 2)
                    if m >= 2:
                        pe.wait_ge(exp_done, m - 1)
                    q, k = qbuf[h % 2], kbuf[h % 2]
                    width = (i + 1) * P
                    for c in range(0, width, BANK):
                        n = max(min(BANK, width - c), FULL_RATE)
                        last = split_product(pe, ps[:, 2 * (m % 2) + c // BANK, 0:n], q[0][:, i * P:(i + 1) * P], q[1][:, i * P:(i + 1) * P],
                                             k[0][:, c:c + n], k[1][:, c:c + n], True, c + n < width)
                    at, zeros = (i * P % BANK - P, 0) if i % (BANK // P) else (0, P)
                    last = pe.matmul(ps[:, 2 * (m % 2) + i * P // BANK, at:at + FULL_RATE], identR[:, :], maskR[:, zeros:zeros + FULL_RATE],
                                     start=False, stop=True)
                    last.then_inc(score_done, 1)
                t = m - LAG
                if 0 <= t < STEPS:
                    pe.wait_ge(prob_ready, t + 1)
                    for b, parts in groups_of(t):
                        g = bank_of[(t, b)]
                        if g >= 2:
                            pe.wait_ge(pt_lo, g - 1)
                        else:
                            pe.wait_ge(v_lo, TILES)
                        for j in range(b, min(b + 4, t % TILES + 1)):
                            last = pe.transpose(ps[:, 4 + g % 2, (j - b) * P:(j - b + 1) * P], prob(t)[:, j * P:(j + 1) * P], keep.ident)
                        last.then_inc(pt_turned, 1)
                t = m - LAG - 1
                for chunk in chunk_of(t):
                    h, qc = divmod(chunk, 2)
                    pe.wait_ge(pt_lo, through[t])
                    if chunk >= 1:
                        pe.wait_ge(out_lo, chunk)
                    else:
                        pe.wait_ge(v_lo, TILES)
                    pair = slice(h // 2 * P, (h // 2 + 1) * P)
                    keys = BLOCK_ROWS * (qc + 1)
                    for j in range(keys):
                        ahead = max(j - BLOCK_ROWS * qc, 0) * P
                        at = slice(PT_OFF[j], PT_OFF[j] + BANK - ahead)
                        last = split_product(pe, ps[:, 6, ahead:BANK], v[0][:, j, pair], v[1][:, j, pair],
                                             pT[0][:, at], pT[1][:, at], j == 0, j == keys - 1)
                    last.then_inc(pv_done, 1)
                for h, piece in projections(m):
                    project(h, piece)
                if m < TILES - V_FIRST:
                    value(m + V_FIRST)
                if 0 <= m - Y0 < TILES:
                    j = m - Y0
                    if j >= 1:
                        pe.wait_ge(y_lo, j)
                    else:
                        pe.wait_ge(proj_lo, 4 * MLA_HEADS)
                    for k in range(KR):
                        last = pe.transpose(ps[:, 7, k * P:(k + 1) * P], keep.q_y[:, j, k * P:(k + 1) * P], keep.ident)
                    last.then_inc(y_turned, 1)


def up_product(pe, keep, up, z, c):
    cols = slice(c * BANK, (c + 1) * BANK)
    bank = (GATE_BANKS, UP_BANKS)[z].start + c
    for k in range(KD):
        last = split_product(pe, keep.ps[:, bank, :], up[0][:, k, z, :], up[1][:, k, z, :],
                             keep.actHi[:, k, cols], keep.actLo[:, k, cols], k == 0, k == KD - 1)
    return last


def mix_output(nc, io, keep):
    KR = RET_WIDTH // P
    with ExitStack() as ctx:
        def sb(name, shape, dt=F32):
            return ctx.enter_context(nc.sbuf_tensor(name, shape, dt))

        def sem(name):
            return ctx.enter_context(nc.semaphore(name))

        wHi = sb("woHi", [P, KD, D_MODEL], F32R)
        wLo = sb("woLo", [P, KD, D_MODEL], F32R)
        raw = keep.raw_wo
        four_rows = keep.q_y.rearrange("p t n -> p (t n)").rearrange("p (b n) -> p b n", b=4)
        g_post, g_pre, xrow = four_rows[:, 0, :], four_rows[:, 1, :], four_rows[:, 2:4, :]
        x1 = sb("x1row", [P, 2, D_MODEL])
        stat = sb("statC", [P, 4, TILES])
        rows = keep.latent.rearrange("p t n -> p (t n)")[:, 0:3 * D_MODEL].rearrange("p (b n) -> p b n", b=3)
        mixn, h2, junk = rows[:, 0, :], rows[:, 1, :], rows[:, 2, :]
        ps = keep.ps

        gains_in = sem("gains_in")
        x_in = [sem("xr_in0"), sem("xr_in1")]
        w_hi = sem("wo_hi")
        w_lo = sem("wo_lo")
        mix_done = sem("mix_done")
        mix_sq = sem("mix_sq")
        mix_rstd = sem("mix_rstd")
        mix_read = sem("mix_read")
        x1_done = sem("x1_done")
        x1_sq = sem("x1_sq")
        x1_rstd = sem("x1_rstd")
        x1_stored = [sem("x1_stored0"), sem("x1_stored1")]
        h2_done = sem("h2_done")
        h2_turned = sem("h2_turned")
        h2_hi = sem("h2_hi")
        h2_lo = sem("h2_lo")

        xr = io.x[0].rearrange("(t p) d -> t p d", p=P)
        wr = io.w_o[0].rearrange("(k p) n -> k p n", p=P)
        x1r = io.x1.rearrange("(t p) d -> t p d", p=P)

        def banks(t):
            return ps[:, 2 * (t % 2):2 * (t % 2) + 2, :].rearrange("p a n -> p (a n)")

        def tile_of(a, t, k0, k1):
            return a[:, k0:k1, t * P:(t + 1) * P]

        block = ctx.enter_context(nc.Block())

        @block.sync
        def _(sp):
            def load_x(t):
                if t >= 2:
                    sp.wait_ge(x1_done, t - 1)
                sp.dma_start(xrow[:, t % 2, :], xr[t]).then_inc(x_in[t % 2], 16)

            load_x(0)
            sp.dma_start(g_post, io.g_post_mix[0].partition_broadcast(P)).then_inc(gains_in, 16)
            for k in range(WO_RING, KD):
                sp.wait_ge(w_lo, k - WO_RING + 1)
                sp.dma_start(raw[:, k % WO_RING, :], wr[k]).then_inc(keep.wo_in[k % WO_RING], 16)
            sp.dma_start(g_pre, io.g_pre_ffn[0].partition_broadcast(P)).then_inc(gains_in, 16)
            load_x(1)
            w_up = io.w_up[0].rearrange("(k p) (z j c) -> p k z j c", p=P, z=2, c=P)
            for z in range(2):
                sp.dma_start(keep.raw_up[:, :, z, :], w_up[:, :, z, 0, :]).then_inc(keep.up_in, 16)
            for t in range(TILES):
                sp.wait_ge(x1_done, t + 1)
                sp.dma_start(x1r[t], x1[:, t % 2, :]).then_inc(x1_stored[t % 2], 16)
                if t + 2 < TILES:
                    load_x(t + 2)
            for b in range(2):
                sp.wait_ge(x1_stored[b], 16 * TILES // 2)

        @block.gpsimd
        def _(pool):
            for t in range(TILES):
                for done, ready, i in ((mix_sq, mix_rstd, 0), (x1_sq, x1_rstd, 2)):
                    pool.wait_ge(done, t + 1)
                    keep.pool_own(pool.tensor_scalar(stat[:, i + 1, t:t + 1], stat[:, i, t:t + 1], 1.0 / D_MODEL, EPS, ALU.mult, ALU.add))
                    pool.tensor_tensor(stat[:, i + 1, t:t + 1], stat[:, i + 1, t:t + 1], keep.neghalf[:, 0:1], ALU.pow).then_inc(ready, 1)

        @block.scalar
        def _(act):
            for k in range(KD):
                act.wait_ge(keep.wo_in[k % WO_RING], 16 * (k // WO_RING + 1))
                if k < KR:
                    act.activation(wHi[:, k, :], raw[:, k % WO_RING, :], ACT.Identity,
                                   scale=keep.cols[:, COL_RET_GN + k:COL_RET_GN + k + 1]).then_inc(w_hi, 1)
                else:
                    act.activation(wHi[:, k, :], raw[:, k % WO_RING, :], ACT.Copy).then_inc(w_hi, 1)
            act.wait_ge(keep.up_in, 32)
            act.wait_ge(w_lo, KD)
            act.activation(keep.up0[0], keep.raw_up, ACT.Copy).then_inc(keep.up_hi, 1)
            for t in range(TILES + 1):
                if t < TILES:
                    act.wait_ge(mix_done, t + 1)
                    if t >= 1:
                        act.wait_ge(x1_sq, t)
                    act.activation(junk, banks(t), ACT.Square, accum_out=stat[:, 0, t:t + 1]).then_inc(mix_sq, 1)
                    act.wait_ge(x1_done, t + 1)
                    act.wait_ge(mix_sq, t + 1)
                    act.activation(junk, x1[:, t % 2, :], ACT.Square, accum_out=stat[:, 2, t:t + 1]).then_inc(x1_sq, 1)
                if t >= 1:
                    act.wait_ge(h2_turned, t)
                    act.activation(tile_of(keep.actHi, t - 1, 0, KD), ps[:, 6:8, :].rearrange("p a (k c) -> p (a k) c", c=P),
                                   ACT.Copy).then_inc(h2_hi, 1)

        @block.vector
        def _(dve):
            for k in range(KD):
                dve.wait_ge(w_hi, k + 1)
                if k < KR:
                    dve.scalar_tensor_tensor(wLo[:, k, :], raw[:, k % WO_RING, :], keep.cols[:, COL_RET_GN + k:COL_RET_GN + k + 1],
                                             wHi[:, k, :].bitcast(F32), ALU.mult, ALU.subtract).then_inc(w_lo, 1)
                else:
                    dve.tensor_tensor(wLo[:, k, :], raw[:, k % WO_RING, :], wHi[:, k, :].bitcast(F32), ALU.subtract).then_inc(w_lo, 1)
            dve.wait_ge(keep.up_hi, 1)
            dve.tensor_tensor(keep.up0[1], keep.raw_up, keep.up0[0].bitcast(F32), ALU.subtract).then_inc(keep.up_lo, 1)
            dve.wait_ge(gains_in, 32)
            for t in range(TILES + 1):
                if t < TILES:
                    dve.wait_ge(mix_rstd, t + 1)
                    if t >= 1:
                        dve.wait_ge(x1_done, t)
                    dve.scalar_tensor_tensor(mixn, banks(t), stat[:, 1, t:t + 1], g_post, ALU.mult, ALU.mult).then_inc(mix_read, 1)
                    dve.wait_ge(mix_read, t + 1)
                    dve.wait_ge(x_in[t % 2], 16 * (t // 2 + 1))
                    if t >= 2:
                        dve.wait_ge(x1_stored[t % 2], 16 * (t // 2))
                    dve.tensor_tensor(x1[:, t % 2, :], mixn, xrow[:, t % 2, :], ALU.add).then_inc(x1_done, 1)
                    dve.wait_ge(x1_rstd, t + 1)
                    if t >= 1:
                        dve.wait_ge(h2_turned, t)
                    dve.scalar_tensor_tensor(h2, x1[:, t % 2, :], stat[:, 3, t:t + 1], g_pre, ALU.mult, ALU.mult).then_inc(h2_done, 1)
                if t >= 1:
                    dve.wait_ge(h2_hi, t)
                    dve.tensor_tensor(tile_of(keep.actLo, t - 1, 0, KD), ps[:, 6:8, :].rearrange("p a (k c) -> p (a k) c", c=P),
                                      tile_of(keep.actHi, t - 1, 0, KD).bitcast(F32), ALU.subtract).then_inc(h2_lo, 1)

        @block.tensor
        def _(pe):
            for t in range(TILES + 1):
                if t < TILES:
                    if t >= 2:
                        pe.wait_ge(mix_read, t - 1)
                    for k in range(KD):
                        if t == 0:
                            pe.wait_ge(w_lo, k + 1)
                        for half in range(2):
                            cols = slice(half * BANK, (half + 1) * BANK)
                            last = split_product(pe, ps[:, 2 * (t % 2) + half, :], keep.actHi[:, k, t * P:(t + 1) * P],
                                                 keep.actLo[:, k, t * P:(t + 1) * P], wHi[:, k, cols], wLo[:, k, cols], k == 0, k == KD - 1)
                    last.then_inc(mix_done, 1)
                if t >= 1:
                    pe.wait_ge(h2_done, t)
                    if t >= 2:
                        pe.wait_ge(h2_lo, t - 1)
                    for k in range(KD):
                        last = pe.transpose(ps[:, 6 + k // 4, (k % 4) * P:(k % 4 + 1) * P], h2[:, k * P:(k + 1) * P], keep.ident)
                    last.then_inc(h2_turned, 1)
                if t >= TILES - 1:
                    if t == TILES - 1:
                        pe.wait_ge(keep.up_lo, 1)
                        pe.wait_ge(h2_lo, BANK // P)
                        pe.wait_ge(mix_read, TILES - 1)
                    up_product(pe, keep, keep.up0, t - TILES + 1, 0)


def conv_ffn(nc, io, keep):
    PAIR = 2
    ROUNDS = FF_TILES // PAIR
    OUTS = TILES * (D_MODEL // BANK)
    DOWN_BANKS = [2, 3, 6, 7]
    RING = len(DOWN_BANKS)
    with ExitStack() as ctx:
        def sb(name, shape, dt=F32):
            return ctx.enter_context(nc.sbuf_tensor(name, shape, dt))

        def sem(name):
            return ctx.enter_context(nc.semaphore(name))

        raw_up = keep.raw_up
        up1 = [sb("wupHi", [P, KD, 2, P], F32R)[:, :, :, :], sb("wupLo", [P, KD, 2, P], F32R)[:, :, :, :]]
        up = [keep.up0, up1]
        raw_dn = sb("raw_dn", [P, PAIR, D_MODEL])
        dn = [sb("wdnHi", [P, PAIR, D_MODEL], F32R), sb("wdnLo", [P, PAIR, D_MODEL], F32R)]
        f = [sb("fHi", [P, PAIR, SEQ], F32R), sb("fLo", [P, PAIR, SEQ], F32R)]
        conv_g = sb("conv_g", [P, SEQ])
        conv_u = sb("conv_u", [P, SEQ])
        gelu = sb("gelu", [P, SEQ])
        ps = keep.ps
        gate_ps = ps[:, GATE_BANKS, :].rearrange("p a n -> p (a n)")
        up_ps = ps[:, UP_BANKS, :].rearrange("p a n -> p (a n)")

        dn_in = sem("dn_in")
        up_in, up_hi, up_lo = keep.up_in, keep.up_hi, keep.up_lo
        dn_hi = sem("dn_hi")
        dn_lo = sem("dn_lo")
        gate_done = sem("gateD_done")
        up_done = sem("upD_done")
        gate_tap = sem("gate_tap")
        up_tap = sem("up_tap")
        gate_read = sem("gate_read")
        up_read = sem("up_read")
        gelu_done = sem("gelu_done")
        product = sem("product")
        f_hi = sem("f_hi")
        f_lo = sem("f_lo")
        down_done = sem("down_done")
        down_free = sem("down_free")
        ffn_zero = sem("ffn_zero")
        tap_own = sem("tap_own")
        f_rstd = sem("f_rstd")

        w_up = io.w_up[0].rearrange("(k p) (z j c) -> p k z j c", p=P, z=2, c=P)
        w_dn = io.w_down[0].rearrange("(j p) n -> p j n", p=P)

        WHOLE = [(0, SEQ)]
        HALVES = [(0, BANK), (BANK, SEQ)]

        def rounds(eng, body):
            body(0, True, False)
            with eng.Fori(1, ROUNDS - 1) as r:
                body(r, False, False)
            body(ROUNDS - 1, False, True)

        def col(at, n):
            return keep.cols[:, bass.ds(n + at, 1)]

        block = ctx.enter_context(nc.Block())

        @block.sync
        def _(sp):
            def load_up(n):
                sp.wait_ge(up_lo, n)
                for z in range(2):
                    sp.dma_start(raw_up[:, :, z, :], w_up[:, :, z, bass.ds(n, 1), :].squeeze(2)).then_inc(up_in, 16)

            def body(r, first, last):
                if not first:
                    load_up(r * PAIR)
                    sp.wait_ge(dn_lo, r)
                else:
                    load_up(1)
                sp.dma_start(raw_dn[:, :, :], w_dn[:, bass.ds(r * PAIR, PAIR), :]).then_inc(dn_in, 16)
                if not first:
                    load_up(r * PAIR + 1)

            rounds(sp, body)
            sp.wait_ge(up_done, FF_TILES - 1)
            x1r = io.x1.rearrange("(t p) d -> t p d", p=P)
            for s in range(KD + PLE_DIM // P):
                if s == 0:
                    sp.wait_ge(up_lo, FF_TILES)
                if s >= GATE_RING:
                    sp.wait_ge(keep.gate_lo, s - GATE_RING + 1)
                src = io.w_ple_gate[0][s * P:(s + 1) * P, :] if s < KD else io.w_ple[0][(s - KD) * P:(s - KD + 1) * P, :]
                sp.dma_start(keep.raw_gate[:, s % GATE_RING, :], src).then_inc(keep.gate_in[s % GATE_RING], 16)
                if s == GATE_RING - 1:
                    for t in range(2):
                        sp.dma_start(keep.four_rows[:, t, :], x1r[t]).then_inc(keep.x1_in[t], 16)
                    for row, gain in ((2, io.g_post_ffn), (3, io.b_ple_gate)):
                        sp.dma_start(keep.four_rows[:, row, :], gain[0].partition_broadcast(P)).then_inc(keep.rows_in, 16)
            sp.wait_ge(keep.rows_in, 32)

        @block.gpsimd
        def _(pool):
            pool.memset(keep.ffn[:, :, :], 0.0).then_inc(ffn_zero, 1)
            mean, rstd = keep.rstd_lat[:, 0, :], keep.rstd_lat[:, 1, :]
            for t in range(TILES):
                pool.wait_ge(keep.f_sq, t + 1)
                keep.pool_own(pool.tensor_scalar(rstd[:, t:t + 1], mean[:, t:t + 1], 1.0 / D_MODEL, EPS, ALU.mult, ALU.add))
                pool.tensor_tensor(rstd[:, t:t + 1], rstd[:, t:t + 1], keep.neghalf[:, 0:1], ALU.pow).then_inc(f_rstd, 1)
            pool.wait_ge(f_rstd, TILES)

        @block.scalar
        def _(act):
            def split_up(n, p, early):
                act.wait_ge(up_in, n * 32 + 32)
                if not early:
                    act.wait_ge(up_done, n - 1)
                act.activation(up[p][0], raw_up, ACT.Copy).then_inc(up_hi, 1)

            def step(n, p, r, first_step, first_round, final=False):
                act.wait_ge(gate_done, n + 1)
                if not first_step:
                    act.wait_ge(gelu_done, n)
                act.activation(conv_g[:, :], gate_ps, ACT.Identity, bias=col(COL_BIAS, n), scale=col(COL_W2, n)).then_inc(gate_tap, 1)
                act.wait_ge(gate_read, n + 1)
                if not first_step:
                    act.wait_ge(product, n)
                act.activation(gelu[:, :], conv_g[:, :], ACT.Gelu_apprx_tanh).then_inc(gelu_done, 1)
                for h, (lo, hi) in enumerate(HALVES if final else WHOLE):
                    act.wait_ge(up_done, n + 1 + h)
                    if not first_step:
                        act.wait_ge(f_lo, n)
                    act.activation(conv_u[:, lo:hi], up_ps[:, lo:hi], ACT.Identity, bias=col(COL_BIAS + FF_TILES, n),
                                   scale=col(COL_W2 + FF_TILES, n)).then_inc(up_tap, 1)
                    act.wait_ge(product, n + 1 + h)
                    if not first_round:
                        act.wait_ge(down_done, r * OUTS)
                    act.activation(f[0][:, p, lo:hi], conv_u[:, lo:hi], ACT.Copy).then_inc(f_hi, 1)

            def body(r, first, last):
                n = r * PAIR
                split_up(n + 1, 1, first)
                step(n, 0, r, first, first)
                act.wait_ge(dn_in, r * 16 + 16)
                act.activation(dn[0][:, :, :], raw_dn[:, :, :], ACT.Copy).then_inc(dn_hi, 1)
                if not last:
                    split_up(n + 2, 0, False)
                step(n + 1, 1, r, False, first, last)

            rounds(act, body)
            for t in range(TILES):
                if t == 0:
                    act.wait_ge(up_done, FF_TILES + 1)
                act.wait_ge(keep.gate_in[t % GATE_RING], 16 * (t // GATE_RING + 1))
                act.activation(keep.actHi[:, t, :], keep.raw_gate[:, t % GATE_RING, :], ACT.Copy).then_inc(keep.gate_hi, 1)
                act.wait_ge(down_free, RING + (ROUNDS - 1) * OUTS + 2 * t + 2)
                if t >= 1:
                    act.wait_ge(keep.f_sq, t)
                act.activation(gelu[:, :], keep.ffn[:, t, :], ACT.Square, accum_out=keep.rstd_lat[:, 0, t:t + 1]).then_inc(keep.f_sq, 1)

        @block.vector
        def _(dve):
            def split_up(p, n):
                dve.wait_ge(up_hi, n + 1)
                dve.tensor_tensor(up[p][1], raw_up, up[p][0].bitcast(F32), ALU.subtract).then_inc(up_lo, 1)

            def convolve(n, src, out, tap, tapped, read, at, lo=0, hi=SEQ, h=0):
                dve.wait_ge(tap, n + 1 + h)
                for back, weight in ((1, COL_W1), (2, COL_W0)):
                    start = max(lo, back)
                    step = dve.scalar_tensor_tensor(out[:, start:hi], src[:, start - back:hi - back], col(weight + at, n), out[:, start:hi],
                                                    ALU.mult, ALU.add)
                    if back == 1:
                        step.then_inc(tap_own, 1)
                        dve.wait_ge(tap_own, tapped)
                    else:
                        step.then_inc(read, 1)

            def multiply(n, lo=0, hi=SEQ, h=0):
                dve.wait_ge(up_read, n + 1 + h)
                dve.wait_ge(gelu_done, n + 1)
                dve.tensor_tensor(conv_u[:, lo:hi], gelu[:, lo:hi], conv_u[:, lo:hi], ALU.mult).then_inc(product, 1)

            def step(n):
                convolve(n, gate_ps, conv_g, gate_tap, n * 2 + 1, gate_read, 0)
                convolve(n, up_ps, conv_u, up_tap, n * 2 + 2, up_read, FF_TILES)

            def finish(n, p, lo=0, hi=SEQ, h=0):
                dve.wait_ge(f_hi, n + 1 + h)
                dve.tensor_tensor(f[1][:, p, lo:hi], conv_u[:, lo:hi], f[0][:, p, lo:hi].bitcast(F32), ALU.subtract).then_inc(f_lo, 1)

            def split_gate(s):
                dve.wait_ge(keep.gate_hi, s + 1)
                dve.tensor_tensor(keep.actLo[:, s, :], keep.raw_gate[:, s % GATE_RING, :], keep.actHi[:, s, :].bitcast(F32),
                                  ALU.subtract).then_inc(keep.gate_lo, 1)

            def add_round(r, outs, last=False):
                for o in outs:
                    t, half = divmod(o, 2)
                    row = keep.ffn[:, t, half * BANK:(half + 1) * BANK]
                    dve.wait_ge(down_done, r * OUTS + o + 1)
                    dve.tensor_tensor(row, ps[:, DOWN_BANKS[o % RING], :], row, ALU.add).then_inc(down_free, 1)
                    if last and half == 1:
                        split_gate(t)

            def body(r, first, last):
                n = r * PAIR
                split_up(1, n + 1)
                step(n)
                if not first:
                    add_round(r - 1, range(RING))
                multiply(n)
                if not first:
                    add_round(r - 1, range(RING, OUTS))
                finish(n, 0)
                dve.wait_ge(dn_hi, r + 1)
                dve.tensor_tensor(dn[1][:, :, :], raw_dn[:, :, :], dn[0][:, :, :].bitcast(F32), ALU.subtract).then_inc(dn_lo, 1)
                if not last:
                    split_up(0, n + 2)
                if not last:
                    step(n + 1)
                    multiply(n + 1)
                    finish(n + 1, 1)
                else:
                    convolve(n + 1, gate_ps, conv_g, gate_tap, n * 2 + 3, gate_read, 0)
                    for h, (lo, hi) in enumerate(HALVES):
                        convolve(n + 1, up_ps, conv_u, up_tap, n * 2 + 4 + h, up_read, FF_TILES, lo, hi, h)
                        multiply(n + 1, lo, hi, h)
                        finish(n + 1, 1, lo, hi, h)

            dve.sem_inc(down_free, RING)
            dve.wait_ge(ffn_zero, 1)
            rounds(dve, body)
            add_round(ROUNDS - 1, range(OUTS), True)

        @block.tensor
        def _(pe):
            def step(n, p, first, final=False):
                pe.wait_ge(up_lo, n + 1)
                for z, read, done in ((0, gate_read, gate_done), (1, up_read, up_done)):
                    if not first:
                        pe.wait_ge(read, n)
                    for c in range(1 if first else 0, SEQ // BANK):
                        last = up_product(pe, keep, up[p], z, c)
                        if final and z == 1 and c == 0:
                            last.then_inc(done, 1)
                    last.then_inc(done, 1)

            def down(r, final=False):
                pe.wait_ge(f_lo, r * PAIR + PAIR)
                pe.wait_ge(dn_lo, r + 1)
                for o in range(OUTS):
                    t, half = divmod(o, 2)
                    if final and t == BANK // P:
                        pe.wait_ge(f_lo, FF_TILES + 1)
                    pe.wait_ge(down_free, r * OUTS + o + 1)
                    for p in range(PAIR):
                        last = split_product(pe, ps[:, DOWN_BANKS[o % RING], :], f[0][:, p, t * P:(t + 1) * P], f[1][:, p, t * P:(t + 1) * P],
                                             dn[0][:, p, half * BANK:(half + 1) * BANK], dn[1][:, p, half * BANK:(half + 1) * BANK],
                                             p == 0, p == PAIR - 1)
                    last.then_inc(down_done, 1)

            def body(r, first, last):
                n = r * PAIR
                step(n, 0, first)
                if not first:
                    down(r - 1)
                step(n + 1, 1, False, last)

            rounds(pe, body)
            down(ROUNDS - 1, True)


def layer_embedding(nc, io, keep):
    KE = PLE_DIM // P
    with ExitStack() as ctx:
        def sb(name, shape, dt=F32):
            return ctx.enter_context(nc.sbuf_tensor(name, shape, dt))

        def sem(name):
            return ctx.enter_context(nc.semaphore(name))

        wg = (keep.actHi, keep.actLo)
        wp = [sb("wpHi", [P, KE, D_MODEL], F32R), sb("wpLo", [P, KE, D_MODEL], F32R)]
        x1, g_ffn, bias = keep.four_rows[:, 0:2, :], keep.four_rows[:, 2, :], keep.four_rows[:, 3, :]
        xT = [sb("x2Hi", [P, 2, KD, P], F32R), sb("x2Lo", [P, 2, KD, P], F32R)]
        pT = [sb("pHi", [P, 2, KE, P], F32R), sb("pLo", [P, 2, KE, P], F32R)]
        prow = sb("prow", [P, 2, PLE_DIM])
        orow = sb("out_row", [P, 2, D_MODEL])
        g_ple = sb("g_ple_row", [P, D_MODEL])
        gate = sb("ple_gate", [P, D_MODEL])
        e = sb("ple_e", [P, D_MODEL])
        junk = sb("junkE", [P, D_MODEL])
        stat = sb("statE", [P, 4, TILES])
        ps = keep.ps
        gate_ps = ps[:, 0:2, :].rearrange("p a n -> p (a n)")
        e_ps = ps[:, 2:4, :].rearrange("p a n -> p (a n)")

        rows_in = keep.rows_in
        x1_in = keep.x1_in
        p_in = [sem("p_in0"), sem("p_in1")]
        x2_part = sem("x2_part")
        x2_done = sem("x2_done")
        x2_turned = sem("x2_turned")
        x2_hi = sem("x2_hi")
        x2_lo = sem("x2_lo")
        gate_done = sem("gateE_done")
        gate_biased = sem("gate_biased")
        gate_sig = sem("gate_sig")
        ple_done = sem("ple_done")
        e_done = sem("e_done")
        e_sq = sem("e_sq")
        e_rstd = sem("e_rstd")
        e_normed = sem("e_normed")
        out_ready = sem("out_ready")
        out_stored = [sem("out_stored0"), sem("out_stored1")]

        x1r = io.x1.rearrange("(t p) d -> t p d", p=P)
        outr = io.out[0].rearrange("(t p) d -> t p d", p=P)
        pr = io.p[0, 0].rearrange("(t p) d -> t p d", p=P)

        def turned_bank(t):
            return ps[:, 4:6, :].rearrange("p a (k c) -> p (a k) c", c=P)

        block = ctx.enter_context(nc.Block())

        @block.sync
        def _(sp):
            def load_rows(t):
                if t >= 2:
                    sp.wait_ge(x2_done, t - 1)
                    sp.wait_ge(x2_turned, t - 1)
                    sp.dma_start(x1[:, t % 2, :], x1r[t]).then_inc(x1_in[t % 2], 16)
                sp.dma_start(prow[:, t % 2, :], pr[t]).then_inc(p_in[t % 2], 16)

            load_rows(0)
            load_rows(1)
            sp.dma_start(g_ple[:, :], io.g_post_ple[0].partition_broadcast(P)).then_inc(rows_in, 16)
            for t in range(TILES):
                if t + 2 < TILES:
                    load_rows(t + 2)
                sp.wait_ge(out_ready, t + 1)
                sp.dma_start(outr[t], orow[:, t % 2, :]).then_inc(out_stored[t % 2], 16)
            for b in range(2):
                sp.wait_ge(out_stored[b], 16 * TILES // 2)

        @block.gpsimd
        def _(pool):

            def rstd(done, ready, i, t):
                pool.wait_ge(done, t + 1)
                keep.pool_own(pool.tensor_scalar(stat[:, i + 1, t:t + 1], stat[:, i, t:t + 1], 1.0 / D_MODEL, EPS, ALU.mult, ALU.add))
                pool.tensor_tensor(stat[:, i + 1, t:t + 1], stat[:, i + 1, t:t + 1], keep.neghalf[:, 0:1], ALU.pow).then_inc(ready, 1)

            for t in range(TILES):
                rstd(e_sq, e_rstd, 2, t)

        @block.scalar
        def _(act):
            squares = [0]

            def square(src, accum, done, t):
                if squares[0]:
                    act.wait_ge(*squares[1])
                act.activation(junk[:, :], src, ACT.Square, accum_out=accum).then_inc(done, 1)
                squares[0:] = [1, (done, t + 1)]

            def turn_hi(t):
                act.wait_ge(x2_turned, t + 1)
                if t >= 2:
                    act.wait_ge(ple_done, t - 1)
                act.activation(xT[0][:, t % 2], turned_bank(t), ACT.Copy).then_inc(x2_hi, 1)
                act.activation(pT[0][:, t % 2], ps[:, 6, 0:KE * P].rearrange("p (k c) -> p k c", c=P), ACT.Copy).then_inc(x2_hi, 1)

            for s in range(KE):
                act.wait_ge(keep.gate_in[(KD + s) % GATE_RING], 16 * ((KD + s) // GATE_RING + 1))
                act.activation(wp[0][:, s, :], keep.raw_gate[:, (KD + s) % GATE_RING, :], ACT.Copy).then_inc(keep.gate_hi, 1)
            turn_hi(0)
            for t in range(TILES):
                if t + 1 < TILES:
                    turn_hi(t + 1)
                act.wait_ge(gate_biased, t + 1)
                act.activation(gate[:, :], gate[:, :], ACT.Sigmoid).then_inc(gate_sig, 1)
                act.wait_ge(e_done, t + 1)
                square(e[:, :], stat[:, 2, t:t + 1], e_sq, t)

        @block.vector
        def _(dve):
            def x2_rows(t):
                row = keep.ffn[:, t, :]
                dve.scalar_tensor_tensor(row, row, keep.rstd_lat[:, 1, t:t + 1], g_ffn, ALU.mult, ALU.mult).then_inc(x2_part, 1)
                dve.wait_ge(x2_part, t + 1)
                dve.wait_ge(x1_in[t % 2], 16 * (t // 2 + 1))
                dve.tensor_tensor(row, row, x1[:, t % 2, :], ALU.add).then_inc(x2_done, 1)

            def turn_lo(t):
                dve.wait_ge(x2_hi, 2 * t + 2)
                dve.tensor_tensor(xT[1][:, t % 2], turned_bank(t), xT[0][:, t % 2].bitcast(F32), ALU.subtract).then_inc(x2_lo, 1)
                dve.tensor_tensor(pT[1][:, t % 2], ps[:, 6, 0:KE * P].rearrange("p (k c) -> p k c", c=P), pT[0][:, t % 2].bitcast(F32),
                                  ALU.subtract).then_inc(x2_lo, 1)

            x2_rows(0)
            for s in range(KE):
                dve.wait_ge(keep.gate_hi, KD + s + 1)
                dve.tensor_tensor(wp[1][:, s, :], keep.raw_gate[:, (KD + s) % GATE_RING, :], wp[0][:, s, :].bitcast(F32),
                                  ALU.subtract).then_inc(keep.gate_lo, 1)
            turn_lo(0)
            x2_rows(1)
            dve.wait_ge(rows_in, 48)
            for t in range(TILES):
                if t + 1 < TILES:
                    turn_lo(t + 1)
                if t + 2 < TILES:
                    x2_rows(t + 2)
                dve.wait_ge(gate_done, t + 1)
                if t >= 1:
                    dve.wait_ge(e_done, t)
                dve.tensor_tensor(gate[:, :], gate_ps, bias, ALU.add).then_inc(gate_biased, 1)
                dve.wait_ge(gate_sig, t + 1)
                dve.wait_ge(ple_done, t + 1)
                if t >= 1:
                    dve.wait_ge(out_ready, t)
                dve.tensor_tensor(e[:, :], e_ps, gate[:, :], ALU.mult).then_inc(e_done, 1)
                dve.wait_ge(e_rstd, t + 1)
                dve.scalar_tensor_tensor(e[:, :], e[:, :], stat[:, 3, t:t + 1], g_ple[:, :], ALU.mult, ALU.mult).then_inc(e_normed, 1)
                dve.wait_ge(e_normed, t + 1)
                if t >= 2:
                    dve.wait_ge(out_stored[t % 2], 16 * (t // 2))
                dve.tensor_tensor(orow[:, t % 2, :], e[:, :], keep.ffn[:, t, :], ALU.add).then_inc(out_ready, 1)

        @block.tensor
        def _(pe):
            def turn(t):
                pe.wait_ge(x2_done, t + 1)
                pe.wait_ge(p_in[t % 2], 16 * (t // 2 + 1))
                if t >= 1:
                    pe.wait_ge(x2_lo, 2 * t)
                for k in range(KD):
                    pe.transpose(ps[:, 4 + k // 4, (k % 4) * P:(k % 4 + 1) * P], keep.ffn[:, t, k * P:(k + 1) * P], keep.ident)
                for k in range(KE):
                    last = pe.transpose(ps[:, 6, k * P:(k + 1) * P], prow[:, t % 2, k * P:(k + 1) * P], keep.ident)
                last.then_inc(x2_turned, 1)

            turn(0)
            for t in range(TILES):
                pe.wait_ge(x2_lo, 2 * t + 2)
                if t >= 1:
                    pe.wait_ge(gate_biased, t)
                for half in range(2):
                    cols = slice(half * BANK, (half + 1) * BANK)
                    for k in range(KD):
                        last = split_product(pe, ps[:, half, :], xT[0][:, t % 2, k, :], xT[1][:, t % 2, k, :],
                                             wg[0][:, k, cols], wg[1][:, k, cols], k == 0, k == KD - 1)
                    if half == 0 and t + 1 < TILES:
                        turn(t + 1)
                last.then_inc(gate_done, 1)
                if t == 0:
                    pe.wait_ge(keep.gate_lo, KD + KE)
                else:
                    pe.wait_ge(e_done, t)
                for half in range(2):
                    cols = slice(half * BANK, (half + 1) * BANK)
                    for k in range(KE):
                        last = split_product(pe, ps[:, 2 + half, :], pT[0][:, t % 2, k, :], pT[1][:, t % 2, k, :],
                                             wp[0][:, k, cols], wp[1][:, k, cols], k == 0, k == KE - 1)
                last.then_inc(ple_done, 1)


INPUTS = ["x", "p", "positions", "w_in", "w_uq", "w_ukv", "w_o", "g_pre_mix", "g_post_mix", "g_q_a", "g_kv_a",
          "g_ret_gn", "w_up", "conv_w", "conv_b", "w_down", "g_pre_ffn", "g_post_ffn", "w_ple", "w_ple_gate",
          "b_ple_gate", "g_post_ple"]


def decoder_layer(nc, io):
    with ExitStack() as ctx:
        def sb(name, shape, dt=F32):
            return ctx.enter_context(nc.sbuf_tensor(name, shape, dt))

        def sem(name):
            return ctx.enter_context(nc.semaphore(name))

        keep = Keep()
        keep.ident = sb("ident", [P, P])[:, :]
        keep.neg = sb("neg", [P, P])[:, :]
        keep.cols = sb("cols", [P, COLS])[:, :]
        keep.neghalf = sb("neghalf", [P, 8])[:, :]
        keep.rstd_lat = sb("rstd_lat", [P, 2, TILES])[:, :, :]
        keep.actHi = sb("actHi", [P, KD, SEQ], F32R)[:, :, :]
        keep.actLo = sb("actLo", [P, KD, SEQ], F32R)[:, :, :]
        hand_base = nc.sbuf_base
        sb("handover", [P, HAND1 + HAND2])

        def hand(name, first, count, dt=F32):
            return nc.alloc_sbuf_tensor_at(name, [P, count], dt, offset=hand_base + 4 * first)[:, :]

        keep.raw_w_in = hand("raw_w_in", 0, HAND1)
        keep.chunk_room = hand("chunk_room", HAND1, HAND2)
        raw_latent = hand("raw_latent", 0, HAND1)
        keep.q1k1 = hand("q1k1", 0, HAND1, F32R)
        keep.wq = hand("wq", HAND1, HAND2, F32R)
        keep.raw_wo = hand("raw_wo", HAND1, HAND2).rearrange("p (s n) -> p s n", s=WO_RING)
        keep.raw_up = hand("raw_up", 0, 2 * D_MODEL).rearrange("p (k z c) -> p k z c", k=KD, z=2)
        keep.up0 = [hand(name, HAND1 + i * 2 * D_MODEL, 2 * D_MODEL, F32R).rearrange("p (k z c) -> p k z c", k=KD, z=2)
                    for i, name in enumerate(("wup0Hi", "wup0Lo"))]
        keep.latent_weights_in = sem("latent_weights_in")
        keep.pool_own = Own(nc.gpsimd, sem("pool_ownCDE"))
        keep.wo_in = [sem(f"wo_in{i}") for i in range(WO_RING)]
        keep.up_in = sem("up_in")
        keep.up_hi = sem("up_hi")
        keep.up_lo = sem("up_lo")
        keep.raw_gate = hand("raw_gate", 0, HAND1).rearrange("p (s n) -> p s n", s=GATE_RING)
        keep.four_rows = hand("four_rows", HAND1, HAND2).rearrange("p (b n) -> p b n", b=4)
        keep.gate_in = [sem(f"gate_in{i}") for i in range(GATE_RING)]
        keep.gate_hi = sem("gate_hi")
        keep.gate_lo = sem("gate_lo")
        keep.x1_in = [sem("x1_in0"), sem("x1_in1")]
        keep.rows_in = sem("rows_in")
        keep.f_sq = sem("f_sq")
        keep.ps = ctx.enter_context(nc.psum_tensor("banks", [P, 8, BANK], F32))
        with ExitStack() as mixer:
            def mb(name, shape, dt=F32):
                return mixer.enter_context(nc.sbuf_tensor(name, shape, dt))

            keep.sin = mb("rope_sin", [P, TILES, NFREQ])[:, :, :]
            keep.cos = mb("rope_cos", [P, TILES, NFREQ])[:, :, :]
            keep.q_y = mb("q_then_y", [P, TILES, RET_WIDTH])[:, :, :]
            keep.latent = mb("latent", [P, TILES, LATENT])[:, :, :]
            uq_cols = KQ * MLA_HEADS * MLA_QK_DIM
            ukv_cols = MLA_HEADS * (MLA_NOPE_DIM + MLA_V_DIM)
            keep.raw_uq = raw_latent[:, 0:uq_cols].rearrange("p (k h n) -> p k h n", k=KQ, h=MLA_HEADS)
            keep.raw_ukv = raw_latent[:, uq_cols:uq_cols + ukv_cols].rearrange("p (h n) -> p h n", h=MLA_HEADS)
            keep.wq_parts = [keep.wq[:, i * 2 * SEQ:(i + 1) * 2 * SEQ].rearrange("p (k h c) -> p k h c", k=KQ, h=MLA_HEADS) for i in range(2)]
            stage_base = nc.sbuf_base
            _, pt_cols = pt_columns()

            def ahead(name, first, count, dt=F32):
                return nc.alloc_sbuf_tensor_at(name, [P, count], dt, offset=stage_base + 4 * first)[:, :]

            keep.krow, keep.trow = (ahead(name, i * SEQ, SEQ).rearrange("p (t c) -> p t c", t=TILES) for i, name in enumerate(("krow", "trow")))
            keep.krow_products = ahead("krow_products", 2 * SEQ, 2 * TILES * MLA_ROPE_DIM).rearrange(
                "p (j t d) -> p j t d", j=2, t=TILES)
            keep.wk = [ahead(name, 2 * pt_cols + i * WK_COLS, WK_COLS, F32R).rearrange("p (h n) -> p h n", h=MLA_HEADS)
                       for i, name in enumerate(("wkHi", "wkLo"))]
            retention_and_projection(nc, io, keep)
            latent_attention(nc, io, keep)
            mix_output(nc, io, keep)
        keep.ffn = sb("ffn_rows", [P, TILES, D_MODEL])[:, :, :]
        conv_ffn(nc, io, keep)
        layer_embedding(nc, io, keep)


def kernel(**inputs):
    import concourse.bacc as bacc
    from concourse.bass_utils import run_bass_kernel_spmd

    nc = bacc.Bacc("TRN2", target_bir_lowering=False, num_devices=1)
    arrays = {name: np.ascontiguousarray(inputs[name]) for name in INPUTS}
    arrays["consts"] = shape_constants()
    drams = {name: nc.dram_tensor(f"in_{name}", a.shape, mybir.dt.from_np(a.dtype), kind="ExternalInput").ap()
             for name, a in arrays.items()}
    out = nc.dram_tensor("out", inputs["x"].shape, F32, kind="ExternalOutput").ap()
    x1 = nc.dram_tensor("x1_scratch", (SEQ, D_MODEL), F32, kind="Internal").ap()
    io = Inputs(out=out, x1=x1, **drams)
    decoder_layer(nc, io)
    r = run_bass_kernel_spmd(nc, [{f"in_{name}": a for name, a in arrays.items()}], core_ids=[0])
    return r.results[0]["out"]
```
